# Optimizing a Trainium2 kernel written in Bass

```python
import functools
import jax
import jax.numpy as jnp
from jax import lax
import numpy as np

D_MODEL = 1024
BATCH = 1
SEQ = 512
DEPTH = 1
DEC_BATCH = 8
DEC_SEQ = 4
PAST_LEN = 1024
PAGE_SIZE = 128

N_HEADS_A = 8
N_KV_A = 2
HEAD_DIM_A = 64
W_A = N_HEADS_A * HEAD_DIM_A
N_IDX_HEADS = 4
IDX_DIM = 64
TOPK_MAX = 256
Q_BLOCK = 128
ROPE_THETA = 500000.0
ROT_A = HEAD_DIM_A // 4
ROT_IDX = IDX_DIM // 4
N_HEADS_B = 8
HEAD_DIM_B = 64
W_B = N_HEADS_B * HEAD_DIM_B
D_DECAY_LORA = 64
D_AAA_LORA = 64
D_GATE_LORA = 128
RWKV_PROJ = 3 * W_B + D_DECAY_LORA + D_AAA_LORA + D_GATE_LORA
GN_EPS = 64e-5
N_MEM = 256
N_HEADS_C = 4
HEAD_DIM_C = 128
W_C = N_HEADS_C * HEAD_DIM_C
N_BRANCH = 3
D_FF = 4 * D_MODEL
RMS_EPS = 1e-6
IN_SIZES = (W_A, N_KV_A * HEAD_DIM_A, N_KV_A * HEAD_DIM_A, N_IDX_HEADS * IDX_DIM, IDX_DIM,
            N_IDX_HEADS, RWKV_PROJ, W_C, N_BRANCH * D_MODEL)
IN_WIDTH = (W_A + 2 * N_KV_A * HEAD_DIM_A + N_IDX_HEADS * IDX_DIM + IDX_DIM + N_IDX_HEADS
            + RWKV_PROJ + W_C + N_BRANCH * D_MODEL)
RWKV_SIZES = (W_B, W_B, W_B, D_DECAY_LORA, D_AAA_LORA, D_GATE_LORA)

kernel_name = "hybrid_dsa_rwkv7_memxattn_step"

def split_last(p, sizes):
    offs = []
    acc = 0
    for s in sizes[:-1]:
        acc += s
        offs.append(acc)
    return jnp.split(p, offs, axis=-1)

def rmsnorm(x, g):
    xf = x.astype(jnp.float32)
    y = xf * lax.rsqrt(jnp.mean(xf * xf, axis=-1, keepdims=True) + RMS_EPS)
    return (y * g.astype(jnp.float32)).astype(x.dtype)

def rope_partial(x, pos, rot_dim):
    half = rot_dim // 2
    inv_freq = ROPE_THETA ** (-jnp.arange(half, dtype=jnp.float32) / half)
    ang = pos.astype(jnp.float32)[:, None] * inv_freq[None, :]
    cos = jnp.cos(ang)[:, None, :]
    sin = jnp.sin(ang)[:, None, :]
    xf = x.astype(jnp.float32)
    x1, x2, rest = xf[..., :half], xf[..., half:rot_dim], xf[..., rot_dim:]
    out = jnp.concatenate([x1 * cos - x2 * sin, x2 * cos + x1 * sin, rest], axis=-1)
    return out.astype(x.dtype)

def index_topk(iq, iw, ik, q_pos, topk):
    s = jax.nn.relu(jnp.einsum('bqhd,bld->bqhl', iq, ik))
    score = jnp.einsum('bqhl,bqh->bql', s, iw).astype(jnp.float32)
    n_keys = ik.shape[1]
    causal = jnp.arange(n_keys)[None, None, :] <= q_pos[None, :, None]
    score = jnp.where(causal, score, -jnp.inf)
    _, idx = lax.top_k(score, topk)
    valid = idx <= q_pos[None, :, None]
    return idx, valid

def sparse_attend(q, k_sel, v_sel, valid):
    B, Tq = q.shape[:2]
    qg = q.reshape(B, Tq, N_KV_A, N_HEADS_A // N_KV_A, HEAD_DIM_A)
    s = jnp.einsum('bqgrd,bqkgd->bqgrk', qg, k_sel).astype(jnp.float32) * (HEAD_DIM_A ** -0.5)
    s = jnp.where(valid[:, :, None, None, :], s, -jnp.inf)
    p = jax.nn.softmax(s, axis=-1).astype(v_sel.dtype)
    o = jnp.einsum('bqgrk,bqkgd->bqgrd', p, v_sel)
    return o.reshape(B, Tq, W_A)

def dsa_prompt(q, k, v, iq, ik, iw):
    B, T = q.shape[:2]
    topk = min(TOPK_MAX, T // 4)
    nb = T // Q_BLOCK
    bsel = jnp.arange(B)[:, None, None]

    def blocks(a):
        return a.reshape((B, nb, Q_BLOCK) + a.shape[2:]).swapaxes(0, 1)

    def one_block(args):
        qb, iqb, iwb, bi = args
        q_pos = bi * Q_BLOCK + jnp.arange(Q_BLOCK)
        idx, valid = index_topk(iqb, iwb, ik, q_pos, topk)
        return sparse_attend(qb, k[bsel, idx], v[bsel, idx], valid)

    o = lax.map(one_block, (blocks(q), blocks(iq), blocks(iw), jnp.arange(nb)))
    return o.swapaxes(0, 1).reshape(B, T, W_A)

def dsa_sample(q, k_new, v_new, iq, ik_new, iw, cache_k, cache_v, cache_idx_k, page_table):
    DB, Tn = q.shape[:2]
    n_keys = PAST_LEN + Tn
    topk = min(TOPK_MAX, n_keys // 4)
    ik_past = cache_idx_k[page_table].reshape(DB, PAST_LEN, IDX_DIM)
    ik_all = jnp.concatenate([ik_past, ik_new.astype(ik_past.dtype)], axis=1)
    q_pos = PAST_LEN + jnp.arange(Tn)
    idx, valid = index_topk(iq, iw, ik_all, q_pos, topk)
    bsel = jnp.arange(DB)[:, None, None]
    in_cache = (idx < PAST_LEN)[..., None, None]
    pc = jnp.minimum(idx, PAST_LEN - 1)
    phys = page_table[bsel, pc // PAGE_SIZE]
    off = pc % PAGE_SIZE
    pn = jnp.clip(idx - PAST_LEN, 0, Tn - 1)
    k_sel = jnp.where(in_cache, cache_k[phys, off], k_new[bsel, pn].astype(cache_k.dtype))
    v_sel = jnp.where(in_cache, cache_v[phys, off], v_new[bsel, pn].astype(cache_v.dtype))
    return sparse_attend(q, k_sel.astype(q.dtype), v_sel.astype(q.dtype), valid)

def rwkv7_time_mix(p_b, shift_prev, wkv_prev, mu, w0, w_up, a0, a_up, g_up, k_k, k_a, r_k, ln_g, ln_b):
    B, T, _ = p_b.shape
    prev = jnp.concatenate([shift_prev[:, None, :].astype(p_b.dtype), p_b[:, :-1]], axis=1)
    ps = p_b + (prev - p_b) * mu
    r, k, v, wl, al, gl = split_last(ps, RWKV_SIZES)
    w_log = -jax.nn.softplus(-(w0 + jnp.tanh(wl) @ w_up)) - 0.5
    decay = jnp.exp(-jnp.exp(w_log.astype(jnp.float32)))
    a = jax.nn.sigmoid(a0 + al @ a_up)
    g = jax.nn.sigmoid(gl) @ g_up

    def heads(t):
        return t.reshape(B, T, N_HEADS_B, HEAD_DIM_B).astype(jnp.float32)

    r_h, v_h, a_h, w_h = heads(r), heads(v), heads(a), heads(decay)
    kk = heads(k * k_k)
    kk = kk / jnp.maximum(jnp.sqrt(jnp.sum(kk * kk, axis=-1, keepdims=True)), 1e-12)
    k_h = heads(k) * (1.0 + (a_h - 1.0) * k_a.reshape(N_HEADS_B, HEAD_DIM_B).astype(jnp.float32))

    def step(S, inp):
        r_t, w_t, k_t, v_t, kk_t, a_t = inp
        sa = jnp.einsum('bhvk,bhk->bhv', S, -kk_t)
        S = (S * w_t[:, :, None, :] + sa[..., None] * (kk_t * a_t)[:, :, None, :]
             + v_t[..., None] * k_t[:, :, None, :])
        return S, jnp.einsum('bhvk,bhk->bhv', S, r_t)

    xs = tuple(t.swapaxes(0, 1) for t in (r_h, w_h, k_h, v_h, kk, a_h))
    S_T, y = lax.scan(step, wkv_prev.astype(jnp.float32), xs)
    y = y.swapaxes(0, 1)
    mean = jnp.mean(y, axis=-1, keepdims=True)
    var = jnp.mean(jnp.square(y - mean), axis=-1, keepdims=True)
    yn = ((y - mean) * lax.rsqrt(var + GN_EPS)).reshape(B, T, W_B)
    yn = yn * ln_g.astype(jnp.float32) + ln_b.astype(jnp.float32)
    bonus = jnp.sum(r_h * k_h * r_k.astype(jnp.float32), axis=-1, keepdims=True) * v_h
    out = (yn + bonus.reshape(B, T, W_B)) * g.astype(jnp.float32)
    return out.astype(p_b.dtype), S_T, p_b[:, -1]

def memory_kv(mem, norm_mem_g, w_mem_kv):
    B = mem.shape[0]
    mk, mv = jnp.split(rmsnorm(mem, norm_mem_g) @ w_mem_kv, 2, axis=-1)
    return (mk.reshape(B, N_MEM, N_HEADS_C, HEAD_DIM_C), mv.reshape(B, N_MEM, N_HEADS_C, HEAD_DIM_C))

def cross_attend(qc, mk, mv):
    B, T = qc.shape[:2]
    s = jnp.einsum('bthd,bmhd->bhtm', qc, mk.astype(qc.dtype)).astype(jnp.float32) * (HEAD_DIM_C ** -0.5)
    p = jax.nn.softmax(s, axis=-1).astype(qc.dtype)
    o = jnp.einsum('bhtm,bmhd->bthd', p, mv.astype(qc.dtype))
    return o.reshape(B, T, W_C)

def token_mixing(x, pos, dsa_fn, mem_k, mem_v, shift_prev, wkv_prev, norm_mix_g, w_in, b_gate,
                 rwkv_params, w_branch_a, w_branch_b, w_branch_c, w_out):
    B, T, _ = x.shape
    p = rmsnorm(x, norm_mix_g) @ w_in
    a_q, a_k, a_v, i_q, i_k, i_w, p_b, c_q, gates = split_last(p, IN_SIZES)
    a_q = rope_partial(a_q.reshape(B, T, N_HEADS_A, HEAD_DIM_A), pos, ROT_A)
    a_k = rope_partial(a_k.reshape(B, T, N_KV_A, HEAD_DIM_A), pos, ROT_A)
    a_v = a_v.reshape(B, T, N_KV_A, HEAD_DIM_A)
    i_q = rope_partial(i_q.reshape(B, T, N_IDX_HEADS, IDX_DIM), pos, ROT_IDX)
    i_k = rope_partial(i_k[:, :, None, :], pos, ROT_IDX)[:, :, 0, :]
    i_w = i_w * ((N_IDX_HEADS * IDX_DIM) ** -0.5)
    o_a = dsa_fn(a_q, a_k, a_v, i_q, i_k, i_w)
    o_b, wkv_new, shift_new = rwkv7_time_mix(p_b, shift_prev, wkv_prev, *rwkv_params)
    o_c = cross_attend(c_q.reshape(B, T, N_HEADS_C, HEAD_DIM_C), mem_k, mem_v)
    g = jax.nn.sigmoid(gates + b_gate).reshape(B, T, N_BRANCH, D_MODEL)
    merged = (g[:, :, 0] * (o_a @ w_branch_a) + g[:, :, 1] * (o_b @ w_branch_b)
              + g[:, :, 2] * (o_c @ w_branch_c))
    return x + merged @ w_out, a_k, a_v, i_k, wkv_new, shift_new

def sq_relu_mlp(x, norm_g, w_up, w_down):
    h = rmsnorm(x, norm_g) @ w_up
    return x + jnp.square(jax.nn.relu(h)) @ w_down

def setup_inputs(seed: int = 0) -> dict:
    key = jax.random.key(seed)
    ks = iter(jax.random.split(key, 48))

    def nrm(shape, scale):
        return jax.random.normal(next(ks), shape, jnp.float32) * scale

    def unif(shape, lo, hi):
        return jax.random.uniform(next(ks), shape, jnp.float32, lo, hi)

    n_pages = PAST_LEN // PAGE_SIZE
    n_phys = (DEC_BATCH * n_pages * 5) // 4
    page_table = jax.random.permutation(next(ks), n_phys)[:DEC_BATCH * n_pages]
    page_table = page_table.reshape(DEC_BATCH, n_pages).astype(jnp.int32)
    return {
        "x_prompt": nrm((BATCH, SEQ, D_MODEL), 1.0),
        "x_sample": nrm((DEC_BATCH, DEC_SEQ, D_MODEL), 1.0),
        "mem_prompt": nrm((BATCH, N_MEM, D_MODEL), 1.0),
        "cache_k": nrm((n_phys, PAGE_SIZE, N_KV_A, HEAD_DIM_A), 1.0),
        "cache_v": nrm((n_phys, PAGE_SIZE, N_KV_A, HEAD_DIM_A), 1.0),
        "cache_idx_k": nrm((n_phys, PAGE_SIZE, IDX_DIM), 1.0),
        "cache_mem_k": nrm((DEC_BATCH, N_MEM, N_HEADS_C, HEAD_DIM_C), 1.0),
        "cache_mem_v": nrm((DEC_BATCH, N_MEM, N_HEADS_C, HEAD_DIM_C), 1.0),
        "state_wkv": nrm((DEC_BATCH, N_HEADS_B, HEAD_DIM_B, HEAD_DIM_B), 0.3),
        "state_shift": nrm((DEC_BATCH, RWKV_PROJ), 1.0),
        "page_table": page_table,
        "norm_mix_g": 1.0 + nrm((D_MODEL,), 0.05),
        "norm_mem_g": 1.0 + nrm((D_MODEL,), 0.05),
        "norm_mlp_g": 1.0 + nrm((D_MODEL,), 0.05),
        "norm_final_g": 1.0 + nrm((D_MODEL,), 0.05),
        "w_in": nrm((D_MODEL, IN_WIDTH), D_MODEL ** -0.5),
        "b_gate": nrm((N_BRANCH * D_MODEL,), 0.02),
        "w_mem_kv": nrm((D_MODEL, 2 * W_C), D_MODEL ** -0.5),
        "rwkv_mu": unif((RWKV_PROJ,), 0.0, 1.0),
        "rwkv_w0": unif((W_B,), -4.0, 1.0),
        "rwkv_w_up": nrm((D_DECAY_LORA, W_B), 0.1 * D_DECAY_LORA ** -0.5),
        "rwkv_a0": nrm((W_B,), 0.1),
        "rwkv_a_up": nrm((D_AAA_LORA, W_B), 0.5 * D_AAA_LORA ** -0.5),
        "rwkv_g_up": nrm((D_GATE_LORA, W_B), D_GATE_LORA ** -0.5),
        "rwkv_k_k": 0.85 + nrm((W_B,), 0.05),
        "rwkv_k_a": 1.0 + nrm((W_B,), 0.05),
        "rwkv_r_k": nrm((N_HEADS_B, HEAD_DIM_B), 0.1),
        "rwkv_ln_g": 1.0 + nrm((W_B,), 0.05),
        "rwkv_ln_b": nrm((W_B,), 0.02),
        "w_branch_a": nrm((W_A, D_MODEL), W_A ** -0.5),
        "w_branch_b": nrm((W_B, D_MODEL), W_B ** -0.5),
        "w_branch_c": nrm((W_C, D_MODEL), W_C ** -0.5),
        "w_out": nrm((D_MODEL, D_MODEL), D_MODEL ** -0.5),
        "w_mlp_up": nrm((D_MODEL, D_FF), D_MODEL ** -0.5),
        "w_mlp_down": nrm((D_FF, D_MODEL), D_FF ** -0.5),
    }

def reference(x_prompt, x_sample, mem_prompt, cache_k, cache_v, cache_idx_k, cache_mem_k, cache_mem_v,
              state_wkv, state_shift, page_table, norm_mix_g, norm_mem_g, norm_mlp_g, norm_final_g,
              w_in, b_gate, w_mem_kv, rwkv_mu, rwkv_w0, rwkv_w_up, rwkv_a0, rwkv_a_up, rwkv_g_up,
              rwkv_k_k, rwkv_k_a, rwkv_r_k, rwkv_ln_g, rwkv_ln_b, w_branch_a, w_branch_b, w_branch_c,
              w_out, w_mlp_up, w_mlp_down):
    rwkv_params = (rwkv_mu, rwkv_w0, rwkv_w_up, rwkv_a0, rwkv_a_up, rwkv_g_up, rwkv_k_k, rwkv_k_a,
                   rwkv_r_k, rwkv_ln_g, rwkv_ln_b)

    B, T, _ = x_prompt.shape
    pos_p = jnp.arange(T)
    shift0 = jnp.zeros((B, RWKV_PROJ), x_prompt.dtype)
    wkv0 = jnp.zeros((B, N_HEADS_B, HEAD_DIM_B, HEAD_DIM_B), jnp.float32)
    y_p = x_prompt
    for _layer in range(DEPTH):
        mem_k_p, mem_v_p = memory_kv(mem_prompt, norm_mem_g, w_mem_kv)
        h_p, k_p, v_p, ik_p, wkv_p, sh_p = token_mixing(
            y_p, pos_p, dsa_prompt, mem_k_p, mem_v_p, shift0, wkv0, norm_mix_g, w_in, b_gate,
            rwkv_params, w_branch_a, w_branch_b, w_branch_c, w_out)
        y_p = sq_relu_mlp(h_p, norm_mlp_g, w_mlp_up, w_mlp_down)
    y_prompt = rmsnorm(y_p, norm_final_g)

    pos_s = PAST_LEN + jnp.arange(x_sample.shape[1])
    dsa_s = functools.partial(dsa_sample, cache_k=cache_k, cache_v=cache_v,
                              cache_idx_k=cache_idx_k, page_table=page_table)
    y_s = x_sample
    for _layer in range(DEPTH):
        h_s, k_s, v_s, ik_s, wkv_s, sh_s = token_mixing(
            y_s, pos_s, dsa_s, cache_mem_k, cache_mem_v, state_shift, state_wkv, norm_mix_g, w_in,
            b_gate, rwkv_params, w_branch_a, w_branch_b, w_branch_c, w_out)
        y_s = sq_relu_mlp(h_s, norm_mlp_g, w_mlp_up, w_mlp_down)
    y_sample = rmsnorm(y_s, norm_final_g)

    return (y_prompt, y_sample, k_p, v_p, ik_p, mem_k_p, mem_v_p, wkv_p, sh_p,
            k_s, v_s, ik_s, wkv_s, sh_s)


_drawn_inputs = setup_inputs


def setup_inputs(seed=0):
    import zlib

    import numpy as np

    out = dict(_drawn_inputs(seed))
    spreads = {}
    factors = {'b_gate': 8.0, 'rwkv_w_up': 7.533, 'rwkv_ln_g': 3.943, 'rwkv_ln_b': 8.0}
    for name, (base, spread) in spreads.items():
        noise = np.random.default_rng([zlib.crc32(name.encode()), seed]).standard_normal(out[name].shape)
        drawn = base * np.exp(spread * noise) if base else spread * noise
        out[name] = jnp.asarray(drawn.astype(out[name].dtype))
    for name, factor in factors.items():
        out[name] = (out[name] * factor).astype(out[name].dtype)
    return out
```

```python
from contextlib import ExitStack

import numpy as np
import concourse.bass as bass
from concourse import mybir

F32 = mybir.dt.float32
BF16 = mybir.dt.bfloat16
I32 = mybir.dt.int32
U32 = mybir.dt.uint32
ALU = mybir.AluOpType
ACT = mybir.ActivationFunctionType
AX = mybir.AxisListType

P = 128
D = 1024
KT = D // P
SEQ, DB, DS = 512, 8, 4
NS = DB * DS
TOK = SEQ + NS
HALF = TOK // 2
PAST, PAGE, TOPK_P, TOPK_S = 1024, 128, 128, 256
KEYS = PAST + NS
NMEM = 256
PB = 1792
PBT = PB // P
PBW = SEQ + 1 + DB * (DS + 1)
C = 128
NCH = SEQ // C
FF = 4096
NEG, GONE = -1e30, -3e38
EPS, GN_EPS = 1e-6, 64e-5
SLABW = KT * 256
RING = 5

AQ, AK, AV, IQ, IK, PBC = 0, 512, 640, 768, 1024, 1092
CQ = PBC + PB
GATE = CQ + 512

CONSTS = [("ident", 128), ("rot", 128), ("blk", 128), ("ones", 128), ("cos", TOK), ("sin", TOK),
          ("mask4", 512), ("lev", 512), ("mlow", 128), ("reset", TOK), ("caus", 128),
          ("rep", 256), ("sel", 32), ("smask4", 128), ("slow", 32), ("snew", 32), ("sblk", 8)]
COFF, _n = {}, 0
for _k, _w in CONSTS:
    COFF[_k] = (_n, _w)
    _n += _w
NCONST = _n


def constants():
    c = {k: np.zeros((P, w), np.float32) for k, w in CONSTS}
    c["ident"][:] = np.eye(P)
    for base in (0, 64):
        for i in range(8):
            c["rot"][base + 8 + i, base + i] = -1.0
            c["rot"][base + i, base + 8 + i] = 1.0
    f = np.arange(P)
    c["blk"][:] = (f[:, None] // 64 == f[None, :] // 64)
    c["ones"][:] = 1.0
    pos = np.concatenate([np.arange(SEQ), np.tile(PAST + np.arange(DS), DB)]).astype(np.float32)
    inv = (np.float32(500000.0) ** (-np.arange(8, dtype=np.float32) / np.float32(8))).astype(np.float32)
    ang = (pos[None, :] * inv[:, None]).astype(np.float32)
    c["cos"][:] = 1.0
    for base in (0, 8, 64, 72):
        c["cos"][base:base + 8] = np.cos(ang)
        c["sin"][base:base + 8] = np.sin(ang)
    s, t = f[:, None], f[None, :]
    strict, incl = (s < t), (s <= t)
    c["mask4"][:] = np.concatenate([strict, incl, strict, incl], 1)
    lev = [strict & (s // 16 == t // 16)]
    for b in (16, 32, 64):
        lev.append((s // (2 * b) == t // (2 * b)) & (s // b < t // b))
    c["lev"][:] = np.concatenate(lev, 1)
    c["mlow"][:] = lev[0].T
    c["reset"][:] = 1.0
    c["reset"][:, 0:SEQ:C] = 0.0
    c["reset"][:, SEQ::DS] = 0.0
    c["caus"][:] = np.where(t > s, NEG, 0.0)
    r = np.arange(P)
    for hb in range(2):
        c["rep"][(hb * 4 + r // 32) * 4 + r % 4, hb * P + r] = 1.0
    c["sel"][r, r % 32] = 1.0
    a = np.arange(NS)
    sb_, tb = a[:, None], a[None, :]
    same = sb_ // 4 == tb // 4
    c["smask4"][0:NS] = np.concatenate([same & (sb_ < tb), same & (sb_ <= tb)] * 2, 1)
    c["slow"][0:NS] = same & (sb_ > tb)
    c["snew"][0:NS] = np.where(same & (tb <= sb_), 0.0, NEG)
    c["sblk"][0:NS] = sb_ // 4 == np.arange(8)[None, :]
    return np.concatenate([c[k] for k, _ in CONSTS], 1).astype(np.float32)


VECS = [("norm_mix_g", 8), ("norm_mem_g", 8), ("norm_mlp_g", 8), ("norm_final_g", 8), ("b_gate", 24),
        ("rwkv_mu", 14), ("rwkv_w0", 4), ("rwkv_a0", 4), ("rwkv_k_k", 4), ("rwkv_k_a", 4),
        ("rwkv_r_k", 4), ("rwkv_ln_g", 4), ("rwkv_ln_b", 4)]
VOFF, _n = {}, 0
for _k, _w in VECS:
    VOFF[_k] = (_n, _w)
    _n += _w
NVEC = _n


def slab_plan():
    def head(base, h):
        return (base + 64 * h, 64)

    s = [("w_in", 0, KT, [(IK, 64), (IK, 64), (IK + 64, 4)]), ("w_in", 0, KT, [(IQ, 256)])]
    s += [("w_in", 0, KT, [head(AQ, t + o) for t in (2 * n, 2 * n + 1) for o in (0, 4)]) for n in range(2)]
    s += [("w_in", 0, KT, [(AK, 256)])]
    s += [("w_mem_kv", 0, KT, [(256 * i, 256)]) for i in range(4)]
    s += [("w_in", 0, KT, [(CQ + 256 * i, 256)]) for i in range(2)]
    s += [("w_in", 0, KT, [(PBC + 256 * i, 256)]) for i in range(7)]
    for jj in range(4):
        for i in range(3):
            s += [("w_in", 0, KT, [(GATE + D * i + 256 * jj, 256)]), (f"w_branch_{'abc'[i]}", 0, 4, [(256 * jj, 256)])]
    s += [("w_out", 0, KT, [(256 * jj, 256)]) for jj in range(4)]
    s += [("w_mlp_up", 0, KT, [(256 * jj, 256)]) for jj in range(16)]
    s += [("w_mlp_down", D * r, KT, [(256 * jj, 256)]) for jj in range(4) for r in range(4)]
    return s


def job_plan():
    jobs = [("ik", 0, 0, 0, 128, "a"), ("iw", 0, 0, 128, 4, "a"), ("iq", 0, 1, 0, 128, "a"), ("iq", 1, 1, 128, 128, "a")]
    jobs += [("aq", i, 2 + i // 2, 128 * (i % 2), 128, "a") for i in range(4)]
    jobs += [("ak", 0, 4, 0, 128, "a"), ("av", 0, 4, 128, 128, "a")]
    jobs += [("mk", h, 5 + h // 2, 128 * (h % 2), 128, "a") for h in range(4)]
    jobs += [("mv", 2 * n + m, 7 + n, 0, 256, "a") for n in range(2) for m in range(2)]
    jobs += [("cq", i, 9 + i // 2, 128 * (i % 2), 128, "a") for i in range(4)]
    jobs += [("pb", i, 11 + i // 2, 128 * (i % 2), 128, "a") for i in range(PBT)]
    s = 18
    for jj in range(4):
        for i in range(3):
            for sub in range(2):
                jobs.append(("gate", 6 * jj + 2 * i + sub, s + 2 * i, 128 * sub, 128, "a"))
                jobs.append(("branch", 6 * jj + 2 * i + sub, s + 2 * i + 1, 128 * sub, 128, "v"))
        s += 6
    jobs += [("out", j, s + j // 2, 128 * (j % 2), 128, "v") for j in range(8)]
    s += 4
    jobs += [("up", j, s + j // 2, 128 * (j % 2), 128, "a") for j in range(32)]
    return jobs


SLABS = slab_plan()
NSLAB = len(SLABS)
JOBS = job_plan()
NJOB = len(JOBS)
DOWN0 = NSLAB - 16
FREED = {}
for _n, _j in enumerate(JOBS):
    FREED[_j[2]] = _n + 1
for _n in range(16):
    FREED[DOWN0 + _n] = NJOB + _n + 1


def merge_at(m):
    return 2 * (m // 6) + m % 2, m % 6 // 2


def job_at(kind, i=0):
    return next(n for n, j in enumerate(JOBS) if j[0] == kind and j[1] == i)


def evacuated(n, eng):
    return sum(j[5] == eng for j in JOBS[:n + 1])


class Sems(dict):

    def __init__(self, make):
        super().__init__()
        self.make = make

    def __missing__(self, name):
        self[name] = self.make(name)
        return self[name]


class Steps:

    def __init__(self, eng, sem):
        self.eng, self.sem, self.n = eng, sem, 0

    def __call__(self, ins):
        self.n += 1
        ins.then_inc(self.sem, 1)
        self.eng.wait_ge(self.sem, self.n)


def build(nc, i, o):
    with ExitStack() as ctx:
        def sb(name, cols, dt=F32):
            return ctx.enter_context(nc.sbuf_tensor(name, [P, cols], dt))

        s = Sems(lambda name: ctx.enter_context(nc.semaphore(name)))
        ring = sb("ring", RING * SLABW)
        cst = sb("cst", NCONST)
        vec = sb("vec", NVEC)
        xT = sb("xT", KT * TOK)
        xn = sb("xn", KT * TOK)
        aq = sb("aq", 4 * TOK)
        cq = sb("cq", 4 * TOK)
        pb = sb("pb", PBT * PBW)
        R = sb("R", 32 * TOK)
        identb = sb("identb", 128, BF16)
        repb = sb("repb", 256, BF16)
        small = sb("small", 192)
        pages = sb("pages", DB * 8, I32)
        ps = ctx.enter_context(nc.psum_tensor("ps", [P, 8, 512], F32))

        def cut(t, off, *dims):
            n = int(np.prod(dims))
            a = t[:, off:off + n]
            names = "abc"[:len(dims)]
            if len(dims) == 1:
                return a
            return a.rearrange("p (%s) -> p %s" % (" ".join(names), " ".join(names)), **dict(zip(names, dims)))

        def k_(name):
            off, w = COFF[name]
            return cst[:, off:off + w]

        def v_(name, j=0):
            off, _ = VOFF[name]
            return vec[:, off + j:off + j + 1]

        ident = k_("ident")
        lora = cst[:, COFF["cos"][0]:COFF["cos"][0] + 1024]
        xT3, xn3 = cut(xT, 0, KT, TOK), cut(xn, 0, KT, TOK)
        aq3, cq3 = cut(aq, 0, 4, TOK), cut(cq, 0, 4, TOK)
        pb3 = cut(pb, 0, PBT, PBW)
        memT, memn = cut(pb, 0, KT, NMEM), cut(pb, KT * NMEM, KT, NMEM)
        ik, iwT, iq = R[:, 0:TOK], R[:, TOK:2 * TOK], cut(R, 2 * TOK, 2, TOK)
        ak, av = R[:, 4 * TOK:5 * TOK], R[:, 5 * TOK:6 * TOK]
        r0 = 6 * TOK
        vt = cut(R, r0, 5, P)
        mkT = cut(R, r0 + 640, 4, NMEM)
        mv = cut(R, r0 + 1664, 2, 512)
        biasp = cut(R, r0 + 2688, 1024).bitcast(BF16).rearrange("p (a b) -> p a b", a=4)
        biass = cut(R, r0 + 3712, KEYS // 2).bitcast(BF16)
        B = r0 + 3712 + KEYS // 2
        ki = cut(R, B, 2, PAST)
        zi = R[:, B + 2048:B + 3200]
        rs = R[:, B + 3200:B + 4256]
        ss = R[0:NS, B + 4256:B + 5312]
        rl = cut(R, B + 5312, 4, 512)
        scp = rs[:, 0:512]
        NB = 28 * TOK
        assert B + 7360 <= NB
        sq = cut(R, NB, 2, TOK)
        rt, rc = R[:, NB + 2 * TOK:NB + 3 * TOK], R[:, NB + 3 * TOK:NB + 4 * TOK]
        rope1, rope2 = rt, sq
        ks = cut(R, B, 2, 8, P)
        vs = cut(R, B + 2048, 4, 8, P)
        za = R[:, B + 6144:B + 7424]
        pr = R[:, B + 7424:B + 7424 + KEYS]
        pt = cut(R, B + 8480, 9, P)
        assert B + 8480 + 9 * P <= 32 * TOK
        pp, ppt = cut(R, B, 2, 512), cut(R, B + 1024, 2, 4, P)
        zc = R[:, B:B + 32 * 132]
        mks, mvs = cut(R, B + 4224, 2, 1024), cut(R, B + 6272, 2, 1024)
        cp, cpt = R[:, B + 8320:B + 8320 + NMEM], cut(R, B + 8320 + NMEM, 2, P)
        xp, xpt = cut(R, B, 2, 4, NMEM), cut(R, B + 2048, 2, 8, P)
        iwc, iws = small[:, 0:20], small[:, 20:21]
        mx, nm, sm, ri = small[:, 24:28], small[:, 28:32], small[:, 32:36], small[:, 36:40]
        epsc, gneps = small[:, 40:41], small[:, 41:42]
        hw0, ha0 = small[:, 44:48], small[:, 48:52]
        c0, scf, sdec = small[:, 52:56], small[:, 56:60], small[:, 60:68]
        T0 = small[:, 68:132]
        sh_in = sb("sh_in", PBT * DB)
        sh_out = sb("sh_out", PBT * 9)
        slot = [R[:, TOK * n:TOK * (n + 1)] for n in range(14)]
        r_, k__, v__, lw, L_, a_, kk, kh = slot[:8]
        AR, bt, kt_, tA, tB = cut(R, 8 * TOK, 2, TOK), slot[10], slot[11], slot[12], slot[13]
        y_ = r_
        G = 14 * TOK
        m4 = cut(R, G, 4, 4, P)
        lev = cut(R, G + 2048, 4, 4, P)
        dx = cut(R, G + 4096, 4, 4, P)
        tt = cut(R, G + 6144, 4, P)
        tm = R[:, G + 6656:G + 6656 + 1536].rearrange("p (a b c) -> p a b c", a=3, b=4)
        zs, us = R[:, G + 8192:G + 8256], R[:, G + 8256:G + 8320]
        tms = cut(R, G + 8320, 3, P)
        assert G + 8704 <= 32 * TOK
        t0s = cut(R, G, DB, 64)
        zaa = R[:, G + 512:G + 800]
        ub, vb = cut(R, G + 1024, DB, 64), cut(R, G + 1536, DB, 64)
        sm4 = cut(R, G + 2048, 4, NS)
        sdl, sd2, sx1, sxt = (R[0:NS, G + 2176 + 32 * n:G + 2208 + 32 * n] for n in range(4))
        mg = cut(R, 0, KT, TOK)
        gb, mt = cut(R, KT * TOK, 2, TOK), R[:, 10 * TOK:11 * TOK]
        hid = cut(R, 0, 32, TOK)
        ub2 = cut(pb, 4 * PBW, 2, TOK)
        nbuf = [(sq, rt, rc)] * 2 + [(cut(pb, 6 * PBW, 2, TOK), pb[:, 8 * PBW:8 * PBW + TOK],
                                      pb[:, 9 * PBW:9 * PBW + TOK])] * 2
        t12, t13 = pb3[:, 12, 0:TOK], pb3[:, 13, 0:TOK]
        SQS = [("aq", aq3), ("cq", cq3)]
        lnlast = evacuated(NJOB - 1, "a")

        def slab(n):
            w = sum(c for _, c in SLABS[n][3])
            off = (n % RING) * SLABW
            return cut(ring, off, SLABS[n][2], w)

        def slab_wait(eng, n):
            eng.wait_ge(s[f"slab{n % RING}"], 16 * (n // RING + 1))

        def out_of(n, eng):
            e = JOBS[n][5]
            eng.wait_ge(s["evac_" + e], evacuated(n, e))

        def pair(b):
            return ps[:, b:b + 2, 0:HALF]

        def h2(t):
            return t.rearrange("p (h c) -> p h c", h=2)

        ROPE = [("ik", 0, ik), ("iq", 0, iq[:, 0]), ("iq", 1, iq[:, 1])]
        ROPE += [("aq", t, aq3[:, t]) for t in range(4)] + [("ak", 0, ak)]
        NU = 32
        scale_c = float(np.float32(128.0 ** -0.5))
        block = ctx.enter_context(nc.Block())

        @block.sync
        def _(sp):
            sp.dma_start(xT3, i["xT"]).then_inc(s["inputs_in"], 16)
            sp.dma_start(cst[:, :], i["const"]).then_inc(s["inputs_in"], 16)
            sp.dma_start(vec[:, :], i["vec"]).then_inc(s["inputs_in"], 16)
            for n, (_, _, kts, cols) in enumerate(SLABS):
                w = kts * sum(c for _, c in cols)
                if n >= RING:
                    sp.wait_ge(s["gemm_done"], FREED[n - RING])
                off = (n % RING) * SLABW
                sp.dma_start(ring[:, off:off + w], i["slabs"][n, :, 0:w]).then_inc(s[f"slab{n % RING}"], 16)
                if n == 1:
                    sp.dma_start(pages[0:1, :], i["pages"]).then_inc(s["aux_in"], 16)
                    sp.dma_start(memT, i["memT"]).then_inc(s["aux_in"], 16)
                    sp.dma_start(sh_in[:, :], i["shT"]).then_inc(s["aux_in"], 16)

        @block.gpsimd
        def _(pool):
            step = Steps(pool, s["pool_step"])
            step(pool.memset(epsc, EPS))
            step(pool.memset(gneps, GN_EPS))
            pool.wait_ge(s["norm_out"], 16)
            step(pool.memset(zi[0:64, :], 0.0))
            pool.wait_ge(s["aux_in"], 48)

            def page_of(b, j):
                return pool.value_load(pages[0:1, 8 * b + j:8 * b + j + 1], min_val=0, max_val=i["ki"].shape[0] - 1)

            def rope_cos(n):
                kind, idx, raw = ROPE[n]
                out_of(job_at(kind, idx), pool)
                if n == 0:
                    pool.wait_ge(s["inputs_in"], 48)
                if n >= 2:
                    pool.wait_ge(s["rope_out"], n - 1)
                pool.tensor_tensor(rope2[:, n % 2], raw, k_("cos"), ALU.mult).then_inc(s["rope_cos"], 1)

            for n in range(3):
                rope_cos(n)
            for b in range(DB):
                if b >= 2:
                    pool.wait_ge(s["ki_used"], b - 1)
                for j in range(8):
                    pg = page_of(b, j)
                    pool.dma_start(ki[0:64, b % 2, P * j:P * (j + 1)],
                                   i["ki"][bass.ds(pg, 1)].rearrange("o p c -> (o p) c")).then_inc(s[f"ki_in{b % 2}"], 16)
            pool.wait_ge(s["rope_out"], 1)
            pool.dma_start(o["ikT"], ik[0:64, :]).then_inc(s["stored"], 16)
            pool.wait_ge(s["gemm_done"], job_at("mv", 3) + 1)
            pool.wait_ge(s["aux_in"], 48)
            pool.memset(pb3[:, :, 0:1], 0.0).then_inc(s["pb_edge"], 1)
            pool.tensor_copy(pb3[:, :, SEQ + 1:PBW:5], cut(sh_in, 0, PBT, DB)).then_inc(s["pb_edge"], 1)
            for n in range(3, 8):
                rope_cos(n)
            pool.wait_ge(s["bias_done"], 4)
            pool.wait_ge(s["selected"], 2)
            step(pool.memset(za, 0.0))
            for hb in range(2):
                for b4 in range(4):
                    b = 4 * hb + b4
                    if b >= 2:
                        pool.wait_ge(s["ks_used"], b - 1)
                    if hb:
                        pool.wait_ge(s["vs_used"], b4 + 1)
                    for j in range(8):
                        pg = page_of(b, j)
                        pool.dma_start(ks[:, b % 2, j], i["kT"][bass.ds(pg, 1)].rearrange("o p c -> (o p) c")).then_inc(s[f"ks_in{b % 2}"], 16)
                        pool.dma_start(vs[:, b4, j], i["v"][bass.ds(pg, 1)].rearrange("o p c -> (o p) c")).then_inc(s[f"vs_in{b4}"], 16)
            pool.wait_ge(s["rope_out"], 8)
            pool.dma_start(lora, i["lora"]).then_inc(s["lora_in"], 16)
            pool.dma_start(o["kT"], ak).then_inc(s["stored"], 16)
            pool.dma_start(o["vT"], av).then_inc(s["stored"], 16)
            pool.dma_start(o["mkT"], mkT).then_inc(s["stored"], 16)
            pool.dma_start(o["mv"], mv).then_inc(s["stored"], 16)
            out_of(job_at("pb", PBT - 1), pool)
            so = cut(sh_out, 0, PBT, 9)
            step(pool.tensor_copy(so[:, :, 0:1], pb3[:, :, SEQ:SEQ + 1]))
            step(pool.tensor_copy(so[:, :, 1:9], pb3[:, :, SEQ + 5:PBW:5]))
            pool.dma_start(o["shT"], sh_out[:, :]).then_inc(s["stored"], 16)
            pool.wait_ge(s["pav_done"], NU)
            pool.wait_ge(s["oA_out"], 2 + 2 + 4)
            step(pool.memset(zc, 0.0))
            for b in range(DB):
                if b >= 2:
                    pool.wait_ge(s["mks_used"], b - 1)
                pool.dma_start(mks[:, b % 2], i["mks"][b]).then_inc(s[f"mks_in{b % 2}"], 16)
            for b in range(DB):
                if b >= 2:
                    pool.wait_ge(s["mvs_used"], b - 1)
                pool.dma_start(mvs[:, b % 2], i["mvs"][b]).then_inc(s[f"mvs_in{b % 2}"], 16)
            pool.wait_ge(s["oC_out"], 1 + 4)
            pool.wait_ge(s["stored"], 16 * 6)

            def diff(dst, tile):
                cur = pb3[:, tile]
                pool.tensor_tensor(dst[:, 0:SEQ], cur[:, 0:SEQ], cur[:, 1:SEQ + 1], ALU.subtract)
                c5 = cur[:, SEQ + 1:PBW].rearrange("p (b c) -> p b c", c=5)
                pool.tensor_tensor(dst[:, SEQ:TOK].rearrange("p (b c) -> p b c", c=4), c5[:, :, 0:4], c5[:, :, 1:5],
                                   ALU.subtract).then_inc(s["diff"], 1)

            pool.wait_ge(s["pb_edge"], 2)
            diff(tA, 12)
            diff(tB, 13)
            for j in range(4):
                if j:
                    pool.wait_ge(s["oB_out"], j)
                diff(r_, j)
                diff(k__, 4 + j)
                diff(v__, 8 + j)
                for hh in range(2):
                    g = 2 * j + hh
                    for c in range(4):
                        pool.wait_ge(s["m4"], 4 * g + c + 1)
                        pool.wait_ge(s["dlow"], 4 * g + c + 1)
                        if g and c == 0:
                            pool.wait_ge(s["t0s_out"] if hh == 0 else s["state"], 16 * j if hh == 0 else 4 * g)
                        pool.tensor_tensor(lev[:, c], m4[:, c, 0:1].to_broadcast([P, 4, P]), cut(cst, COFF["lev"][0], 4, P),
                                           ALU.mult).then_inc(s["lev"], 1)
                        pool.wait_ge(s["lev"], 4 * g + c + 1)
                        pool.tensor_tensor(dx[:, c, 1], dx[:, c, 0], ident, ALU.add)
                        pool.tensor_copy(dx[:, c, 2], lev[:, c, 0])
                        pool.tensor_tensor(dx[:, c, 3], lev[:, c, 0], ident, ALU.add).then_inc(s["dx_set"], 1)
                pool.wait_ge(s["state"], 4 * (2 * j + 2))
                pool.dma_start(t0s, i["wkvT"][j]).then_inc(s["t0s_in"], 16)
                step(pool.memset(zaa, 0.0))
                for hh in range(2):
                    pbs = slice(64 * hh, 64 * hh + 64)
                    pool.tensor_copy(zaa[pbs].rearrange("p (b c) -> p b c", c=36)[:, :, 0:4],
                                     AR[pbs, 0, SEQ:TOK].rearrange("p (b c) -> p b c", c=4)).then_inc(s["zaa"], 1)
                pool.wait_ge(s["state"], 4 * (2 * j + 2))
                pool.dma_start(o["wkvP"][j], T0).then_inc(s["T0_out"], 16)
                pool.wait_ge(s["sstate"], 2 * (j + 1))
                pool.dma_start(o["wkvS"][j], t0s).then_inc(s["t0s_out"], 16)
            for k in range(KT):
                pool.wait_ge(s["norm_out"], 25 + k)
                pool.dma_start(o["yT"][:, k], xn3[:, k]).then_inc(s["stored"], 16)
            pool.wait_ge(s["stored"], 16 * (6 + KT))
            pool.wait_ge(s["T0_out"], 16 * 4)
            pool.wait_ge(s["t0s_out"], 16 * 4)

        @block.tensor
        def _(pe):
            def norm(n, N, src_bank=4):
                hn = N // 2 if N > 512 else N
                for k in range(KT):
                    pe.wait_ge(s["norm_sq"], KT * n + k + 1)
                    for h in range(2 if N > 512 else 1):
                        mm = pe.matmul(ps[:, 4 + h, 0:hn], k_("ones"), nbuf[n][0][:, k % 2, h * hn:(h + 1) * hn],
                                       start=(k == 0), stop=(k == KT - 1))
                    mm.then_inc(s["norm_ss"], 1)

            def job(n, src):
                kind, idx, sl, c0_, w, _ = JOBS[n]
                slab_wait(pe, sl)
                if n >= 2:
                    out_of(n - 2, pe)
                W = slab(sl)
                b = 2 * (n % 2)
                kts = SLABS[sl][2]
                for k in range(kts):
                    a, z = k == 0, k == kts - 1
                    if kind == "mk":
                        mm = pe.matmul(ps[:, b, 0:NMEM], W[:, k, c0_:c0_ + w], memn[:, k], start=a, stop=z)
                    elif kind == "mv":
                        m = idx % 2
                        mm = pe.matmul(ps[:, b, 0:w], memn[:, k, P * m:P * (m + 1)], W[:, k, 0:w], start=a, stop=z)
                    else:
                        for h in range(2):
                            mm = pe.matmul(ps[0:w, b + h, 0:HALF], W[:, k, c0_:c0_ + w],
                                           src[:, k, h * HALF:(h + 1) * HALF], start=a, stop=z)
                mm.then_inc(s["gemm_done"], 1)

            def rope(n):
                kind, idx, raw = ROPE[n]
                out_of(job_at(kind, idx), pe)
                if n >= 2:
                    pe.wait_ge(s["rope_sin"], n - 1)
                for h in range(2):
                    mm = pe.matmul(ps[:, 4 + 2 * (n % 2) + h, 0:HALF], k_("rot"), raw[:, h * HALF:(h + 1) * HALF],
                                   start=True, stop=True)
                mm.then_inc(s["rope_rot"], 1)

            pe.wait_ge(s["inputs_in"], 48)
            norm(0, TOK)
            pe.wait_ge(s["norm_rt"], 1)
            norm(1, NMEM)
            pe.wait_ge(s["norm_out"], 8)
            for n in range(4):
                job(n, xn3)
            pe.wait_ge(s["norm_rt"], 2)
            for n in range(3):
                rope(n)
            pe.wait_ge(s["rope_sin"], 3)
            out_of(1, pe)
            for t in range(5):
                w = P if t < 4 else NS
                mm = pe.transpose(ps[0:w, 7, 4 * t:4 * t + 4], iwT[0:4, P * t:P * t + w], ident[0:4, 0:4])
            mm.then_inc(s["iw_tok"], 1)
            pe.wait_ge(s["zi_set"], 4)
            for b in range(DB):
                pe.wait_ge(s[f"ki_in{b % 2}"], 128 * (b // 2 + 1))
                for h in range(2):
                    pe.matmul(ps[:, 4 + h, :], zi[0:64, P * b:P * (b + 1)], ki[0:64, b % 2, 512 * h:512 * (h + 1)],
                              start=(b == 0), stop=(b == DB - 1))
                pe.matmul(ps[:, 6, 0:NS], zi[0:64, P * b:P * (b + 1)], ik[0:64, SEQ:TOK],
                          start=(b == 0), stop=(b == DB - 1)).then_inc(s["ki_used"], 1)
            pe.wait_ge(s["rs"], 1)
            for h in range(3):
                w = 512 if h < 2 else NS
                mm = pe.matmul(ps[0:NS, 4 + h, 0:w], k_("sel"), rs[:, 512 * h:512 * h + w], start=True, stop=True)
            mm.then_inc(s["ssum"], 1)
            pe.wait_ge(s["ss_out"], 1)
            for t in range(1, 4):
                for h in range(4):
                    if t >= 2:
                        pe.wait_ge(s["relu"], 4 * (t - 2) + h + 1)
                    hp = slice(64 * (h % 2), 64 * (h % 2) + 64)
                    pe.matmul(ps[:, 4 + h, 0:P * (t + 1)], iq[hp, h // 2, P * t:P * (t + 1)], ik[hp, 0:P * (t + 1)],
                              start=True, stop=True).then_inc(s["iscore"], 1)
            for n in range(4, job_at("gate", 0)):
                if JOBS[n][0] == "mk" and JOBS[n][1] == 0:
                    pe.wait_ge(s["norm_out"], 16)
                job(n, xn3)
            pe.wait_ge(s["relu"], 12)
            for n in range(3, 8):
                rope(n)
            pe.wait_ge(s["rope_sin"], 8)
            for t in range(5):
                w = P if t < 4 else NS
                mm = pe.transpose(ps[0:w, 6 + t // 4, P * (t % 4):P * (t % 4 + 1)], av[:, P * t:P * t + w], ident)
            mm.then_inc(s["v_tok"], 1)

            pe.wait_ge(s["za_set"], 4)
            pe.wait_ge(s["v_tok_out"], 2)
            pe.wait_ge(s["bf_const"], 2)
            pe.wait_ge(s["selected"], 2)
            for hb in range(2):
                if hb:
                    pe.wait_ge(s["s_exp"], 1)
                for b4 in range(4):
                    b = 4 * hb + b4
                    pe.wait_ge(s[f"ks_in{b % 2}"], 128 * (b // 2 + 1))
                    w = za[:, 640 * hb + P * b4:640 * hb + P * (b4 + 1)]
                    for h in range(2):
                        pe.matmul(ps[:, 4 + h, :], w, ks[:, b % 2, 4 * h:4 * h + 4], start=(b4 == 0), stop=False)
                    pe.matmul(ps[:, 6, 0:NS], w, ak[:, SEQ:TOK], start=(b4 == 0), stop=False).then_inc(s["ks_used"], 1)
                for h in range(3):
                    w = 512 if h < 2 else NS
                    mm = pe.matmul(ps[:, 4 + h, 0:w], repb[0:NS, P * hb:P * (hb + 1)], biass[0:NS, 512 * h:512 * h + w],
                                   start=False, stop=True)
                mm.then_inc(s["s_score"], 1)
                pe.wait_ge(s["s_prob"], hb + 1)
                if hb == 0:
                    out_of(job_at("pb", PBT - 1), pe)
                for t in range(9):
                    w = P if t < 8 else NS
                    mm = pe.transpose(ps[0:w, t // 4, P * (t % 4):P * (t % 4 + 1)], pr[:, P * t:P * t + w], ident)
                mm.then_inc(s["s_pT"], 1)
                pe.wait_ge(s["s_pT_out"], 3 * (hb + 1))
                if hb:
                    pe.wait_ge(s["oA_out"], 2)
                for b4 in range(4):
                    pe.wait_ge(s[f"vs_in{b4}"], 128 * (hb + 1))
                    for t in range(8):
                        pe.matmul(ps[:, 3, 32 * b4:32 * b4 + 32], vs[:, b4, t], pt[:, t, 32 * b4:32 * b4 + 32],
                                  start=(t == 0), stop=False)
                    pe.matmul(ps[:, 3, 32 * b4:32 * b4 + 32], vt[0:NS, 4], pt[0:NS, 8, 32 * b4:32 * b4 + 32],
                              start=False, stop=True).then_inc(s["vs_used"], 1)

            def unit(u):
                t, h = u // 8, u % 8
                return t, h // 2, slice(64 * (h % 2), 64 * (h % 2) + 64), h % 2

            def p_score(u):
                t, ht, hp, half = unit(u)
                if u >= 2:
                    pe.wait_ge(s["p_exp"], u - 1)
                pe.matmul(ps[:, 4 + u % 2, 0:P * (t + 1)], aq3[hp, ht, P * t:P * (t + 1)], ak[hp, 0:P * (t + 1)],
                          start=True, stop=False)
                pe.matmul(ps[:, 4 + u % 2, 0:P * (t + 1)], identb[:, :], biasp[:, t, 0:P * (t + 1)],
                          start=False, stop=True).then_inc(s["p_score"], 1)

            def p_turn(u):
                t, ht, hp, half = unit(u)
                pe.wait_ge(s["p_prob"], u + 1)
                if u >= 2:
                    pe.wait_ge(s["p_pT_out"], u - 1)
                for k in range(t + 1):
                    mm = pe.transpose(ps[:, 6 + u % 2, P * k:P * (k + 1)], pp[:, u % 2, P * k:P * (k + 1)], ident)
                mm.then_inc(s["p_pT"], 1)

            def p_out(u):
                t, ht, hp, half = unit(u)
                pe.wait_ge(s["p_pT_out"], u + 1)
                if u % 8 == 0 and t >= 2:
                    pe.wait_ge(s["oA_out"], 4 + t - 1)
                for k in range(t + 1):
                    mm = pe.matmul(ps[hp, t % 2, P * ht:P * (ht + 1)], vt[:, k, hp], ppt[:, u % 2, k],
                                   start=(k == 0), stop=(k == t))
                mm.then_inc(s["pav_done"], 1)

            pe.wait_ge(s["bias_done"], 4)
            pe.wait_ge(s["s_pT_out"], 6)
            pe.wait_ge(s["s_exp"], 2)
            for u in range(NU + 2):
                if u < NU:
                    p_score(u)
                if 1 <= u <= NU:
                    p_turn(u - 1)
                if u >= 2:
                    p_out(u - 2)

            pe.wait_ge(s["zc_set"], 1)
            pe.wait_ge(s["p_exp"], NU)
            for b in range(DB):
                pe.wait_ge(s[f"mks_in{b % 2}"], 16 * (b // 2 + 1))
                for h in range(4):
                    n = 4 * b + h
                    mm = pe.matmul(ps[:, 4, 0:NMEM], zc[:, P * n:P * (n + 1)], mks[:, b % 2, NMEM * h:NMEM * (h + 1)],
                                   start=(n == 0), stop=(n == 31))
                mm.then_inc(s["mks_used"], 1)
            pe.wait_ge(s["c_prob"], 1)
            for m in range(2):
                mm = pe.transpose(ps[:, 5, P * m:P * (m + 1)], cp[:, P * m:P * (m + 1)], ident)
            mm.then_inc(s["c_pT"], 1)
            pe.wait_ge(s["c_pT_out"], 1)
            for b in range(DB):
                pe.wait_ge(s[f"mvs_in{b % 2}"], 16 * (b // 2 + 1))
                for h in range(4):
                    n = 4 * b + h
                    for m in range(2):
                        mm = pe.matmul(ps[:, 2, 4 * n:4 * n + 4], mvs[:, b % 2, 512 * m + P * h:512 * m + P * (h + 1)],
                                       cpt[:, m, 4 * n:4 * n + 4], start=(m == 0), stop=(m == 1))
                mm.then_inc(s["mvs_used"], 1)

            pe.wait_ge(s["oC_out"], 1)
            for t in range(4):
                if t >= 1:
                    pe.wait_ge(s["x_exp"], 4 * t)
                for h in range(4):
                    mm = pe.matmul(ps[:, 4 + h // 2, NMEM * (h % 2):NMEM * (h % 2 + 1)], cq3[:, h, P * t:P * (t + 1)],
                                   mkT[:, h], start=True, stop=True)
                mm.then_inc(s["x_score"], 1)
                pe.wait_ge(s["x_prob"], t + 1)
                if t >= 1:
                    pe.wait_ge(s["x_pT_out"], 2 * t)
                for h in range(4):
                    for m in range(2):
                        mm = pe.transpose(ps[:, 6 + h // 2, P * (2 * (h % 2) + m):P * (2 * (h % 2) + m + 1)],
                                          xp[:, t % 2, h, P * m:P * (m + 1)], ident)
                mm.then_inc(s["x_pT"], 1)
                pe.wait_ge(s["x_pT_out"], 2 * (t + 1))
                if t >= 2:
                    pe.wait_ge(s["oC_out"], t)
                for h in range(4):
                    for m in range(2):
                        mm = pe.matmul(ps[:, t % 2, P * h:P * (h + 1)], mv[:, m, P * h:P * (h + 1)],
                                       xpt[:, t % 2, 2 * h + m], start=(m == 0), stop=(m == 1))
                mm.then_inc(s["xav_done"], 1)

            def wide(b, w, src):
                for h in range(2):
                    mm = pe.matmul(ps[:, b + h, 0:HALF], w, src[:, h * HALF:(h + 1) * HALF], start=True, stop=True)
                return mm

            pe.wait_ge(s["oC_out"], 5)
            pe.wait_ge(s["lora_in"], 16)
            pe.wait_ge(s["t12"], 2)
            for j in range(4):
                cols = slice(P * j, P * (j + 1))
                if j:
                    pe.wait_ge(s["oB_out"], j)
                wide(0, lora[0:64, cols], t12[0:64]).then_inc(s["lora_up"], 1)
                wide(2, lora[64:128, cols], t12[64:128]).then_inc(s["lora_up"], 1)
                pe.wait_ge(s["kk_sq"], j + 1)
                pe.wait_ge(s["tanhs"], 2 * j + 1)
                wide(0, k_("blk"), tA).then_inc(s["kk_ss"], 1)
                pe.wait_ge(s["rk"], j + 1)
                pe.wait_ge(s["tanhs"], 2 * j + 2)
                wide(2, k_("blk"), L_).then_inc(s["rk_sum"], 1)
                pe.wait_ge(s["factors"], j + 1)
                pe.wait_ge(s["bonus"], j + 1)
                for n, src in enumerate((v__, bt, kt_)):
                    for c in range(4):
                        pe.transpose(ps[:, n, P * c:P * (c + 1)], src[:, P * c:P * (c + 1)], ident)
                    mm = pe.transpose(ps[0:NS, 3, P * n:P * (n + 1)], src[:, SEQ:TOK], ident)
                mm.then_inc(s["tm"], 1)
                for hh in range(2):
                    g = 2 * j + hh
                    hp = slice(64 * hh, 64 * hh + 64)
                    for c in range(4):
                        t = slice(C * c, C * (c + 1))
                        if hh:
                            pe.wait_ge(s["state"], 4 * g)
                            pe.wait_ge(s["y_chunk"], 4 * g)
                        pe.matmul(ps[:, 4 + c, 0:256], bt[hp, t], AR[hp, :, t], start=True, stop=True)
                        pe.matmul(ps[:, 4 + c, 256:512], kt_[hp, t], AR[hp, :, t], start=True,
                                  stop=True).then_inc(s["pairs"], 1)
                    if hh == 0:
                        pe.wait_ge(s["tm_out"], 4 * (j + 1))
                    for c in range(4):
                        t = slice(C * c, C * (c + 1))
                        pe.matmul(ps[:, c, 0:P], AR[hp, 0, t], bt[hp, t], start=True, stop=True).then_inc(s["low"], 1)
                    for r in range(4):
                        for c in range(4):
                            if r == 0:
                                pe.wait_ge(s["dx_set"], 4 * g + c + 1)
                                pe.matmul(ps[:, 4 + c, 0:P], dx[:, c, 2], dx[:, c, 0], start=True, stop=True)
                                mm = pe.matmul(ps[:, 4 + c, 256:256 + P], dx[:, c, 0], dx[:, c, 2], start=True, stop=True)
                            else:
                                pe.wait_ge(s["dsq"], 12 * g + 4 * (r - 1) + c + 1)
                                if r > 1:
                                    pe.wait_ge(s["xup"], 12 * g + 4 * (r - 2) + c + 1)
                                if r < 3:
                                    pe.matmul(ps[:, 4 + c, 0:P], dx[:, c, 2], dx[:, c, 0], start=True, stop=True)
                                    pe.matmul(ps[:, 4 + c, 256:256 + P], dx[:, c, 0], dx[:, c, 2], start=True, stop=True)
                                pe.matmul(ps[:, c, 0:P], dx[:, c, 2], dx[:, c, 1], start=True, stop=True)
                                mm = pe.matmul(ps[:, c, P:256], dx[:, c, 0], dx[:, c, 3], start=True, stop=True)
                            mm.then_inc(s["round"], 1)
                    for l in range(3):
                        for c in range(4):
                            if l == 0:
                                pe.wait_ge(s["xup"], 12 * g + 8 + c + 1)
                            else:
                                pe.wait_ge(s["xlev"], 12 * g + 4 * (l - 1) + c + 1)
                            pe.matmul(ps[:, 4 + c, 0:P], lev[:, c, l + 1], dx[:, c, 1], start=True,
                                      stop=True).then_inc(s["mx"], 1)
                        for c in range(4):
                            pe.wait_ge(s["mx_out"], 12 * g + 4 * l + c + 1)
                            if l < 2:
                                pe.matmul(ps[:, c, 0:P], dx[:, c, 3], tt[:, c], start=True, stop=True)
                            pe.matmul(ps[:, c, P:256], tt[:, c], dx[:, c, 3], start=True,
                                      stop=True).then_inc(s["xmx"], 1)
                    pe.wait_ge(s["mx_out"], 12 * g + 12)
                    for c in range(4):
                        t = slice(C * c, C * (c + 1))
                        n = 4 * g + c
                        mm = pe.matmul(ps[:, 4, 0:64], m4[:, c, 2], tm[:, 0, c, hp], start=True, stop=(c == 0))
                        if c:
                            pe.wait_ge(s["state"], n)
                            mm = pe.matmul(ps[:, 4, 0:64], AR[hp, 0, t], T0[hp], start=False, stop=True)
                        mm.then_inc(s["z"], 1)
                        pe.wait_ge(s["z_out"], n + 1)
                        pe.wait_ge(s["xlev"], 12 * g + 8 + c + 1)
                        pe.matmul(ps[:, 5, 0:64], dx[:, c, 3], zs, start=True, stop=True).then_inc(s["u"], 1)
                        pe.wait_ge(s["u_out"], n + 1)
                        pe.matmul(ps[hp, 7, 0:64], tm[:, 1, c, hp], us, start=True, stop=False)
                        pe.matmul(ps[hp, 7, 0:64], tm[:, 2, c, hp], tm[:, 0, c, hp], start=False,
                                  stop=True).then_inc(s["dstate"], 1)
                        if c:
                            pe.wait_ge(s["y_chunk"], n)
                        pe.matmul(ps[hp, 6, 0:P], tm[:, 0, c, hp], m4[:, c, 3], start=True, stop=False)
                        if c:
                            pe.matmul(ps[hp, 6, 0:P], T0[hp], AR[hp, 1, t], start=False, stop=False)
                        pe.matmul(ps[hp, 6, 0:P], us, m4[:, c, 1], start=False, stop=True).then_inc(s["ychunk"], 1)
                pe.wait_ge(s["state"], 8 * (j + 1))
                pe.wait_ge(s["y_chunk"], 8 * (j + 1))
                pe.wait_ge(s["t0s_in"], 16 * (j + 1))
                pe.wait_ge(s["zaa"], 2 * (j + 1))
                for hh in range(2):
                    n = 2 * j + hh
                    hp = slice(64 * hh, 64 * hh + 64)
                    st = slice(SEQ, TOK)
                    pe.matmul(ps[0:NS, 4, 0:64], bt[hp, st], AR[hp, :, st], start=True, stop=True)
                    pe.matmul(ps[0:NS, 4, 64:128], kt_[hp, st], AR[hp, :, st], start=True, stop=True)
                    pe.matmul(ps[0:NS, 5, 0:NS], AR[hp, 0, st], bt[hp, st], start=True, stop=True).then_inc(s["s_pairs"], 1)
                    pe.wait_ge(s["s_m4"], 3 * n + 3)
                    pe.matmul(ps[0:NS, 6, 0:NS], sm4[0:NS, 0], sdl, start=True, stop=True).then_inc(s["s_inv"], 1)
                    pe.wait_ge(s["s_inv_out"], 2 * n + 1)
                    pe.matmul(ps[0:NS, 7, 0:NS], sd2, sx1, start=True, stop=True).then_inc(s["s_inv"], 1)
                    pe.matmul(ps[0:NS, 0, 0:64], sm4[0:NS, 2], tms[0:NS, 0, hp], start=True, stop=False)
                    for b in range(DB):
                        mm = pe.matmul(ps[0:NS, 0, 0:64], zaa[hp, NS * b:NS * (b + 1)], t0s[hp, b], start=False,
                                       stop=(b == DB - 1))
                    mm.then_inc(s["s_z"], 1)
                    pe.wait_ge(s["s_z_out"], n + 1)
                    pe.wait_ge(s["s_inv_out"], 2 * n + 2)
                    pe.matmul(ps[0:NS, 1, 0:64], sxt, zs[0:NS], start=True, stop=True).then_inc(s["s_u"], 1)
                    pe.wait_ge(s["s_u_out"], n + 1)
                    pe.matmul(ps[hp, 2, 0:NS], tms[0:NS, 0, hp], sm4[0:NS, 3], start=True, stop=False)
                    for b in range(DB):
                        pe.matmul(ps[hp, 2, 4 * b:4 * b + 4], t0s[hp, b], AR[hp, 1, SEQ + 4 * b:SEQ + 4 * b + 4],
                                  start=False, stop=False)
                    pe.matmul(ps[hp, 2, 0:NS], us[0:NS], sm4[0:NS, 1], start=False, stop=True).then_inc(s["s_y"], 1)
                    pe.wait_ge(s["s_blk"], 2 * (n + 1))
                    pe.matmul(ps[hp, 3, :], tms[0:NS, 1, hp], ub[0:NS], start=True, stop=False)
                    pe.matmul(ps[hp, 3, :], tms[0:NS, 2, hp], vb[0:NS], start=False, stop=True).then_inc(s["s_dstate"], 1)
                    pe.wait_ge(s["sstate"], n + 1)
                pe.wait_ge(s["s_y_out"], 2 * (j + 1))
                wide(0, k_("blk"), y_).then_inc(s["mean"], 1)
                pe.wait_ge(s["yc_sq"], j + 1)
                wide(2, k_("blk"), tA).then_inc(s["var"], 1)
                pe.wait_ge(s["yc"], j + 1)
                wide(0, lora[:, 512 + P * j:512 + P * (j + 1)], t13).then_inc(s["g"], 1)

            srcs = [aq3, pb3[:, 0:4, 0:TOK], cq3]
            pe.wait_ge(s["oB_out"], 4)
            for n in range(job_at("gate", 0), job_at("out", 0)):
                kind, idx, *_ = JOBS[n]
                if kind == "gate":
                    job(n, xn3)
                else:
                    job(n, srcs[merge_at(idx)[1]])
            pe.wait_ge(s["merged"], 8)
            for n in range(job_at("out", 0), job_at("up", 0)):
                job(n, mg)
            norm(2, TOK)
            pe.wait_ge(s["norm_out"], 24)
            for n in range(job_at("up", 0), NJOB):
                job(n, xn3)
            for jj in range(4):
                for r in range(4):
                    n = DOWN0 + 4 * jj + r
                    slab_wait(pe, n)
                    W = slab(n)
                    if r == 0 and jj == 0:
                        pe.wait_ge(s["evac_a"], lnlast)
                        pe.wait_ge(s["norm_rt"], 3)
                    if r == 0 and jj >= 2:
                        pe.wait_ge(s["down_out"], 2 * (jj - 1))
                    pe.wait_ge(s["hid"], 8 * (r + 1))
                    for sub in range(2):
                        for k in range(KT):
                            for h in range(2):
                                mm = pe.matmul(ps[:, 4 * (jj % 2) + 2 * sub + h, 0:HALF], W[:, k, P * sub:P * (sub + 1)],
                                               hid[:, 8 * r + k, h * HALF:(h + 1) * HALF],
                                               start=(r == 0 and k == 0), stop=(r == 3 and k == KT - 1))
                    mm.then_inc(s["gemm_done"], 1)
            pe.wait_ge(s["down_out"], 8)
            norm(3, TOK)

        @block.scalar
        def _(act):
            step = Steps(act, s["act_step"])

            def norm(n, src, N):
                for k in range(KT):
                    if KT * n + k >= 2:
                        act.wait_ge(s["norm_ss"], KT * n + k - 1)
                    if n >= 2:
                        act.wait_ge(s["evac_v"] if n == 2 else s["down_out"],
                                    evacuated(job_at("out", k), "v") if n == 2 else k + 1)
                    act.activation(nbuf[n][0][:, k % 2, 0:N], src[:, k], ACT.Square).then_inc(s["norm_sq"], 1)
                act.wait_ge(s["norm_ss"], KT * (n + 1))
                if n:
                    act.wait_ge(s["norm_rc"], n)
                if N > 512:
                    act.activation(h2(nbuf[n][1][:, 0:N]), pair(4), ACT.Sqrt, bias=epsc, scale=1.0 / D).then_inc(s["norm_rt"], 1)
                else:
                    act.activation(nbuf[n][1][:, 0:N], ps[:, 4, 0:N], ACT.Sqrt, bias=epsc, scale=1.0 / D).then_inc(s["norm_rt"], 1)

            def evac(n):
                kind, idx, sl, c0_, w, e = JOBS[n]
                act.wait_ge(s["gemm_done"], n + 1)
                b = 2 * (n % 2)
                src = ps[0:min(w, P), b:b + 2, 0:HALF]
                fn = ACT.Copy
                if kind == "pb":
                    if idx == 0:
                        act.wait_ge(s["pb_edge"], 2)
                    dst = pb3[:, idx]
                    act.activation(dst[:, 1:HALF + 1], ps[:, b, 0:HALF], fn)
                    act.activation(dst[:, HALF + 1:SEQ + 1], ps[:, b + 1, 0:SEQ - HALF], fn)
                    last = act.activation(dst[:, SEQ + 1:PBW].rearrange("p (b c) -> p b c", c=5)[:, :, 1:5],
                                          ps[:, b + 1, SEQ - HALF:HALF].rearrange("p (b c) -> p b c", c=4), fn)
                elif kind == "mk":
                    last = act.activation(mkT[:, idx], ps[:, b, 0:NMEM], fn)
                elif kind == "mv":
                    last = act.activation(mv[:, idx % 2, 256 * (idx // 2):256 * (idx // 2 + 1)], ps[:, b, 0:w], fn)
                elif kind == "gate":
                    if idx >= 2:
                        act.wait_ge(s["evac_v"], evacuated(job_at("branch", idx - 2), "v"))
                    dj, br = merge_at(idx)
                    last = act.activation(h2(gb[:, idx % 2]), src, ACT.Sigmoid, bias=v_("b_gate", 8 * br + dj))
                elif kind == "up":
                    if idx >= 2:
                        act.wait_ge(s["hid"], idx - 1)
                    last = act.activation(h2(ub2[:, idx % 2]), src, ACT.Relu)
                else:
                    dst = {"ik": lambda: ik, "iw": lambda: iwT[0:4], "iq": lambda: iq[:, idx], "aq": lambda: aq3[:, idx],
                           "ak": lambda: ak, "av": lambda: av, "cq": lambda: cq3[:, idx]}[kind]()
                    last = act.activation(h2(dst), src, fn)
                last.then_inc(s["evac_a"], 1)

            act.wait_ge(s["inputs_in"], 48)
            act.wait_ge(s["pool_step"], 2)
            norm(0, xT3, TOK)
            act.wait_ge(s["aux_in"], 48)
            norm(1, memT, NMEM)
            act.wait_ge(s["norm_out"], 16)
            for n in range(4):
                evac(n)
            for t in range(1, 4):
                for h in range(4):
                    act.wait_ge(s["iscore"], 4 * (t - 1) + h + 1)
                    if t >= 2:
                        act.wait_ge(s["isum"], 4 * (t - 2) + h + 1)
                    act.activation(rl[:, h, 0:P * (t + 1)], ps[:, 4 + h, 0:P * (t + 1)], ACT.Relu).then_inc(s["relu"], 1)
            for n in range(4, job_at("gate", 0)):
                evac(n)
            act.wait_ge(s["v_tok"], 1)
            act.activation(vt[:, 0:4], cut(ps[:, 6], 0, 4, P), ACT.Copy).then_inc(s["v_tok_out"], 1)
            act.activation(vt[0:NS, 4], ps[0:NS, 7, 0:P], ACT.Copy).then_inc(s["v_tok_out"], 1)
            flat = ps[:, 4:7].rearrange("p a b -> p (a b)")[:, 0:KEYS]
            for hb in range(2):
                act.wait_ge(s["s_max"], hb + 1)
                if hb:
                    act.wait_ge(s["s_pT"], hb)
                act.activation(pr, flat, ACT.Exp, bias=nm[:, 0:1], scale=0.125, accum_out=sm[:, 0:1]).then_inc(s["s_exp"], 1)
                act.wait_ge(s["s_pT"], hb + 1)
                if hb:
                    act.wait_ge(s["vs_used"], 4)
                act.activation(pt[:, 0:4], cut(ps[:, 0], 0, 4, P), ACT.Copy).then_inc(s["s_pT_out"], 1)
                act.activation(pt[:, 4:8], cut(ps[:, 1], 0, 4, P), ACT.Copy).then_inc(s["s_pT_out"], 1)
                act.activation(pt[0:NS, 8], ps[0:NS, 2, 0:P], ACT.Copy).then_inc(s["s_pT_out"], 1)
                act.wait_ge(s["vs_used"], 4 * (hb + 1))
                for g in range(2):
                    gp = slice(64 * g, 64 * g + 64)
                    dst = aq3[gp, :, SEQ + 16 * hb:SEQ + 16 * hb + 16].rearrange("p t (b q) -> p b t q", b=4)
                    src = ps[gp, 3, 0:128].rearrange("p (b g t q) -> p b g t q", b=4, g=2, t=4)[:, :, g]
                    act.activation(dst, src, ACT.Copy).then_inc(s["oA_out"], 1)
            for u in range(NU + 2):
                if u < NU:
                    t = u // 8
                    act.wait_ge(s["p_max"], u + 1)
                    if u >= 2:
                        act.wait_ge(s["p_pT"], u - 1)
                    elif u == 0:
                        act.wait_ge(s["vs_used"], 8)
                    act.activation(pp[:, u % 2, 0:P * (t + 1)], ps[:, 4 + u % 2, 0:P * (t + 1)], ACT.Exp,
                                   bias=nm[:, u % 4:u % 4 + 1], scale=0.125,
                                   accum_out=sm[:, u % 4:u % 4 + 1]).then_inc(s["p_exp"], 1)
                if 1 <= u <= NU:
                    w = u - 1
                    t = w // 8
                    act.wait_ge(s["p_pT"], w + 1)
                    if w >= 2:
                        act.wait_ge(s["pav_done"], w - 1)
                    act.activation(ppt[:, w % 2, 0:t + 1], cut(ps[:, 6 + w % 2], 0, t + 1, P),
                                   ACT.Copy).then_inc(s["p_pT_out"], 1)
                if u >= 2 and (u - 2) % 8 == 7:
                    t = (u - 2) // 8
                    act.wait_ge(s["pav_done"], u - 1)
                    act.activation(aq3[:, :, P * t:P * (t + 1)], cut(ps[:, t % 2], 0, 4, P), ACT.Copy).then_inc(s["oA_out"], 1)
            act.wait_ge(s["c_max"], 1)
            act.activation(cp, ps[:, 4, 0:NMEM], ACT.Exp, bias=nm[:, 0:1], scale=scale_c,
                           accum_out=sm[:, 0:1]).then_inc(s["c_exp"], 1)
            act.wait_ge(s["c_pT"], 1)
            act.activation(cpt, cut(ps[:, 5], 0, 2, P), ACT.Copy).then_inc(s["c_pT_out"], 1)
            act.wait_ge(s["mvs_used"], 8)
            act.activation(cq3[:, :, SEQ:TOK].rearrange("p h (b q) -> p b h q", b=DB),
                           ps[:, 2, 0:P].rearrange("p (b h q) -> p b h q", b=DB, h=4), ACT.Copy).then_inc(s["oC_out"], 1)
            for t in range(4):
                act.wait_ge(s["x_max"], t + 1)
                for h in range(4):
                    act.activation(xp[:, t % 2, h], ps[:, 4 + h // 2, NMEM * (h % 2):NMEM * (h % 2 + 1)], ACT.Exp,
                                   bias=nm[:, h:h + 1], scale=scale_c, accum_out=sm[:, h:h + 1]).then_inc(s["x_exp"], 1)
                act.wait_ge(s["x_pT"], t + 1)
                for n in range(2):
                    act.activation(xpt[:, t % 2, 4 * n:4 * n + 4], cut(ps[:, 6 + n], 0, 4, P), ACT.Copy).then_inc(s["x_pT_out"], 1)
                act.wait_ge(s["xav_done"], t + 1)
                act.activation(cq3[:, :, P * t:P * (t + 1)], cut(ps[:, t % 2], 0, 4, P), ACT.Copy).then_inc(s["oC_out"], 1)
            act.wait_ge(s["mix"], 2)
            act.activation(t12[0:64], tA[0:64], ACT.Tanh)
            act.activation(t12[64:128], tA[64:128], ACT.Copy).then_inc(s["t12"], 1)
            act.activation(t13, tB, ACT.Sigmoid).then_inc(s["t12"], 1)
            for j in range(4):
                act.wait_ge(s["half_bias"], 2)
                act.wait_ge(s["lora_up"], 2 * j + 1)
                act.activation(h2(lw), pair(0), ACT.Tanh, bias=hw0[:, j:j + 1], scale=0.5).then_inc(s["tanhs"], 1)
                act.wait_ge(s["lora_up"], 2 * j + 2)
                act.activation(h2(a_), pair(2), ACT.Tanh, bias=ha0[:, j:j + 1], scale=0.5).then_inc(s["tanhs"], 1)
                act.wait_ge(s["kk"], 2 * j + 1)
                act.wait_ge(s["t12"], 2)
                act.activation(tA, kk, ACT.Square).then_inc(s["kk_sq"], 1)
                act.wait_ge(s["kk_ss"], j + 1)
                act.activation(h2(tA), pair(0), ACT.Sqrt).then_inc(s["kk_rt"], 1)
                act.wait_ge(s["lx"], j + 1)
                act.activation(tA, L_, ACT.Exp).then_inc(s["exps"], 1)
                act.activation(tB, L_, ACT.Exp, scale=-1.0).then_inc(s["exps"], 1)
                act.activation(lw, a_, ACT.Exp).then_inc(s["exps"], 1)
                act.activation(scf, scf, ACT.Exp).then_inc(s["exps"], 1)
                act.wait_ge(s["tm"], j + 1)
                for n in range(3):
                    act.activation(tm[:, n], cut(ps[:, n], 0, 4, P), ACT.Copy).then_inc(s["tm_out"], 1)
                act.activation(tms[0:NS], cut(ps[0:NS, 3], 0, 3, P), ACT.Copy).then_inc(s["tm_out"], 1)
                for hh in range(2):
                    g = 2 * j + hh
                    hp = slice(64 * hh, 64 * hh + 64)
                    for r in range(3):
                        for c in range(4):
                            act.wait_ge(s["round"], 16 * g + 4 * r + c + 1)
                            act.activation(dx[:, c, 0::2], cut(ps[:, 4 + c], 0, 4, P)[:, 0::2], ACT.Copy).then_inc(s["dsq"], 1)
                    for l in range(3):
                        for c in range(4):
                            act.wait_ge(s["mx"], 12 * g + 4 * l + c + 1)
                            act.activation(tt[:, c], ps[:, 4 + c, 0:P], ACT.Copy).then_inc(s["mx_out"], 1)
                    for c in range(4):
                        n = 4 * g + c
                        act.wait_ge(s["z"], n + 1)
                        act.activation(zs, ps[:, 4, 0:64], ACT.Copy).then_inc(s["z_out"], 1)
                        act.wait_ge(s["u"], n + 1)
                        act.activation(us, ps[:, 5, 0:64], ACT.Copy).then_inc(s["u_out"], 1)
                        act.wait_ge(s["ychunk"], n + 1)
                        act.activation(y_[hp, C * c:C * (c + 1)], ps[hp, 6, 0:P], ACT.Copy).then_inc(s["y_chunk"], 1)
                for hh in range(2):
                    n = 2 * j + hh
                    hp = slice(64 * hh, 64 * hh + 64)
                    act.wait_ge(s["s_z"], n + 1)
                    act.activation(zs[0:NS], ps[0:NS, 0, 0:64], ACT.Copy).then_inc(s["s_z_out"], 1)
                    act.wait_ge(s["s_u"], n + 1)
                    act.activation(us[0:NS], ps[0:NS, 1, 0:64], ACT.Copy).then_inc(s["s_u_out"], 1)
                    act.wait_ge(s["s_y"], n + 1)
                    act.activation(y_[hp, SEQ:TOK], ps[hp, 2, 0:NS], ACT.Copy).then_inc(s["s_y_out"], 1)
                act.wait_ge(s["yc"], j + 1)
                act.activation(tA, y_, ACT.Square).then_inc(s["yc_sq"], 1)
                act.wait_ge(s["var"], j + 1)
                act.activation(h2(tA), pair(2), ACT.Sqrt, bias=gneps, scale=1.0 / 64).then_inc(s["y_rt"], 1)
            for n in range(job_at("gate", 0), job_at("out", 0)):
                if JOBS[n][5] == "a":
                    if n == job_at("gate", 0):
                        act.wait_ge(s["oB_out"], 4)
                    evac(n)
            norm(2, xT3, TOK)
            act.wait_ge(s["norm_out"], 24)
            for n in range(job_at("up", 0), NJOB):
                evac(n)
            norm(3, xT3, TOK)

        @block.vector
        def _(dve):
            step = Steps(dve, s["dve_step"])

            def norm(n, src, dst, N, g):
                dve.wait_ge(s["norm_rt"], n + 1)
                if n:
                    dve.wait_ge(s["norm_out"], 8 * n)
                rt, rc = nbuf[n][1:]
                dve.reciprocal(rc[:, 0:N], rt[:, 0:N]).then_inc(s["norm_rc"], 1)
                dve.wait_ge(s["norm_rc"], n + 1)
                for k in range(KT):
                    dve.scalar_tensor_tensor(dst[:, k], src[:, k], v_(g, k), rc[:, 0:N], ALU.mult,
                                             ALU.mult).then_inc(s["norm_out"], 1)

            def rope(n):
                kind, idx, raw = ROPE[n]
                dve.wait_ge(s["rope_rot"], n + 1)
                if n:
                    dve.wait_ge(s["rope_out"], n)
                dve.tensor_tensor(h2(rope1), pair(4 + 2 * (n % 2)), h2(k_("sin")), ALU.mult).then_inc(s["rope_sin"], 1)
                dve.wait_ge(s["rope_sin"], n + 1)
                dve.wait_ge(s["rope_cos"], n + 1)
                dve.tensor_tensor(raw, rope1, rope2[:, n % 2], ALU.add).then_inc(s["rope_out"], 1)

            dve.wait_ge(s["inputs_in"], 48)
            dve.tensor_copy(identb[:, :], ident).then_inc(s["bf_const"], 1)
            dve.tensor_copy(repb[0:NS, :], k_("rep")[0:NS]).then_inc(s["bf_const"], 1)
            dve.tensor_scalar(hw0, vec[:, VOFF["rwkv_w0"][0]:VOFF["rwkv_w0"][0] + 4], 0.5, None, ALU.mult).then_inc(s["half_bias"], 1)
            dve.tensor_scalar(ha0, vec[:, VOFF["rwkv_a0"][0]:VOFF["rwkv_a0"][0] + 4], 0.5, None, ALU.mult).then_inc(s["half_bias"], 1)
            dve.wait_ge(s["inputs_in"], 48)
            norm(0, xT3, xn3, TOK, "norm_mix_g")
            norm(1, memT, memn, NMEM, "norm_mem_g")
            for n in range(3):
                rope(n)
            dve.wait_ge(s["pool_step"], 3)
            dve.wait_ge(s["rope_out"], 3)
            for h in range(4):
                hp = slice(64 * (h % 2), 64 * (h % 2) + 64)
                dst = zi[0:64, 32 * h:32 * h + DB * 132].rearrange("p (b c) -> p b c", c=132)[:, :, 0:4] if h < 4 else None
                dve.tensor_copy(dst, iq[hp, h // 2, SEQ:TOK].rearrange("p (b q) -> p b q", q=4)).then_inc(s["zi_set"], 1)
            dve.wait_ge(s["iw_tok"], 1)
            step(dve.tensor_scalar(iwc[:, 0:16], ps[:, 7, 0:16], 0.0625, None, ALU.mult))
            step(dve.tensor_scalar(iwc[0:NS, 16:20], ps[0:NS, 7, 16:20], 0.0625, None, ALU.mult))
            for h in range(4):
                step(dve.tensor_copy(iws[32 * h:32 * h + 32], iwc[0:NS, 16 + h:17 + h]))
            flat = ps[:, 4:7].rearrange("p a b -> p (a b)")[:, 0:KEYS]
            dve.wait_ge(s["ki_used"], 8)
            dve.tensor_scalar(rs, flat, 0.0, iws, ALU.max, ALU.mult).then_inc(s["rs"], 1)
            dve.wait_ge(s["ssum"], 1)
            step(dve.tensor_copy(ss[:, 0:PAST], flat[0:NS, 0:PAST]))
            dve.tensor_tensor(ss[:, PAST:KEYS], flat[0:NS, PAST:KEYS], k_("snew")[0:NS], ALU.add).then_inc(s["ss_out"], 1)
            dve.wait_ge(s["ss_out"], 1)
            dve.tensor_copy(biasp[:, 0, 0:P], k_("caus")).then_inc(s["bias_done"], 1)

            def select(sc, m8, k):
                for _ in range(k // 8):
                    step(dve.max(m8, sc))
                    step(dve.match_replace(sc, m8, sc, GONE))

            m8 = small[:, 132:140]
            for t in range(1, 4):
                n = P * (t + 1)
                sc = scp[:, 0:n]
                for h in range(4):
                    dve.wait_ge(s["relu"], 4 * (t - 1) + h + 1)
                    if h == 0:
                        ins = dve.tensor_scalar(sc, rl[:, 0, 0:n], iwc[:, 4 * t:4 * t + 1], None, ALU.mult)
                    else:
                        dve.wait_ge(s["isum"], 4 * (t - 1) + h)
                        ins = dve.scalar_tensor_tensor(sc, rl[:, h, 0:n], iwc[:, 4 * t + h:4 * t + h + 1], sc, ALU.mult, ALU.add)
                    ins.then_inc(s["isum"], 1)
                dve.wait_ge(s["isum"], 4 * t)
                step(dve.tensor_tensor(sc[:, P * t:n], sc[:, P * t:n], k_("caus"), ALU.add))
                select(sc, m8, TOPK_P)
                dve.tensor_scalar(biasp[:, t, 0:n], sc, -2e38, NEG, ALU.is_gt, ALU.mult).then_inc(s["bias_done"], 1)
                dve.wait_ge(s["bias_done"], t + 1)
            select(ss, m8[0:NS], TOPK_S)
            dve.tensor_scalar(biass[0:NS], ss, -2e38, NEG, ALU.is_gt, ALU.mult).then_inc(s["selected"], 1)
            dve.memset(small[:, 140:141], 0.0).then_inc(s["selected"], 1)
            for n in range(3, 8):
                rope(n)
            dve.wait_ge(s["pool_step"], 4)
            dve.wait_ge(s["rope_out"], 8)
            for hb in range(2):
                for g in range(2):
                    gp = slice(64 * g, 64 * g + 64)
                    dst = za[gp, 640 * hb:640 * hb + 640].rearrange("p (b c) -> p b c", c=160)[:, :, 16 * g:16 * g + 16]
                    dst = dst.rearrange("p b (t q) -> p b t q", q=4)
                    src = aq3[gp, :, SEQ + 16 * hb:SEQ + 16 * hb + 16].rearrange("p t (b q) -> p b t q", b=4)
                    dve.tensor_copy(dst, src).then_inc(s["za_set"], 1)
            for hb in range(2):
                dve.wait_ge(s["s_score"], hb + 1)
                step(dve.tensor_reduce(mx[:, 0:1], flat, AX.X, ALU.max))
                if hb:
                    dve.wait_ge(s["s_exp"], hb)
                dve.tensor_scalar(nm[:, 0:1], mx[:, 0:1], -0.125, None, ALU.mult).then_inc(s["s_max"], 1)
                dve.wait_ge(s["s_exp"], hb + 1)
                step(dve.reciprocal(ri[:, 0:1], sm[:, 0:1]))
                dve.tensor_scalar(pr, pr, ri[:, 0:1], None, ALU.mult).then_inc(s["s_prob"], 1)
            dve.wait_ge(s["s_prob"], 2)
            for u in range(NU + 1):
                if u < NU:
                    t, q = u // 8, u % 4
                    dve.wait_ge(s["p_score"], u + 1)
                    if u >= 4:
                        dve.wait_ge(s["p_exp"], u - 3)
                    step(dve.tensor_reduce(mx[:, q:q + 1], ps[:, 4 + u % 2, 0:P * (t + 1)], AX.X, ALU.max))
                    dve.tensor_scalar(nm[:, q:q + 1], mx[:, q:q + 1], -0.125, None, ALU.mult).then_inc(s["p_max"], 1)
                if u >= 1:
                    w = u - 1
                    t, q = w // 8, w % 4
                    dve.wait_ge(s["p_exp"], w + 1)
                    step(dve.reciprocal(ri[:, q:q + 1], sm[:, q:q + 1]))
                    dve.tensor_scalar(pp[:, w % 2, 0:P * (t + 1)], pp[:, w % 2, 0:P * (t + 1)], ri[:, q:q + 1], None,
                                      ALU.mult).then_inc(s["p_prob"], 1)
            dve.wait_ge(s["pool_step"], 7)
            dve.tensor_copy(zc.rearrange("p (b h c) -> p b h c", b=DB, h=4)[:, :, :, 0:4],
                            cq3[:, :, SEQ:TOK].rearrange("p h (b q) -> p b h q", b=DB)).then_inc(s["zc_set"], 1)
            dve.wait_ge(s["mks_used"], 8)
            dve.wait_ge(s["p_prob"], NU)
            step(dve.tensor_reduce(mx[:, 0:1], ps[:, 4, 0:NMEM], AX.X, ALU.max))
            dve.tensor_scalar(nm[:, 0:1], mx[:, 0:1], -scale_c, None, ALU.mult).then_inc(s["c_max"], 1)
            dve.wait_ge(s["c_exp"], 1)
            step(dve.reciprocal(ri[:, 0:1], sm[:, 0:1]))
            dve.tensor_scalar(cp, cp, ri[:, 0:1], None, ALU.mult).then_inc(s["c_prob"], 1)
            for t in range(4):
                dve.wait_ge(s["x_score"], t + 1)
                step(dve.tensor_reduce(mx, ps[:, 4:6].rearrange("p a (h m) -> p (a h) m", h=2), AX.X, ALU.max))
                dve.tensor_scalar(nm, mx, -scale_c, None, ALU.mult).then_inc(s["x_max"], 1)
                dve.wait_ge(s["x_exp"], 4 * (t + 1))
                step(dve.reciprocal(ri, sm))
                dve.tensor_tensor(xp[:, t % 2], xp[:, t % 2], ri.unsqueeze(2).to_broadcast([P, 4, NMEM]),
                                  ALU.mult).then_inc(s["x_prob"], 1)

            def mix(dst, tile, n):
                cur = pb3[:, tile]
                dve.wait_ge(s["diff"], n + 1)
                mu = v_("rwkv_mu", tile)
                dve.scalar_tensor_tensor(dst[:, 0:SEQ], dst[:, 0:SEQ], mu, cur[:, 1:SEQ + 1], ALU.mult, ALU.add)
                d4 = dst[:, SEQ:TOK].rearrange("p (b c) -> p b c", c=4)
                c5 = cur[:, SEQ + 1:PBW].rearrange("p (b c) -> p b c", c=5)
                dve.scalar_tensor_tensor(d4, d4, mu, c5[:, :, 1:5], ALU.mult, ALU.add).then_inc(s["mix"], 1)

            mix(tA, 12, 0)
            mix(tB, 13, 1)
            CL = -0.5 * float(np.exp(-0.5))
            for j in range(4):
                for n, (dst, tile) in enumerate(((r_, j), (k__, 4 + j), (v__, 8 + j))):
                    mix(dst, tile, 2 + 3 * j + n)
                dve.wait_ge(s["mix"], 2 + 3 * (j + 1))
                dve.tensor_scalar(kk, k__, v_("rwkv_k_k", j), None, ALU.mult).then_inc(s["kk"], 1)
                dve.wait_ge(s["tanhs"], 2 * j + 1)
                step(dve.tensor_scalar(lw, lw, CL, CL, ALU.mult, ALU.add))
                dve.wait_ge(s["tanhs"], 2 * j + 2)
                step(dve.tensor_scalar(a_, a_, 0.5, 0.5, ALU.mult, ALU.add))
                step(dve.tensor_tensor_scan(L_, k_("reset"), lw, 0.0, ALU.mult, ALU.add))
                dve.wait_ge(s["kk_rt"], j + 1)
                step(dve.tensor_scalar(tA, tA, 1e-12, None, ALU.max))
                step(dve.reciprocal(tB, tA))
                dve.tensor_tensor(kk, kk, tB, ALU.mult).then_inc(s["kk"], 1)
                dve.wait_ge(s["kk"], 2 * j + 2)
                dve.tensor_tensor(bt, kk, a_, ALU.mult)
                step(dve.tensor_scalar(tB, a_, 1.0, v_("rwkv_k_a", j), ALU.subtract, ALU.mult))
                step(dve.scalar_tensor_tensor(kh, tB, 1.0, k__, ALU.add, ALU.mult))
                step(dve.tensor_copy(c0, L_[:, C // 2 - 1:SEQ:C]))
                l3 = L_[:, 0:SEQ].rearrange("p (c t) -> p c t", c=4)
                step(dve.tensor_tensor(l3, l3, c0.unsqueeze(2).to_broadcast([P, 4, C]), ALU.subtract))
                step(dve.tensor_copy(scf, L_[:, C - 1:SEQ:C]))
                step(dve.tensor_tensor(scf[:, 0:3], scf[:, 0:3], c0[:, 1:4], ALU.add))
                dve.tensor_tensor(a_, L_, lw, ALU.subtract).then_inc(s["lx"], 1)
                dve.wait_ge(s["exps"], 4 * (j + 1))
                dve.scalar_tensor_tensor(L_, r_, v_("rwkv_r_k", j), kh, ALU.mult, ALU.mult).then_inc(s["rk"], 1)
                dve.tensor_copy(sdec, tA[:, SEQ + 3:TOK:4])
                dve.tensor_tensor(AR[:, 1], r_, tA, ALU.mult)
                dve.scalar_tensor_tensor(AR[:, 0], kk, -1.0, lw, ALU.mult, ALU.mult)
                dve.tensor_tensor(bt, bt, tB, ALU.mult)
                dve.tensor_tensor(kt_, kh, tB, ALU.mult).then_inc(s["factors"], 1)
                dve.wait_ge(s["rk_sum"], j + 1)
                dve.tensor_tensor(h2(L_), pair(2), h2(v__), ALU.mult).then_inc(s["bonus"], 1)
                for hh in range(2):
                    g = 2 * j + hh
                    hp = slice(64 * hh, 64 * hh + 64)
                    for c in range(4):
                        dve.wait_ge(s["pairs"], 4 * g + c + 1)
                        if c == 0 and hh == 0 and j:
                            dve.wait_ge(s["t0s_out"], 16 * j)
                        dve.tensor_tensor(m4[:, c], cut(ps[:, 4 + c], 0, 4, P), cut(cst, COFF["mask4"][0], 4, P),
                                          ALU.mult).then_inc(s["m4"], 1)
                    for c in range(4):
                        dve.wait_ge(s["low"], 4 * g + c + 1)
                        dve.tensor_tensor(dx[:, c, 0], ps[:, c, 0:P], k_("mlow"), ALU.mult).then_inc(s["dlow"], 1)
                    for r in range(1, 4):
                        for c in range(4):
                            dve.wait_ge(s["round"], 16 * g + 4 * r + c + 1)
                            dve.tensor_tensor(dx[:, c, 1::2], dx[:, c, 1::2], cut(ps[:, c], 0, 2, P),
                                              ALU.add).then_inc(s["xup"], 1)
                    for l in range(3):
                        for c in range(4):
                            dve.wait_ge(s["xmx"], 12 * g + 4 * l + c + 1)
                            if l < 2:
                                ins = dve.tensor_tensor(dx[:, c, 1::2], dx[:, c, 1::2], cut(ps[:, c], 0, 2, P), ALU.add)
                            else:
                                ins = dve.tensor_tensor(dx[:, c, 3], dx[:, c, 3], ps[:, c, P:256], ALU.add)
                            ins.then_inc(s["xlev"], 1)
                    for c in range(4):
                        n = 4 * g + c
                        dve.wait_ge(s["dstate"], n + 1)
                        if c:
                            dve.wait_ge(s["ychunk"], n)
                            dve.wait_ge(s["ychunk"], n + 1)
                            step(dve.tensor_tensor(T0[hp], T0[hp], ps[hp, 7, 0:64], ALU.add))
                            ins = dve.tensor_scalar(T0[hp], T0[hp], scf[hp, c:c + 1], None, ALU.mult)
                        else:
                            if j:
                                dve.wait_ge(s["T0_out"], 16 * j)
                            ins = dve.tensor_scalar(T0[hp], ps[hp, 7, 0:64], scf[hp, 0:1], None, ALU.mult)
                        ins.then_inc(s["state"], 1)
                for hh in range(2):
                    n = 2 * j + hh
                    hp = slice(64 * hh, 64 * hh + 64)
                    dve.wait_ge(s["s_pairs"], n + 1)
                    dve.tensor_tensor(sm4[0:NS], cut(ps[0:NS, 4], 0, 4, NS), cut(cst, COFF["smask4"][0], 4, NS)[0:NS],
                                      ALU.mult).then_inc(s["s_m4"], 1)
                    dve.tensor_tensor(sdl, ps[0:NS, 5, 0:NS], k_("slow")[0:NS], ALU.mult).then_inc(s["s_m4"], 1)
                    dve.wait_ge(s["s_m4"], 3 * n + 2)
                    dve.tensor_tensor(sx1, sm4[0:NS, 0], ident[0:NS, 0:NS], ALU.add).then_inc(s["s_m4"], 1)
                    dve.wait_ge(s["s_inv"], 2 * n + 1)
                    dve.tensor_copy(sd2, ps[0:NS, 6, 0:NS]).then_inc(s["s_inv_out"], 1)
                    dve.wait_ge(s["s_inv"], 2 * n + 2)
                    dve.tensor_tensor(sxt, sx1, ps[0:NS, 7, 0:NS], ALU.add).then_inc(s["s_inv_out"], 1)
                    bl = k_("sblk")[0:NS].unsqueeze(2).to_broadcast([NS, DB, 64])
                    dve.tensor_tensor(vb[0:NS], tms[0:NS, 0:1, hp].to_broadcast([NS, DB, 64]), bl, ALU.mult).then_inc(s["s_blk"], 1)
                    dve.wait_ge(s["s_u_out"], n + 1)
                    dve.tensor_tensor(ub[0:NS], us[0:NS].unsqueeze(1).to_broadcast([NS, DB, 64]), bl, ALU.mult).then_inc(s["s_blk"], 1)
                    dve.wait_ge(s["s_dstate"], n + 1)
                    step(dve.tensor_tensor(t0s[hp], t0s[hp], cut(ps[hp, 3], 0, DB, 64), ALU.add))
                    dve.tensor_tensor(t0s[hp], t0s[hp], sdec[hp].unsqueeze(2).to_broadcast([64, DB, 64]), ALU.mult).then_inc(s["sstate"], 1)
                dve.wait_ge(s["mean"], j + 1)
                dve.scalar_tensor_tensor(h2(y_), pair(0), -1.0 / 64, h2(y_), ALU.mult, ALU.add).then_inc(s["yc"], 1)
                dve.wait_ge(s["y_rt"], j + 1)
                step(dve.reciprocal(tB, tA))
                step(dve.tensor_tensor(y_, y_, tB, ALU.mult))
                step(dve.tensor_scalar(y_, y_, v_("rwkv_ln_g", j), v_("rwkv_ln_b", j), ALU.mult, ALU.add))
                step(dve.tensor_tensor(y_, y_, L_, ALU.add))
                dve.wait_ge(s["g"], j + 1)
                dve.tensor_tensor(h2(pb3[:, j, 0:TOK]), pair(0), h2(y_), ALU.mult).then_inc(s["oB_out"], 1)

            for n in range(job_at("gate", 0), job_at("out", 0)):
                kind, idx, _, _, _, e = JOBS[n]
                if e != "v":
                    continue
                b = 2 * (n % 2)
                dve.wait_ge(s["gemm_done"], n + 1)
                out_of(n - 1, dve)
                dj, br = merge_at(idx)
                if br == 0:
                    dve.tensor_tensor(h2(mg[:, dj]), pair(b), h2(gb[:, idx % 2]), ALU.mult).then_inc(s["evac_v"], 1)
                    dve.wait_ge(s["evac_v"], evacuated(n, "v"))
                else:
                    dve.tensor_tensor(h2(mt), pair(b), h2(gb[:, idx % 2]), ALU.mult).then_inc(s["evac_v"], 1)
                    dve.wait_ge(s["evac_v"], evacuated(n, "v"))
                    ins = dve.tensor_tensor(mg[:, dj], mg[:, dj], mt, ALU.add)
                    if br == 2:
                        ins.then_inc(s["merged"], 1)
                        dve.wait_ge(s["merged"], dj + 1)
                    else:
                        step(ins)
            for n in range(job_at("out", 0), job_at("up", 0)):
                dve.wait_ge(s["gemm_done"], n + 1)
                dve.tensor_tensor(h2(xT3[:, JOBS[n][1]]), pair(2 * (n % 2)), h2(xT3[:, JOBS[n][1]]), ALU.add).then_inc(s["evac_v"], 1)
            norm(2, xT3, xn3, TOK, "norm_mlp_g")
            dve.wait_ge(s["t0s_out"], 16 * 4)
            for j in range(32):
                out_of(job_at("up", j), dve)
                dve.tensor_tensor(hid[:, j], ub2[:, j % 2], ub2[:, j % 2], ALU.mult).then_inc(s["hid"], 1)
            for jj in range(4):
                dve.wait_ge(s["gemm_done"], NJOB + 4 * (jj + 1))
                for sub in range(2):
                    j = 2 * jj + sub
                    dve.tensor_tensor(h2(xT3[:, j]), pair(4 * (jj % 2) + 2 * sub), h2(xT3[:, j]), ALU.add).then_inc(s["down_out"], 1)
            dve.wait_ge(s["down_out"], 8)
            norm(3, xT3, xn3, TOK, "norm_final_g")


_OUTS = {"yT": (P, KT, TOK), "kT": (P, TOK), "vT": (P, TOK), "ikT": (64, TOK), "mkT": (P, 4, NMEM), "mv": (P, 2, 512),
         "wkvP": (4, P, 64), "wkvS": (4, P, DB, 64), "shT": (P, PBT * 9)}


def kernel(**a):
    import concourse.bacc as bacc
    from concourse.bass_utils import run_bass_kernel_spmd

    a = {k: np.asarray(v) for k, v in a.items()}
    n_phys = a["cache_k"].shape[0]

    def feat(x):
        return np.ascontiguousarray(x.T.reshape(-1, P, x.shape[0]).transpose(1, 0, 2))

    order = np.concatenate([np.arange(64) + 64 * (t + o) for t in range(4) for o in (0, 4)])
    w = {k: a[k] for k in ("w_in", "w_mem_kv", "w_branch_b", "w_branch_c", "w_out", "w_mlp_up", "w_mlp_down")}
    w["w_branch_a"] = a["w_branch_a"][order]
    slabs = np.zeros((NSLAB, P, SLABW), np.float32)
    for n, (name, r0, kts, cols) in enumerate(SLABS):
        m = np.concatenate([w[name][r0:r0 + kts * P, c:c + k] for c, k in cols], 1)
        slabs[n, :, 0:kts * m.shape[1]] = m.reshape(kts, P, -1).transpose(1, 0, 2).reshape(P, -1)
    ins = {
        "xT": feat(np.concatenate([a["x_prompt"].reshape(SEQ, D), a["x_sample"].reshape(NS, D)])),
        "memT": feat(a["mem_prompt"].reshape(NMEM, D)),
        "const": constants(),
        "vec": np.concatenate([a[k].reshape(-1, P).T for k, _ in VECS], 1),
        "slabs": slabs,
        "lora": np.concatenate([np.concatenate([a["rwkv_w_up"], a["rwkv_a_up"]], 0), a["rwkv_g_up"]], 1),
        "shT": feat(a["state_shift"]).reshape(P, -1),
        "pages": a["page_table"].reshape(1, -1),
        "ki": a["cache_idx_k"].transpose(0, 2, 1),
        "kT": a["cache_k"].reshape(n_phys, PAGE, P).transpose(0, 2, 1),
        "v": a["cache_v"].reshape(n_phys, PAGE, P),
        "mks": a["cache_mem_k"].transpose(0, 3, 2, 1).reshape(DB, P, 4 * NMEM),
        "mvs": a["cache_mem_v"].reshape(DB, 2, P, 512).transpose(0, 2, 1, 3).reshape(DB, P, 1024),
        "wkvT": a["state_wkv"].transpose(1, 3, 0, 2).reshape(4, P, DB, 64),
    }
    nc = bacc.Bacc("TRN2", target_bir_lowering=False, num_devices=1)
    arrays, i, o = {}, {}, {}
    for k, x in ins.items():
        x = np.ascontiguousarray(x)
        arrays["in_" + k] = x
        i[k] = nc.dram_tensor("in_" + k, x.shape, mybir.dt.from_np(x.dtype), kind="ExternalInput").ap()
    for k, shape in _OUTS.items():
        o[k] = nc.dram_tensor("out_" + k, shape, F32, kind="ExternalOutput").ap()
    build(nc, i, o)
    r = run_bass_kernel_spmd(nc, [arrays], core_ids=[0]).results[0]
    g = {k: r["out_" + k] for k in _OUTS}
    y = g["yT"].transpose(2, 1, 0).reshape(TOK, D)
    k, v, ik = g["kT"].T, g["vT"].T, g["ikT"].T
    sh = g["shT"].reshape(P, PBT, 9).transpose(2, 1, 0).reshape(9, PB)
    mkT = g["mkT"].reshape(P, 4, NMEM).transpose(2, 1, 0)
    mv = g["mv"].transpose(1, 0, 2).reshape(NMEM, 4, P)
    wp = g["wkvP"].reshape(8, 64, 64).transpose(0, 2, 1)
    ws = g["wkvS"].reshape(8, 64, DB, 64).transpose(2, 0, 3, 1)
    out = (y[:SEQ].reshape(1, SEQ, D), y[SEQ:].reshape(DB, DS, D), k[:SEQ].reshape(1, SEQ, 2, 64), v[:SEQ].reshape(1, SEQ, 2, 64),
           ik[:SEQ].reshape(1, SEQ, 64), mkT[None], mv[None], wp[None], sh[0:1], k[SEQ:].reshape(DB, DS, 2, 64),
           v[SEQ:].reshape(DB, DS, 2, 64), ik[SEQ:].reshape(DB, DS, 64), ws, sh[1:])
    return tuple(np.ascontiguousarray(x) for x in out)
```

```python
from contextlib import ExitStack

import numpy as np
import concourse.bass as bass
from concourse import mybir

F32 = mybir.dt.float32
F32R = mybir.dt.float32r
BF16 = mybir.dt.bfloat16
I32 = mybir.dt.int32
U32 = mybir.dt.uint32
ALU = mybir.AluOpType
ACT = mybir.ActivationFunctionType
AX = mybir.AxisListType

P = 128
D = 1024
KT = D // P
SEQ, DB, DS = 512, 8, 4
NS = DB * DS
TOK = SEQ + NS
HALF = TOK // 2
PAST, PAGE, TOPK_P, TOPK_S = 1024, 128, 128, 256
KEYS = PAST + NS
NMEM = 256
PB = 1792
PBT = PB // P
PBW = SEQ + 1 + DB * (DS + 1)
C = 128
NCH = SEQ // C
FF = 4096
NEG, GONE = -1e30, -3e38
EPS, GN_EPS = 1e-6, 64e-5
SLABW = KT * 256
RING = 5

AQ, AK, AV, IQ, IK, PBC = 0, 512, 640, 768, 1024, 1092
CQ = PBC + PB
GATE = CQ + 512

CONSTS = [("ident", 128), ("rot", 128), ("blk", 128), ("ones", 128), ("cos", TOK), ("sin", TOK),
          ("mask4", 512), ("lev", 512), ("mlow", 128), ("reset", TOK), ("caus", 128),
          ("rep", 256), ("sel", 32), ("smask4", 128), ("slow", 32), ("snew", 32), ("sblk", 8)]
COFF, _n = {}, 0
for _k, _w in CONSTS:
    COFF[_k] = (_n, _w)
    _n += _w
NCONST = _n


def constants():
    c = {k: np.zeros((P, w), np.float32) for k, w in CONSTS}
    c["ident"][:] = np.eye(P)
    for base in (0, 64):
        for i in range(8):
            c["rot"][base + 8 + i, base + i] = -1.0
            c["rot"][base + i, base + 8 + i] = 1.0
    f = np.arange(P)
    c["blk"][:] = (f[:, None] // 64 == f[None, :] // 64)
    c["ones"][:] = 1.0
    pos = np.concatenate([np.arange(SEQ), np.tile(PAST + np.arange(DS), DB)]).astype(np.float32)
    inv = (np.float32(500000.0) ** (-np.arange(8, dtype=np.float32) / np.float32(8))).astype(np.float32)
    ang = (pos[None, :] * inv[:, None]).astype(np.float32)
    c["cos"][:] = 1.0
    for base in (0, 8, 64, 72):
        c["cos"][base:base + 8] = np.cos(ang)
        c["sin"][base:base + 8] = np.sin(ang)
    s, t = f[:, None], f[None, :]
    strict, incl = (s < t), (s <= t)
    c["mask4"][:] = np.concatenate([strict, incl, strict, incl], 1)
    lev = [strict & (s // 16 == t // 16)]
    for b in (16, 32, 64):
        lev.append((s // (2 * b) == t // (2 * b)) & (s // b < t // b))
    c["lev"][:] = np.concatenate(lev, 1)
    c["mlow"][:] = lev[0].T
    c["reset"][:] = 1.0
    c["reset"][:, 0:SEQ:C] = 0.0
    c["reset"][:, SEQ::DS] = 0.0
    c["caus"][:] = np.where(t > s, NEG, 0.0)
    r = np.arange(P)
    for hb in range(2):
        c["rep"][(hb * 4 + r // 32) * 4 + r % 4, hb * P + r] = 1.0
    c["sel"][r, r % 32] = 1.0
    a = np.arange(NS)
    sb_, tb = a[:, None], a[None, :]
    same = sb_ // 4 == tb // 4
    c["smask4"][0:NS] = np.concatenate([same & (sb_ < tb), same & (sb_ <= tb)] * 2, 1)
    c["slow"][0:NS] = same & (sb_ > tb)
    c["snew"][0:NS] = np.where(same & (tb <= sb_), 0.0, NEG)
    c["sblk"][0:NS] = sb_ // 4 == np.arange(8)[None, :]
    return np.concatenate([c[k] for k, _ in CONSTS], 1).astype(np.float32)


VECS = [("norm_mix_g", 8), ("norm_mem_g", 8), ("norm_mlp_g", 8), ("norm_final_g", 8), ("b_gate", 24),
        ("rwkv_mu", 14), ("rwkv_w0", 4), ("rwkv_a0", 4), ("rwkv_k_k", 4), ("rwkv_k_a", 4),
        ("rwkv_r_k", 4), ("rwkv_ln_g", 4), ("rwkv_ln_b", 4)]
VOFF, _n = {}, 0
for _k, _w in VECS:
    VOFF[_k] = (_n, _w)
    _n += _w
NVEC = _n


MLP_ORDER = [("up", 0), ("up", 1), ("down", 0), ("up", 2), ("down", 1), ("up", 3), ("down", 2), ("down", 3)]


PB_ORDER = [12, 13] + [t for j in range(4) for t in (j, 4 + j, 8 + j)]


def slab_plan():
    def head(base, h):
        return (base + 64 * h, 64)

    s = [("w_in", 0, KT, [(IK, 64), (IK, 64), (IK + 64, 4)]), ("w_in", 0, KT, [(IQ, 256)])]
    s += [("w_in", 0, KT, [head(AQ, t + o) for t in (2 * n, 2 * n + 1) for o in (0, 4)]) for n in range(2)]
    s += [("w_in", 0, KT, [(AK, 256)])]
    s += [("w_mem_kv", 0, KT, [(256 * i, 256)]) for i in range(4)]
    s += [("w_in", 0, KT, [(CQ + 256 * i, 256)]) for i in range(2)]
    s += [("w_in", 0, KT, [(PBC + P * a, P), (PBC + P * b, P)]) for a, b in zip(PB_ORDER[::2], PB_ORDER[1::2])]
    s += [("w_in", 0, KT, [(GATE + D * i + 256 * jj, 256)]) for jj in range(4) for i in range(3)]
    s += [(f"w_branch_{'abc'[i]}", 0, 4, [(256 * jj, 256)]) for jj in range(4) for i in range(3)]
    s += [("w_out", 0, KT, [(256 * jj, 256)]) for jj in range(4)]
    for kind, r in MLP_ORDER:
        if kind == "up":
            s += [("w_mlp_up", 0, KT, [(256 * (4 * r + jj), 256)]) for jj in range(4)]
        else:
            s += [("w_mlp_down", D * r, KT, [(256 * jj, 256)]) for jj in range(4)]
    return s


def job_plan():
    jobs = [("ik", 0, 0, 0, 128, "a"), ("iw", 0, 0, 128, 4, "a"), ("iq", 0, 1, 0, 128, "a"), ("iq", 1, 1, 128, 128, "a")]
    jobs += [("aq", i, 2 + i // 2, 128 * (i % 2), 128, "a") for i in range(4)]
    jobs += [("ak", 0, 4, 0, 128, "a"), ("av", 0, 4, 128, 128, "a")]
    jobs += [("mk", h, 5 + h // 2, 128 * (h % 2), 128, "a") for h in range(4)]
    jobs += [("mv", 2 * n + m, 7 + n, 0, 256, "a") for n in range(2) for m in range(2)]
    jobs += [("cq", i, 9 + i // 2, 128 * (i % 2), 128, "a") for i in range(4)]
    jobs += [("pb", t, 11 + n // 2, 128 * (n % 2), 128, "a") for n, t in enumerate(PB_ORDER)]
    s = 18
    jobs += [("gate", m, s + m // 2, 128 * (m % 2), 128, "a") for m in range(24)]
    s += 12
    jobs += [("branch", m, s + m // 2, 128 * (m % 2), 128, "v") for m in range(24)]
    s += 12
    jobs += [("out", j, s + j // 2, 128 * (j % 2), 128, "v") for j in range(8)]
    s += 4
    for kind, r in MLP_ORDER:
        jobs += [(kind, 8 * r + j, s + j // 2, 128 * (j % 2), 128, "a" if kind == "up" else "v") for j in range(8)]
        s += 4
    return jobs


SLABS = slab_plan()
NSLAB = len(SLABS)
JOBS = job_plan()
NJOB = len(JOBS)
SPLIT0 = next(n for n, j in enumerate(JOBS) if j[0] == "branch")
SPLIT_SLAB = JOBS[SPLIT0][2]
FILL0 = next(n for n, j in enumerate(JOBS) if j[0] == "mk")
LAND = 3
FREED = {}
for _n, _j in enumerate(JOBS):
    FREED[_j[2]] = _n + 1 - (SPLIT0 if _n >= SPLIT0 else 0)


PART = {"source": 0, "merge": 12, "x": KT + 12, "hid": 2 * KT + 12}


def merge_at(m):
    return 2 * (m // 6) + m % 2, m % 6 // 2


def merges(m):
    return sum(m_ % 6 >= 2 for m_ in range(m + 1))


def job_at(kind, i=0):
    return next(n for n, j in enumerate(JOBS) if j[0] == kind and j[1] == i)


def evacuated(n, eng):
    return sum(j[5] == eng for j in JOBS[:n + 1])


def bank_of(n):
    return 2 if FILL0 <= n < SPLIT0 else 2 * (n % 2)


def before_in_bank(n):
    return next((m for m in range(n - 1, -1, -1) if bank_of(m) == bank_of(n)), None)


def fill_plan():
    steps = [(n, k) for n in range(FILL0, SPLIT0) for k in range(KT)]
    waits = [(("p", u), 5) for u in range(34)] + [(("need", "cq", 3), 0), (("need", "pb", 13), 0), (("close", "p", 0), 0)]
    waits += [(("x", t, n), 4) for t in range(4) for n in range(3)] + [(("c", n), 4) for n in range(3)]
    for j in range(4):
        waits += [(("need", "pb", 8 + j), 0)]
        waits += [(("prep", j, n), b) for n, b in enumerate((10, 16, 10))]
        waits += [(("close", "tm", j), 0)]
        for g in (2 * j, 2 * j + 1):
            waits += [(("chunk", 4 * g + c, n), 2) for c in range(4) for n in range(3)]
            if g % 2 == 0:
                waits += [(("close", "group", g), 0)]
        for g in (2 * j, 2 * j + 1):
            waits += [(("dec", g, n), 2) for n in range(5)]
        waits += [(("gn", j, n), b) for n, b in enumerate((6, 6, 10))]
    waits += [(("need", "gate", 23), 0)]
    plan, done, at = {}, {}, 0
    for tag, budget in waits:
        plan[tag], done[tag] = [], []
        while at < len(steps):
            n, k = steps[at]
            cost = 1 if JOBS[n][0] in ("mk", "mv") else 2
            if tag[0] == "need":
                if n > job_at(tag[1], tag[2]):
                    break
            elif tag[0] == "close":
                if k == 0:
                    break
            elif budget < cost:
                break
            budget -= cost
            plan[tag].append((n, k))
            if k == KT - 1:
                done[tag].append(n)
            at += 1
    assert at == len(steps)
    return plan, done


FILLS, FILLED = fill_plan()


class Sems(dict):

    def __init__(self, make):
        super().__init__()
        self.make = make

    def __missing__(self, name):
        self[name] = self.make(name)
        return self[name]


class Steps:

    def __init__(self, eng, sem):
        self.eng, self.sem, self.n = eng, sem, 0

    def __call__(self, ins):
        self.n += 1
        ins.then_inc(self.sem, 1)
        self.eng.wait_ge(self.sem, self.n)


def build(nc, i, o):
    with ExitStack() as ctx:
        def sb(name, cols, dt=F32):
            return ctx.enter_context(nc.sbuf_tensor(name, [P, cols], dt))

        s = Sems(lambda name: ctx.enter_context(nc.semaphore(name)))
        cst = sb("cst", NCONST)
        vec = sb("vec", NVEC)
        xT = sb("xT", KT * TOK)
        identb = sb("identb", 128, BF16)
        repb = sb("repb", 256, BF16)
        small = sb("small", 192)
        pages = sb("pages", DB * 8, I32)
        sh_in = sb("sh_in", PBT * DB)
        sh_out = sb("sh_out", PBT * 9 + 2)

        def over(name, off, cols, dt=F32):
            with ExitStack() as put:
                if off:
                    put.enter_context(nc.sbuf_tensor("under_" + name, [P, off], F32))
                return put.enter_context(nc.sbuf_tensor(name, [P, cols], dt))

        XN, AQO, CQO, RINGO = 0, KT * TOK, 12 * TOK, 16 * TOK
        PBO = RINGO + RING * SLABW
        RO = PBO + -(-PBT * PBW // 8) * 8
        xn, aq, cq = over("xn", XN, KT * TOK), over("aq", AQO, 4 * TOK), over("cq", CQO, 4 * TOK)
        ring, pb, R = over("ring", RINGO, RING * SLABW), over("pb", PBO, PBT * PBW), over("R", RO, 32 * TOK)
        land = over("land", RINGO, LAND * SLABW)
        wh, wl = over("wh", RINGO + 6144, 2048, F32R), over("wl", RINGO + 8192, 2048, F32R)
        FREE = PBO + -(-4 * PBW // 8) * 8
        xlo, xhi = over("xlo", XN, KT * TOK, F32R), over("xhi", RO, KT * TOK, F32R)
        alo, clo = over("alo", AQO, 4 * TOK, F32R), over("clo", CQO, 4 * TOK, F32R)
        blo, shi = over("blo", PBO, 4 * PBW, F32R), over("shi", RO + 8 * TOK, 12 * TOK, F32R)
        mhi, mlo = over("mhi", RO + 20 * TOK, 8 * TOK, F32R), over("mlo", RO + 28 * TOK, 4 * TOK, F32R)
        mlo2 = over("mlo2", FREE, 4 * TOK, F32R)
        tail = over("tail", FREE + 4 * TOK, 6 * TOK)
        hh0, hl0 = over("hh0", RO + 8 * TOK, 8 * TOK, F32R), over("hl0", RO + 16 * TOK, 8 * TOK, F32R)
        hh1, hl1 = over("hh1", RO + 24 * TOK, 8 * TOK, F32R), over("hl1", AQO, 8 * TOK, F32R)
        mlpt = over("mlpt", FREE, 4 * TOK)
        yo = over("yo", RO, KT * TOK)
        ps = ctx.enter_context(nc.psum_tensor("ps", [P, 8, 512], F32))

        def cut(t, off, *dims):
            n = int(np.prod(dims))
            a = t[:, off:off + n]
            names = "abc"[:len(dims)]
            if len(dims) == 1:
                return a
            return a.rearrange("p (%s) -> p %s" % (" ".join(names), " ".join(names)), **dict(zip(names, dims)))

        def k_(name):
            off, w = COFF[name]
            return cst[:, off:off + w]

        def v_(name, j=0):
            off, _ = VOFF[name]
            return vec[:, off + j:off + j + 1]

        ident = k_("ident")
        lora = cst[:, COFF["cos"][0]:COFF["cos"][0] + 1024]
        xT3, xn3 = cut(xT, 0, KT, TOK), cut(xn, 0, KT, TOK)
        aq3, cq3 = cut(aq, 0, 4, TOK), cut(cq, 0, 4, TOK)
        pb3 = cut(pb, 0, PBT, PBW)
        memT, memn = cut(pb, 0, KT, NMEM), cut(pb, KT * NMEM, KT, NMEM)
        ik, iwT, iq = R[:, 0:TOK], R[:, TOK:2 * TOK], cut(R, 2 * TOK, 2, TOK)
        ak, av = R[:, 4 * TOK:5 * TOK], R[:, 5 * TOK:6 * TOK]
        r0 = 6 * TOK
        vt = cut(R, r0, 5, P)
        mkT = cut(R, r0 + 640, 4, NMEM)
        mv = cut(R, r0 + 1664, 2, 512)
        biasp = cut(R, r0 + 2688, 1024).bitcast(BF16).rearrange("p (a b) -> p a b", a=4)
        biass = cut(R, r0 + 3712, KEYS // 2).bitcast(BF16)
        B = r0 + 3712 + KEYS // 2
        ki = [R[0:64, B + PAST * n:B + PAST * (n + 1)] for n in range(2)]
        ki += [R[0:64, r0 + 640 + PAST * n:r0 + 640 + PAST * (n + 1)] for n in range(2)]
        ki += [cq[0:64, PAST * n:PAST * (n + 1)] for n in range(2)]
        ki += [pb[0:64, 4096 + PAST * n:4096 + PAST * (n + 1)] for n in range(2)]
        zi = R[:, B + 2048:B + 3200]
        rs = R[:, B + 3200:B + 4256]
        ss = R[0:NS, B + 4256:B + 5312]
        rl = cut(R, B + 5312, 4, 512)
        scp = rs[:, 0:512]
        NB = 28 * TOK
        assert B + 7360 <= NB
        sq = cut(R, NB, 2, TOK)
        rt, rc = R[:, NB + 2 * TOK:NB + 3 * TOK], R[:, NB + 3 * TOK:NB + 4 * TOK]
        rope1, rope2 = rt, sq
        kvb = [cut(pb, 2048 * n, 8, 2 * P) for n in range(3)]
        kvb += [cut(R, B + 5312, 8, 2 * P), cut(R, B + 7360, 8, 2 * P)]
        za = R[:, B + 2048:B + 3328]
        pr = R[:, B + 4256:B + 5312]
        pt = cut(R, B, 9, P)
        pp, ppt = cut(R, B, 2, 512), cut(R, B + 1024, 2, 4, P)
        zc = R[:, B:B + 32 * 132]
        mks, mvs = cut(R, B + 4224, 2, 1024), cut(R, B + 6272, 2, 1024)
        cp, cpt = R[:, B + 8320:B + 8320 + NMEM], cut(R, B + 8320 + NMEM, 2, P)
        xp, xpt = cut(R, B, 2, 4, NMEM), cut(R, B + 2048, 2, 8, P)
        iwc, iws = small[:, 0:20], small[:, 20:21]
        mx, nm, sm, ri = small[:, 24:28], small[:, 28:32], small[:, 32:36], small[:, 36:40]
        epsc, gneps = small[:, 40:41], small[:, 41:42]
        hgate = small[:, 144:168]
        hw0, ha0 = small[:, 44:48], small[:, 48:52]
        c0, scf, sdec = small[:, 52:56], small[:, 56:60], small[:, 60:68]
        T0 = small[:, 68:132]
        slot = [R[:, TOK * n:TOK * (n + 1)] for n in range(14)]
        r_, k__, v__, lw, L_, a_, kk, kh = slot[:8]
        AR, bt, kt_, tA, tB = cut(R, 8 * TOK, 2, TOK), slot[10], slot[11], slot[12], slot[13]
        y_ = r_
        G = 14 * TOK
        m4 = cut(R, G, 4, 4, P)
        lev = cut(R, G + 2048, 4, 4, P)
        dx = cut(R, G + 4096, 4, 4, P)
        tt = cut(R, G + 6144, 4, P)
        tm = R[:, G + 6656:G + 6656 + 1536].rearrange("p (a b c) -> p a b c", a=3, b=4)
        zs, us = R[:, G + 8192:G + 8256], R[:, G + 8256:G + 8320]
        tms = cut(R, G + 8320, 3, P)
        assert G + 8704 <= 32 * TOK
        t0s = cut(R, G, DB, 64)
        zaa = R[:, G + 512:G + 800]
        ub, vb = cut(R, G + 1024, DB, 64), cut(R, G + 1536, DB, 64)
        sm4 = cut(R, G + 2048, 4, NS)
        sdl, sd2, sx1, sxt = (R[0:NS, G + 2176 + 32 * n:G + 2208 + 32 * n] for n in range(4))
        tail3, mlpt3 = cut(tail, 0, 6, TOK), cut(mlpt, 0, 4, TOK)
        gb, mt, acc = tail3[:, 0:3], tail3[:, 3], tail3[:, 4:6]
        ub2, hsq, nx = mlpt3[:, 0:2], mlpt3[:, 2:4], mlpt3[:, 0:2]
        nbuf = [(sq, rt, rc)] * 2 + [(tail3[:, 0:2], tail3[:, 2], tail3[:, 3])] * 2
        gst = cut(R, 30 * TOK, 2, TOK)
        t12, t13 = pb3[:, 12, 0:TOK], pb3[:, 13, 0:TOK]

        def tiles(t, n, pitch=TOK):
            return [t[:, pitch * k:pitch * k + TOK] for k in range(n)]

        X = (tiles(xhi, 8), tiles(xlo, 8))
        S = tiles(shi, 12)
        HEADS = [(S[0:4], tiles(alo, 4)), (S[4:8], tiles(blo, 4, PBW)), (S[8:12], tiles(clo, 4))]
        M = (tiles(mhi, 8), tiles(mlo, 4) + tiles(mlo2, 4))
        H = [(tiles(hh0, 8), tiles(hl0, 8)), (tiles(hh1, 8), tiles(hl1, 8))]
        SOURCES = []
        for _src, _to in zip((aq3, pb3[:, 0:4, 0:TOK], cq3), HEADS):
            SOURCES += [(_src[:, k], _to[0][k], _to[1][k]) for k in range(4)]

        def slab(n):
            w = sum(c for _, c in SLABS[n][3])
            if n >= SPLIT_SLAB:
                return cut(land, (n - SPLIT_SLAB) % LAND * SLABW, SLABS[n][2], w)
            return cut(ring, (n % RING) * SLABW, SLABS[n][2], w)

        def slab_wait(eng, n):
            if n >= SPLIT_SLAB:
                m = n - SPLIT_SLAB
                eng.wait_ge(s[f"land{m % LAND}"], 16 * (m // LAND + 1))
            else:
                eng.wait_ge(s[f"slab{n % RING}"], 16 * (n // RING + 1))

        def split_views(n):
            _, _, sl, c0_, w, _ = JOBS[n]
            kts, q = SLABS[sl][2], n % 2
            return (slab(sl)[:, :, c0_:c0_ + w], cut(wh, 1024 * q, kts, P), cut(wl, 1024 * q, kts, P))

        def weights_hi(act, n):
            if n >= NJOB:
                return
            slab_wait(act, JOBS[n][2])
            act.wait_ge(s["gemm_done"], max(n - 1, SPLIT0))
            src, hi, _ = split_views(n)
            act.activation(hi, src, ACT.Copy).then_inc(s["weights_hi"], 1)

        def weights_lo(dve, n):
            if n >= NJOB:
                return
            dve.wait_ge(s["weights_hi"], n - SPLIT0 + 1)
            src, hi, lo = split_views(n)
            dve.tensor_tensor(lo, src, hi.bitcast(F32), ALU.subtract).then_inc(s["weights_lo"], 1)

        def out_of(n, eng):
            e = JOBS[n][5]
            eng.wait_ge(s["evac_" + e], evacuated(n, e))

        def bank_free(n, eng):
            if before_in_bank(n) is not None:
                out_of(before_in_bank(n), eng)

        def page_dma(eng, dst, pages_of, b, j, sem):
            pg = eng.value_load(pages[0:1, 8 * b + j:8 * b + j + 1], min_val=0, max_val=i["ki"].shape[0] - 1)
            eng.dma_start(dst, pages_of[bass.ds(pg, 1)].rearrange("o p c -> (o p) c")).then_inc(sem, 16)

        def pair(b):
            return ps[:, b:b + 2, 0:HALF]

        def h2(t):
            return t.rearrange("p (h c) -> p h c", h=2)

        ROPE = [("ik", 0, ik), ("iq", 0, iq[:, 0]), ("iq", 1, iq[:, 1])]
        ROPE += [("aq", t, aq3[:, t]) for t in range(4)] + [("ak", 0, ak)]
        NU = 32
        scale_c = float(np.float32(128.0 ** -0.5))
        block = ctx.enter_context(nc.Block())

        @block.sync
        def _(sp):
            sp.dma_start(xT3, i["xT"]).then_inc(s["inputs_in"], 16)
            sp.dma_start(cst[:, :], i["const"]).then_inc(s["inputs_in"], 16)
            sp.dma_start(vec[:, :], i["vec"]).then_inc(s["inputs_in"], 16)

            def stream(first, last):
                for n in range(first, last):
                    _, _, kts, cols = SLABS[n]
                    w = kts * sum(c for _, c in cols)
                    if n >= RING:
                        sp.wait_ge(s["gemm_done"], FREED[n - RING])
                    off = (n % RING) * SLABW
                    sp.dma_start(ring[:, off:off + w], i["slabs"][n, :, 0:w]).then_inc(s[f"slab{n % RING}"], 16)

            stream(0, 2)
            sp.dma_start(pages[0:1, :], i["pages"]).then_inc(s["aux_in"], 16)
            sp.dma_start(memT, i["memT"]).then_inc(s["aux_in"], 16)
            sp.dma_start(sh_in[:, :], i["shT"]).then_inc(s["aux_in"], 16)
            stream(2, RING)
            sp.wait_ge(s["aux_in"], 48)
            for b in range(DB):
                for j in range(8):
                    page_dma(sp, ki[b][:, P * j:P * (j + 1)], i["ki"], b, j, s[f"ki_in{b % 2}"])

            def kv_row(b):
                for j in range(8):
                    page_dma(sp, kvb[b % 5][:, j], i["kv"], b, j, s[f"kv_in{b % 5}"])

            stream(RING, 13)
            sp.wait_ge(s["gemm_done"], job_at("mv", 3) + 1)
            for b in range(3):
                kv_row(b)
            sp.wait_ge(s["isum"], 12)
            kv_row(3)
            sp.wait_ge(s["rope_out"], 8)
            kv_row(4)
            stream(13, 17)
            for b in range(5, DB):
                sp.wait_ge(s["vs_used"], b - 4)
                kv_row(b)
            stored_gates = 0
            for n in range(17, SPLIT_SLAB + 5):
                if n < SPLIT_SLAB:
                    stream(n, n + 1)
                while stored_gates < 24 and JOBS[job_at("gate", stored_gates)][2] <= n - RING:
                    m = stored_gates
                    out_of(job_at("gate", m), sp)
                    sp.dma_start(i["gates"][m], gst[:, m % 2]).then_inc(s[f"gate_stored{m % 2}"], 16)
                    stored_gates += 1
            def gate_in(m):
                if m >= 3:
                    out_of(job_at("branch", m - 3), sp)
                sp.dma_start(gb[:, m % 3], i["gates"][m]).then_inc(s[f"gate_in{m % 3}"], 16)

            for n in range(SPLIT_SLAB, NSLAB):
                _, _, kts, cols = SLABS[n]
                w = kts * sum(c for _, c in cols)
                m = n - SPLIT_SLAB
                if m < LAND:
                    sp.wait_ge(s["gemm_done"], SPLIT0)
                else:
                    sp.wait_ge(s["weights_lo"], FREED[n - LAND])
                off = m % LAND * SLABW
                sp.dma_start(land[:, off:off + w], i["slabs"][n, :, 0:w]).then_inc(s[f"land{m % LAND}"], 16)
                if m == 1:
                    sp.wait_ge(s["oB_out"], 4)
                    for q in range(2):
                        sp.wait_ge(s[f"gate_stored{q}"], 16 * 12)
                if 1 <= m <= 12:
                    gate_in(2 * (m - 1))
                    gate_in(2 * (m - 1) + 1)

        @block.gpsimd
        def _(pool):
            step = Steps(pool, s["pool_step"])
            step(pool.memset(epsc, EPS))
            step(pool.memset(gneps, GN_EPS))
            pool.wait_ge(s["norm_out"], 16)
            step(pool.memset(zi[0:64, :], 0.0))
            pool.wait_ge(s["aux_in"], 48)

            def rope_cos(n):
                kind, idx, raw = ROPE[n]
                out_of(job_at(kind, idx), pool)
                if n == 0:
                    pool.wait_ge(s["inputs_in"], 48)
                if n >= 2:
                    pool.wait_ge(s["rope_out"], n - 1)
                pool.tensor_tensor(rope2[:, n % 2], raw, k_("cos"), ALU.mult).then_inc(s["rope_cos"], 1)

            for n in range(3):
                rope_cos(n)
            pool.wait_ge(s["rope_out"], 1)
            pool.dma_start(o["ikT"], ik[0:64, :]).then_inc(s["stored"], 16)
            for n in range(3, 8):
                rope_cos(n)

            def edges(tiles_):
                pool.memset(pb3[:, tiles_, 0:1], 0.0).then_inc(s["pb_edge"], 1)
                pool.tensor_copy(pb3[:, tiles_, SEQ + 1:PBW:5], cut(sh_in, 0, PBT, DB)[:, tiles_]).then_inc(s["pb_edge"], 1)

            edges(slice(12, 14))
            pool.wait_ge(s["ss_out"], 1)
            step(pool.memset(za, 0.0))
            pool.wait_ge(s["rope_out"], 8)
            pool.dma_start(lora, i["lora"]).then_inc(s["lora_in"], 16)
            pool.dma_start(o["kT"], ak).then_inc(s["stored"], 16)
            out_of(job_at("av"), pool)
            pool.dma_start(o["vT"], av).then_inc(s["stored"], 16)
            out_of(job_at("mv", 3), pool)
            pool.dma_start(o["mkT"], mkT).then_inc(s["stored"], 16)
            pool.dma_start(o["mv"], mv).then_inc(s["stored"], 16)
            pool.wait_ge(s["vs_used"], 8)
            edges(slice(0, 12))

            def mks_in(b):
                if b >= 2:
                    pool.wait_ge(s["mks_used"], b - 1)
                pool.dma_start(mks[:, b % 2], i["mks"][b]).then_inc(s[f"mks_in{b % 2}"], 16)

            def mvs_in(b):
                if b >= 2:
                    pool.wait_ge(s["mvs_used"], b - 1)
                pool.dma_start(mvs[:, b % 2], i["mvs"][b]).then_inc(s[f"mvs_in{b % 2}"], 16)

            for b in range(2):
                mks_in(b)
            for b in range(2):
                mvs_in(b)
            pool.wait_ge(s["xav_done"], 4)
            step(pool.memset(zc, 0.0))
            for b in range(2, DB):
                mks_in(b)
            for b in range(2, DB):
                mvs_in(b)
            pool.wait_ge(s["oC_out"], 1 + 4)
            pool.wait_ge(s["stored"], 16 * 5)
            so = cut(sh_out, 0, PBT, 9)

            def diff(dst, tile):
                cur = pb3[:, tile]
                out_of(job_at("pb", tile), pool)
                pool.tensor_copy(so[:, tile, 0:1], cur[:, SEQ:SEQ + 1])
                pool.tensor_copy(so[:, tile, 1:9], cur[:, SEQ + 5:PBW:5])
                pool.tensor_tensor(dst[:, 0:SEQ], cur[:, 0:SEQ], cur[:, 1:SEQ + 1], ALU.subtract)
                c5 = cur[:, SEQ + 1:PBW].rearrange("p (b c) -> p b c", c=5)
                pool.tensor_tensor(dst[:, SEQ:TOK].rearrange("p (b c) -> p b c", c=4), c5[:, :, 0:4], c5[:, :, 1:5],
                                   ALU.subtract).then_inc(s["diff"], 1)

            pool.wait_ge(s["pb_edge"], 4)
            diff(tA, 12)
            diff(tB, 13)
            for j in range(4):
                if j:
                    pool.wait_ge(s["oB_out"], j)
                diff(r_, j)
                diff(k__, 4 + j)
                diff(v__, 8 + j)
                for hh in range(2):
                    g = 2 * j + hh
                    for c in range(4):
                        pool.wait_ge(s["m4"], 4 * g + c + 1)
                        pool.wait_ge(s["dlow"], 4 * g + c + 1)
                        if g and c == 0:
                            pool.wait_ge(s["t0s_out"] if hh == 0 else s["state"], 16 * j if hh == 0 else 4 * g)
                        pool.tensor_tensor(lev[:, c], m4[:, c, 0:1].to_broadcast([P, 4, P]), cut(cst, COFF["lev"][0], 4, P),
                                           ALU.mult).then_inc(s["lev"], 1)
                        pool.wait_ge(s["lev"], 4 * g + c + 1)
                        pool.tensor_tensor(dx[:, c, 1], dx[:, c, 0], ident, ALU.add)
                        pool.tensor_copy(dx[:, c, 2], lev[:, c, 0])
                        pool.tensor_tensor(dx[:, c, 3], lev[:, c, 0], ident, ALU.add).then_inc(s["dx_set"], 1)
                pool.wait_ge(s["state"], 4 * (2 * j + 2))
                pool.dma_start(t0s, i["wkvT"][j]).then_inc(s["t0s_in"], 16)
                step(pool.memset(zaa, 0.0))
                for hh in range(2):
                    pbs = slice(64 * hh, 64 * hh + 64)
                    pool.tensor_copy(zaa[pbs].rearrange("p (b c) -> p b c", c=36)[:, :, 0:4],
                                     AR[pbs, 0, SEQ:TOK].rearrange("p (b c) -> p b c", c=4)).then_inc(s["zaa"], 1)
                pool.wait_ge(s["state"], 4 * (2 * j + 2))
                pool.dma_start(o["wkvP"][j], T0).then_inc(s["T0_out"], 16)
                pool.wait_ge(s["sstate"], 2 * (j + 1))
                pool.dma_start(o["wkvS"][j], t0s).then_inc(s["t0s_out"], 16)
            pool.wait_ge(s["diff"], 14)
            pool.dma_start(o["shT"], sh_out[:, 0:PBT * 9]).then_inc(s["stored"], 16)
            for k in range(KT):
                pool.wait_ge(s["norm_out"], 25 + k)
                pool.dma_start(o["yT"][:, k], cut(yo, 0, KT, TOK)[:, k]).then_inc(s["stored"], 16)
            pool.wait_ge(s["stored"], 16 * (6 + KT))
            pool.wait_ge(s["T0_out"], 16 * 4)
            pool.wait_ge(s["t0s_out"], 16 * 4)

        @block.tensor
        def _(pe):
            def norm(n, N, src_bank=4):
                hn = N // 2 if N > 512 else N
                for k in range(KT):
                    pe.wait_ge(s["norm_sq"], KT * n + k + 1)
                    for h in range(2 if N > 512 else 1):
                        mm = pe.matmul(ps[:, 4 + h, 0:hn], k_("ones"), nbuf[n][0][:, k % 2, h * hn:(h + 1) * hn],
                                       start=(k == 0), stop=(k == KT - 1))
                    mm.then_inc(s["norm_ss"], 1)

            def job(n, src, only=None):
                kind, idx, sl, c0_, w, _ = JOBS[n]
                if only in (None, 0):
                    slab_wait(pe, sl)
                    bank_free(n, pe)
                W = slab(sl)
                b = bank_of(n)
                kts = SLABS[sl][2]
                for k in range(kts) if only is None else (only,):
                    a, z = k == 0, k == kts - 1
                    if kind == "mk":
                        mm = pe.matmul(ps[:, b, 0:NMEM], W[:, k, c0_:c0_ + w], memn[:, k], start=a, stop=z)
                    elif kind == "mv":
                        m = idx % 2
                        mm = pe.matmul(ps[:, b, 0:w], memn[:, k, P * m:P * (m + 1)], W[:, k, 0:w], start=a, stop=z)
                    else:
                        for h in range(2):
                            mm = pe.matmul(ps[0:w, b + h, 0:HALF], W[:, k, c0_:c0_ + w],
                                           src[:, k, h * HALF:(h + 1) * HALF], start=a, stop=z)
                if only in (None, kts - 1):
                    mm.then_inc(s["gemm_done"], 1)

            filled = [FILL0 - 1]

            def fill(*tag):
                for n, k in FILLS[tag]:
                    job(n, xn3, only=k)
                    filled[0] = n

            def fill_close(*tag):
                fill("close", *tag)
                out_of(filled[0], pe)

            def rope(n):
                kind, idx, raw = ROPE[n]
                out_of(job_at(kind, idx), pe)
                if n >= 2:
                    pe.wait_ge(s["rope_sin"], n - 1)
                for h in range(2):
                    mm = pe.matmul(ps[:, 4 + 2 * (n % 2) + h, 0:HALF], k_("rot"), raw[:, h * HALF:(h + 1) * HALF],
                                   start=True, stop=True)
                mm.then_inc(s["rope_rot"], 1)

            pe.wait_ge(s["inputs_in"], 48)
            norm(0, TOK)
            pe.wait_ge(s["norm_rt"], 1)
            norm(1, NMEM)
            pe.wait_ge(s["norm_out"], 8)
            for n in range(4):
                job(n, xn3)
            pe.wait_ge(s["norm_rt"], 2)
            for n in range(3):
                rope(n)
            pe.wait_ge(s["rope_sin"], 3)
            out_of(1, pe)
            for t in range(5):
                w = P if t < 4 else NS
                mm = pe.transpose(ps[0:w, 7, 4 * t:4 * t + 4], iwT[0:4, P * t:P * t + w], ident[0:4, 0:4])
            mm.then_inc(s["iw_tok"], 1)
            pe.wait_ge(s["zi_set"], 5)
            for t in range(1, 4):
                for h in range(4):
                    if t >= 2:
                        pe.wait_ge(s["relu"], 4 * (t - 2) + h + 1)
                    hp = slice(64 * (h % 2), 64 * (h % 2) + 64)
                    pe.matmul(ps[:, 4 + h, 0:P * (t + 1)], iq[hp, h // 2, P * t:P * (t + 1)], ik[hp, 0:P * (t + 1)],
                              start=True, stop=True).then_inc(s["iscore"], 1)
            for n in range(4, FILL0):
                job(n, xn3)
            pe.wait_ge(s["zi_set"], 4)
            for q in range(2):
                pe.wait_ge(s[f"ki_in{q}"], 128 * 4)
            pe.wait_ge(s["relu"], 12)
            for b in range(DB):
                for h in range(2):
                    pe.matmul(ps[:, 4 + h, :], zi[0:64, P * b:P * (b + 1)], ki[b][:, 512 * h:512 * (h + 1)],
                              start=(b == 0), stop=(b == DB - 1))
                pe.matmul(ps[:, 6, 0:NS], zi[0:64, P * b:P * (b + 1)], ik[0:64, SEQ:TOK],
                          start=(b == 0), stop=(b == DB - 1)).then_inc(s["ki_used"], 1)
            pe.wait_ge(s["rs"], 1)
            for h in range(3):
                w = 512 if h < 2 else NS
                mm = pe.matmul(ps[0:NS, 4 + h, 0:w], k_("sel"), rs[:, 512 * h:512 * h + w], start=True, stop=True)
            mm.then_inc(s["ssum"], 1)
            pe.wait_ge(s["ss_out"], 1)
            for n in range(3, 8):
                rope(n)
            pe.wait_ge(s["rope_sin"], 8)
            out_of(job_at("av"), pe)
            for t in range(5):
                w = P if t < 4 else NS
                mm = pe.transpose(ps[0:w, 6 + t // 4, P * (t % 4):P * (t % 4 + 1)], av[:, P * t:P * t + w], ident)
            mm.then_inc(s["v_tok"], 1)

            def unit(u):
                t, h = u // 8, u % 8
                return t, h // 2, slice(64 * (h % 2), 64 * (h % 2) + 64), h % 2

            def p_score(u):
                t, ht, hp, half = unit(u)
                if u >= 2:
                    pe.wait_ge(s["p_exp"], u - 1)
                pe.matmul(ps[:, 4 + u % 2, 0:P * (t + 1)], aq3[hp, ht, P * t:P * (t + 1)], ak[hp, 0:P * (t + 1)],
                          start=True, stop=False)
                pe.matmul(ps[:, 4 + u % 2, 0:P * (t + 1)], identb[:, :], biasp[:, t, 0:P * (t + 1)],
                          start=False, stop=True).then_inc(s["p_score"], 1)

            def p_turn(u):
                t, ht, hp, half = unit(u)
                pe.wait_ge(s["p_prob"], u + 1)
                if u >= 2:
                    pe.wait_ge(s["p_pT_out"], u - 1)
                for k in range(t + 1):
                    mm = pe.transpose(ps[:, 6 + u % 2, P * k:P * (k + 1)], pp[:, u % 2, P * k:P * (k + 1)], ident)
                mm.then_inc(s["p_pT"], 1)

            def p_out(u):
                t, ht, hp, half = unit(u)
                pe.wait_ge(s["p_pT_out"], u + 1)
                if u % 8 == 0 and t >= 2:
                    pe.wait_ge(s["oA_out"], t - 1)
                for k in range(t + 1):
                    mm = pe.matmul(ps[hp, t % 2, P * ht:P * (ht + 1)], vt[:, k, hp], ppt[:, u % 2, k],
                                   start=(k == 0), stop=(k == t))
                mm.then_inc(s["pav_done"], 1)

            pe.wait_ge(s["rope_out"], 8)
            pe.wait_ge(s["bias_done"], 4)
            pe.wait_ge(s["v_tok_out"], 2)
            pe.wait_ge(s["bf_const"], 2)
            for u in range(NU + 2):
                if u < NU:
                    p_score(u)
                if 1 <= u <= NU:
                    p_turn(u - 1)
                if u >= 2:
                    p_out(u - 2)
                fill("p", u)
            fill("need", "cq", 3)
            fill("need", "pb", 13)
            fill_close("p", 0)

            pe.wait_ge(s["za_set"], 4)
            pe.wait_ge(s["p_exp"], NU)
            pe.wait_ge(s["p_pT_out"], NU)
            pe.wait_ge(s["selected"], 1)
            for hb in range(2):
                if hb:
                    pe.wait_ge(s["s_exp"], 1)
                for b4 in range(4):
                    b = 4 * hb + b4
                    kv = kvb[b % 5]
                    pe.wait_ge(s[f"kv_in{b % 5}"], 128 * (b // 5 + 1))
                    w = za[:, 640 * hb + P * b4:640 * hb + P * (b4 + 1)]
                    for h in range(2):
                        pe.matmul(ps[:, 4 + h, :], w, kv[:, 4 * h:4 * h + 4, 0:P], start=(b4 == 0), stop=False)
                    pe.matmul(ps[:, 6, 0:NS], w, ak[:, SEQ:TOK], start=(b4 == 0), stop=False)
                for h in range(3):
                    w = 512 if h < 2 else NS
                    mm = pe.matmul(ps[:, 4 + h, 0:w], repb[0:NS, P * hb:P * (hb + 1)], biass[0:NS, 512 * h:512 * h + w],
                                   start=False, stop=True)
                mm.then_inc(s["s_score"], 1)
                pe.wait_ge(s["s_prob"], hb + 1)
                if hb == 0:
                    pe.wait_ge(s["oA_out"], 4)
                for t in range(9):
                    w = P if t < 8 else NS
                    mm = pe.transpose(ps[0:w, t // 4, P * (t % 4):P * (t % 4 + 1)], pr[:, P * t:P * t + w], ident)
                mm.then_inc(s["s_pT"], 1)
                pe.wait_ge(s["s_pT_out"], 3 * (hb + 1))
                if hb:
                    pe.wait_ge(s["oA_out"], 6)
                for b4 in range(4):
                    kv = kvb[(4 * hb + b4) % 5]
                    for t in range(8):
                        pe.matmul(ps[:, 3, 32 * b4:32 * b4 + 32], kv[:, t, P:2 * P], pt[:, t, 32 * b4:32 * b4 + 32],
                                  start=(t == 0), stop=False)
                    pe.matmul(ps[:, 3, 32 * b4:32 * b4 + 32], vt[0:NS, 4], pt[0:NS, 8, 32 * b4:32 * b4 + 32],
                              start=False, stop=True).then_inc(s["vs_used"], 1)

            pe.wait_ge(s["s_exp"], 2)
            pe.wait_ge(s["oA_out"], 8)
            for t in range(4):
                if t >= 1:
                    pe.wait_ge(s["x_exp"], 4 * t)
                for h in range(4):
                    mm = pe.matmul(ps[:, 4 + h // 2, NMEM * (h % 2):NMEM * (h % 2 + 1)], cq3[:, h, P * t:P * (t + 1)],
                                   mkT[:, h], start=True, stop=True)
                mm.then_inc(s["x_score"], 1)
                fill("x", t, 0)
                pe.wait_ge(s["x_prob"], t + 1)
                if t >= 1:
                    pe.wait_ge(s["x_pT_out"], 2 * t)
                for h in range(4):
                    for m in range(2):
                        mm = pe.transpose(ps[:, 6 + h // 2, P * (2 * (h % 2) + m):P * (2 * (h % 2) + m + 1)],
                                          xp[:, t % 2, h, P * m:P * (m + 1)], ident)
                mm.then_inc(s["x_pT"], 1)
                fill("x", t, 1)
                pe.wait_ge(s["x_pT_out"], 2 * (t + 1))
                if t >= 2:
                    pe.wait_ge(s["oC_out"], t - 1)
                for h in range(4):
                    for m in range(2):
                        mm = pe.matmul(ps[:, t % 2, P * h:P * (h + 1)], mv[:, m, P * h:P * (h + 1)],
                                       xpt[:, t % 2, 2 * h + m], start=(m == 0), stop=(m == 1))
                mm.then_inc(s["xav_done"], 1)
                fill("x", t, 2)

            pe.wait_ge(s["zc_set"], 1)
            pe.wait_ge(s["x_exp"], 16)
            for b in range(DB):
                pe.wait_ge(s[f"mks_in{b % 2}"], 16 * (b // 2 + 1))
                for h in range(4):
                    n = 4 * b + h
                    mm = pe.matmul(ps[:, 4, 0:NMEM], zc[:, P * n:P * (n + 1)], mks[:, b % 2, NMEM * h:NMEM * (h + 1)],
                                   start=(n == 0), stop=(n == 31))
                mm.then_inc(s["mks_used"], 1)
            fill("c", 0)
            pe.wait_ge(s["x_prob"], 5)
            for m in range(2):
                mm = pe.transpose(ps[:, 5, P * m:P * (m + 1)], cp[:, P * m:P * (m + 1)], ident)
            mm.then_inc(s["x_pT"], 1)
            fill("c", 1)
            pe.wait_ge(s["x_pT_out"], 9)
            pe.wait_ge(s["oC_out"], 4)
            for b in range(DB):
                pe.wait_ge(s[f"mvs_in{b % 2}"], 16 * (b // 2 + 1))
                for h in range(4):
                    n = 4 * b + h
                    for m in range(2):
                        mm = pe.matmul(ps[:, 0, 4 * n:4 * n + 4], mvs[:, b % 2, 512 * m + P * h:512 * m + P * (h + 1)],
                                       cpt[:, m, 4 * n:4 * n + 4], start=(m == 0), stop=(m == 1))
                mm.then_inc(s["mvs_used"], 1)
            fill("c", 2)

            def wide(b, w, src):
                for h in range(2):
                    mm = pe.matmul(ps[:, b + h, 0:HALF], w, src[:, h * HALF:(h + 1) * HALF], start=True, stop=True)
                return mm

            pe.wait_ge(s["oC_out"], 5)
            pe.wait_ge(s["lora_in"], 16)
            for j in range(4):
                fill("need", "pb", 8 + j)
                if j == 0:
                    pe.wait_ge(s["t12"], 2)
                cols = slice(P * j, P * (j + 1))
                if j:
                    pe.wait_ge(s["oB_out"], j)
                wide(0, lora[0:64, cols], t12[0:64]).then_inc(s["lora_up"], 1)
                wide(4, lora[64:128, cols], t12[64:128]).then_inc(s["lora_up"], 1)
                fill("prep", j, 0)
                pe.wait_ge(s["kk_sq"], j + 1)
                pe.wait_ge(s["tanhs"], 2 * j + 1)
                wide(0, k_("blk"), tA).then_inc(s["kk_ss"], 1)
                fill("prep", j, 1)
                pe.wait_ge(s["rk"], j + 1)
                pe.wait_ge(s["tanhs"], 2 * j + 2)
                wide(6, k_("blk"), L_).then_inc(s["rk_sum"], 1)
                fill("prep", j, 2)
                pe.wait_ge(s["factors"], j + 1)
                pe.wait_ge(s["bonus"], j + 1)
                fill_close("tm", j)
                for n, src in enumerate((v__, bt, kt_)):
                    for c in range(4):
                        pe.transpose(ps[:, n, P * c:P * (c + 1)], src[:, P * c:P * (c + 1)], ident)
                    mm = pe.transpose(ps[0:NS, 3, P * n:P * (n + 1)], src[:, SEQ:TOK], ident)
                mm.then_inc(s["tm"], 1)
                for hh in range(2):
                    g = 2 * j + hh
                    hp = slice(64 * hh, 64 * hh + 64)
                    for c in range(4):
                        t = slice(C * c, C * (c + 1))
                        if hh:
                            pe.wait_ge(s["state"], 4 * g)
                            pe.wait_ge(s["y_chunk"], 4 * g)
                        pe.matmul(ps[:, 4 + c, 0:256], bt[hp, t], AR[hp, :, t], start=True, stop=True)
                        pe.matmul(ps[:, 4 + c, 256:512], kt_[hp, t], AR[hp, :, t], start=True,
                                  stop=True).then_inc(s["pairs"], 1)
                    if hh == 0:
                        pe.wait_ge(s["tm_out"], 4 * (j + 1))
                    if hh:
                        fill_close("group", 2 * j)
                    for c in range(4):
                        t = slice(C * c, C * (c + 1))
                        pe.matmul(ps[:, c, 0:P], AR[hp, 0, t], bt[hp, t], start=True, stop=True).then_inc(s["low"], 1)
                    for r in range(4):
                        for c in range(4):
                            if r == 0:
                                pe.wait_ge(s["dx_set"], 4 * g + c + 1)
                                pe.matmul(ps[:, 4 + c, 0:P], dx[:, c, 2], dx[:, c, 0], start=True, stop=True)
                                mm = pe.matmul(ps[:, 4 + c, 256:256 + P], dx[:, c, 0], dx[:, c, 2], start=True, stop=True)
                            else:
                                pe.wait_ge(s["dsq"], 12 * g + 4 * (r - 1) + c + 1)
                                if r > 1:
                                    pe.wait_ge(s["xup"], 12 * g + 4 * (r - 2) + c + 1)
                                if r < 3:
                                    pe.matmul(ps[:, 4 + c, 0:P], dx[:, c, 2], dx[:, c, 0], start=True, stop=True)
                                    pe.matmul(ps[:, 4 + c, 256:256 + P], dx[:, c, 0], dx[:, c, 2], start=True, stop=True)
                                pe.matmul(ps[:, c, 0:P], dx[:, c, 2], dx[:, c, 1], start=True, stop=True)
                                mm = pe.matmul(ps[:, c, P:256], dx[:, c, 0], dx[:, c, 3], start=True, stop=True)
                            mm.then_inc(s["round"], 1)
                    for l in range(3):
                        for c in range(4):
                            if l == 0:
                                pe.wait_ge(s["xup"], 12 * g + 8 + c + 1)
                            else:
                                pe.wait_ge(s["xlev"], 12 * g + 4 * (l - 1) + c + 1)
                            pe.matmul(ps[:, 4 + c, 0:P], lev[:, c, l + 1], dx[:, c, 1], start=True,
                                      stop=True).then_inc(s["mx"], 1)
                        for c in range(4):
                            pe.wait_ge(s["mx_out"], 12 * g + 4 * l + c + 1)
                            if l < 2:
                                pe.matmul(ps[:, c, 0:P], dx[:, c, 3], tt[:, c], start=True, stop=True)
                            pe.matmul(ps[:, c, P:256], tt[:, c], dx[:, c, 3], start=True,
                                      stop=True).then_inc(s["xmx"], 1)
                    pe.wait_ge(s["mx_out"], 12 * g + 12)
                    for c in range(4):
                        t = slice(C * c, C * (c + 1))
                        n = 4 * g + c
                        mm = pe.matmul(ps[:, 4, 0:64], m4[:, c, 2], tm[:, 0, c, hp], start=True, stop=(c == 0))
                        if c:
                            pe.wait_ge(s["state"], n)
                            mm = pe.matmul(ps[:, 4, 0:64], AR[hp, 0, t], T0[hp], start=False, stop=True)
                        mm.then_inc(s["z"], 1)
                        if c == 0:
                            pe.wait_ge(s["xlev"], 12 * g + 12)
                        fill("chunk", n, 0)
                        pe.wait_ge(s["z_out"], n + 1)
                        pe.wait_ge(s["xlev"], 12 * g + 8 + c + 1)
                        pe.matmul(ps[:, 5, 0:64], dx[:, c, 3], zs, start=True, stop=True).then_inc(s["u"], 1)
                        fill("chunk", n, 1)
                        pe.wait_ge(s["u_out"], n + 1)
                        pe.matmul(ps[hp, 7, 0:64], tm[:, 1, c, hp], us, start=True, stop=False)
                        pe.matmul(ps[hp, 7, 0:64], tm[:, 2, c, hp], tm[:, 0, c, hp], start=False,
                                  stop=True).then_inc(s["dstate"], 1)
                        if c:
                            pe.wait_ge(s["y_chunk"], n)
                        pe.matmul(ps[hp, 6, 0:P], tm[:, 0, c, hp], m4[:, c, 3], start=True, stop=False)
                        if c:
                            pe.matmul(ps[hp, 6, 0:P], T0[hp], AR[hp, 1, t], start=False, stop=False)
                        pe.matmul(ps[hp, 6, 0:P], us, m4[:, c, 1], start=False, stop=True).then_inc(s["ychunk"], 1)
                        fill("chunk", n, 2)
                pe.wait_ge(s["state"], 8 * (j + 1))
                pe.wait_ge(s["y_chunk"], 8 * (j + 1))
                pe.wait_ge(s["t0s_in"], 16 * (j + 1))
                pe.wait_ge(s["zaa"], 2 * (j + 1))
                for hh in range(2):
                    n = 2 * j + hh
                    hp = slice(64 * hh, 64 * hh + 64)
                    st = slice(SEQ, TOK)
                    pe.matmul(ps[0:NS, 4, 0:64], bt[hp, st], AR[hp, :, st], start=True, stop=True)
                    pe.matmul(ps[0:NS, 4, 64:128], kt_[hp, st], AR[hp, :, st], start=True, stop=True)
                    pe.matmul(ps[0:NS, 5, 0:NS], AR[hp, 0, st], bt[hp, st], start=True, stop=True).then_inc(s["s_pairs"], 1)
                    fill("dec", n, 0)
                    pe.wait_ge(s["s_m4"], 3 * n + 3)
                    pe.matmul(ps[0:NS, 6, 0:NS], sm4[0:NS, 0], sdl, start=True, stop=True).then_inc(s["s_inv"], 1)
                    fill("dec", n, 1)
                    pe.wait_ge(s["s_inv_out"], 2 * n + 1)
                    pe.matmul(ps[0:NS, 7, 0:NS], sd2, sx1, start=True, stop=True).then_inc(s["s_inv"], 1)
                    pe.matmul(ps[0:NS, 0, 0:64], sm4[0:NS, 2], tms[0:NS, 0, hp], start=True, stop=False)
                    for b in range(DB):
                        mm = pe.matmul(ps[0:NS, 0, 0:64], zaa[hp, NS * b:NS * (b + 1)], t0s[hp, b], start=False,
                                       stop=(b == DB - 1))
                    mm.then_inc(s["s_z"], 1)
                    fill("dec", n, 2)
                    pe.wait_ge(s["s_z_out"], n + 1)
                    pe.wait_ge(s["s_inv_out"], 2 * n + 2)
                    pe.matmul(ps[0:NS, 1, 0:64], sxt, zs[0:NS], start=True, stop=True).then_inc(s["s_u"], 1)
                    fill("dec", n, 3)
                    pe.wait_ge(s["s_u_out"], n + 1)
                    pe.matmul(ps[hp, 5, 0:NS], tms[0:NS, 0, hp], sm4[0:NS, 3], start=True, stop=False)
                    for b in range(DB):
                        pe.matmul(ps[hp, 5, 4 * b:4 * b + 4], t0s[hp, b], AR[hp, 1, SEQ + 4 * b:SEQ + 4 * b + 4],
                                  start=False, stop=False)
                    pe.matmul(ps[hp, 5, 0:NS], us[0:NS], sm4[0:NS, 1], start=False, stop=True).then_inc(s["s_y"], 1)
                    pe.wait_ge(s["s_blk"], 2 * (n + 1))
                    pe.matmul(ps[hp, 4, :], tms[0:NS, 1, hp], ub[0:NS], start=True, stop=False)
                    pe.matmul(ps[hp, 4, :], tms[0:NS, 2, hp], vb[0:NS], start=False, stop=True).then_inc(s["s_dstate"], 1)
                    fill("dec", n, 4)
                    pe.wait_ge(s["sstate"], n + 1)
                    pe.wait_ge(s["s_y_out"], n + 1)
                pe.wait_ge(s["s_y_out"], 2 * (j + 1))
                wide(0, k_("blk"), y_).then_inc(s["mean"], 1)
                fill("gn", j, 0)
                pe.wait_ge(s["yc_sq"], j + 1)
                wide(4, k_("blk"), tA).then_inc(s["var"], 1)
                fill("gn", j, 1)
                pe.wait_ge(s["yc"], j + 1)
                wide(0, lora[:, 512 + P * j:512 + P * (j + 1)], t13).then_inc(s["g"], 1)
                fill("gn", j, 2)
            fill("need", "gate", 23)

            def split_job(n, src, wait=None):
                kts = SLABS[JOBS[n][2]][2]
                pe.wait_ge(s["weights_lo"], n - SPLIT0 + 1)
                bank_free(n, pe)
                _, whi, wlo = split_views(n)
                b = bank_of(n)
                hi, lo = src
                for k in range(kts):
                    if wait:
                        wait(k)
                    a, z = k == 0, k == kts - 1
                    for h in range(2):
                        c = slice(h * HALF, (h + 1) * HALF)
                        pe.matmul(ps[:, b + h, 0:HALF], whi[:, k], hi[k][:, c], start=a, stop=False)
                        pe.matmul(ps[:, b + h, 0:HALF], whi[:, k], lo[k][:, c], start=False, stop=False)
                    for h in range(2):
                        c = slice(h * HALF, (h + 1) * HALF)
                        mm = pe.matmul(ps[:, b + h, 0:HALF], wlo[:, k], hi[k][:, c], start=False, stop=z)
                mm.then_inc(s["gemm_done"], 1)

            def norm_sum(n, k):
                pe.wait_ge(s["norm_sq"], KT * n + k + 1)
                for h in range(2):
                    mm = pe.matmul(ps[:, 4 + h, 0:HALF], k_("ones"), nbuf[n][0][:, k % 2, h * HALF:(h + 1) * HALF],
                                   start=(k == 0), stop=(k == KT - 1))
                mm.then_inc(s["norm_ss"], 1)

            for n in range(SPLIT0, job_at("out", 0)):
                kind, idx, *_ = JOBS[n]
                br = merge_at(idx)[1]
                if idx < 6 and idx % 2 == 0:
                    pe.wait_ge(s["part_lo"], 4 * (br + 1))
                split_job(n, HEADS[br])
            pe.wait_ge(s["part_lo"], PART["merge"] + 8)
            for n in range(job_at("out", 0), job_at("up", 0)):
                j = JOBS[n][1]
                split_job(n, M)
                if j >= 2:
                    norm_sum(2, j - 2)
            norm_sum(2, 6)
            norm_sum(2, 7)
            for n in range(job_at("up", 0), NJOB):
                kind, idx, *_ = JOBS[n]
                if kind == "up":
                    split_job(n, X, (lambda k: pe.wait_ge(s["part_lo"], PART["x"] + k + 1)) if idx == 0 else None)
                else:
                    r = idx // 8
                    if idx % 8 == 0:
                        pe.wait_ge(s["part_lo"], PART["hid"] + 8 * (r + 1))
                    if idx == 24:
                        pe.wait_ge(s["norm_rt"], 3)
                    split_job(n, H[r % 2])
                    if idx >= 26:
                        norm_sum(3, idx - 26)
            norm_sum(3, 6)
            norm_sum(3, 7)

        @block.scalar
        def _(act):
            step = Steps(act, s["act_step"])

            def square(n, src, N, k):
                if KT * n + k >= 2:
                    act.wait_ge(s["norm_ss"], KT * n + k - 1)
                if n >= 2:
                    out_of(job_at("out", k) if n == 2 else job_at("down", 24 + k), act)
                act.activation(nbuf[n][0][:, k % 2, 0:N], src[:, k], ACT.Square).then_inc(s["norm_sq"], 1)

            def norm(n, src, N, first=0):
                for k in range(first, KT):
                    square(n, src, N, k)
                act.wait_ge(s["norm_ss"], KT * (n + 1))
                if n:
                    act.wait_ge(s["norm_rc"], n)
                if N > 512:
                    act.activation(h2(nbuf[n][1][:, 0:N]), pair(4), ACT.Sqrt, bias=epsc, scale=1.0 / D).then_inc(s["norm_rt"], 1)
                else:
                    act.activation(nbuf[n][1][:, 0:N], ps[:, 4, 0:N], ACT.Sqrt, bias=epsc, scale=1.0 / D).then_inc(s["norm_rt"], 1)

            def evac(n):
                kind, idx, sl, c0_, w, e = JOBS[n]
                act.wait_ge(s["gemm_done"], n + 1)
                b = bank_of(n)
                src = ps[0:min(w, P), b:b + 2, 0:HALF]
                fn = ACT.Copy
                if kind == "pb":
                    act.wait_ge(s["pb_edge"], 2 if idx >= 12 else 4)
                    dst = pb3[:, idx]
                    act.activation(dst[:, 1:HALF + 1], ps[:, b, 0:HALF], fn)
                    act.activation(dst[:, HALF + 1:SEQ + 1], ps[:, b + 1, 0:SEQ - HALF], fn)
                    last = act.activation(dst[:, SEQ + 1:PBW].rearrange("p (b c) -> p b c", c=5)[:, :, 1:5],
                                          ps[:, b + 1, SEQ - HALF:HALF].rearrange("p (b c) -> p b c", c=4), fn)
                elif kind == "mk":
                    last = act.activation(mkT[:, idx], ps[:, b, 0:NMEM], fn)
                elif kind == "mv":
                    last = act.activation(mv[:, idx % 2, 256 * (idx // 2):256 * (idx // 2 + 1)], ps[:, b, 0:w], fn)
                elif kind == "gate":
                    if idx >= 2:
                        act.wait_ge(s[f"gate_stored{idx % 2}"], 16 * (idx // 2))
                    dj, br = merge_at(idx)
                    last = act.activation(h2(gst[:, idx % 2]), src, ACT.Tanh, bias=hgate[:, 8 * br + dj:8 * br + dj + 1], scale=0.5)
                elif kind == "up":
                    if idx >= 2:
                        act.wait_ge(s["hid_sq"], idx - 1)
                        act.wait_ge(s["part_hi"], PART["hid"] + idx - 1)
                    last = act.activation(h2(ub2[:, idx % 2]), src, ACT.Relu)
                else:
                    dst = {"ik": lambda: ik, "iw": lambda: iwT[0:4], "iq": lambda: iq[:, idx], "aq": lambda: aq3[:, idx],
                           "ak": lambda: ak, "av": lambda: av, "cq": lambda: cq3[:, idx]}[kind]()
                    last = act.activation(h2(dst), src, fn)
                last.then_inc(s["evac_a"], 1)

            def evacs(*tag):
                for n in FILLED[tag]:
                    evac(n)

            act.wait_ge(s["inputs_in"], 48)
            act.wait_ge(s["pool_step"], 2)
            norm(0, xT3, TOK)
            act.wait_ge(s["aux_in"], 48)
            norm(1, memT, NMEM)
            act.wait_ge(s["norm_out"], 16)
            for n in range(4):
                evac(n)
            for t in range(1, 4):
                for h in range(4):
                    act.wait_ge(s["iscore"], 4 * (t - 1) + h + 1)
                    if t >= 2:
                        act.wait_ge(s["isum"], 4 * (t - 2) + h + 1)
                    act.activation(rl[:, h, 0:P * (t + 1)], ps[:, 4 + h, 0:P * (t + 1)], ACT.Relu).then_inc(s["relu"], 1)
            for n in range(4, FILL0):
                evac(n)
            act.wait_ge(s["v_tok"], 1)
            act.activation(vt[:, 0:4], cut(ps[:, 6], 0, 4, P), ACT.Copy).then_inc(s["v_tok_out"], 1)
            act.activation(vt[0:NS, 4], ps[0:NS, 7, 0:P], ACT.Copy).then_inc(s["v_tok_out"], 1)
            for u in range(NU + 2):
                if u < NU:
                    t = u // 8
                    act.wait_ge(s["p_max"], u + 1)
                    if u >= 2:
                        act.wait_ge(s["p_pT"], u - 1)
                    act.activation(pp[:, u % 2, 0:P * (t + 1)], ps[:, 4 + u % 2, 0:P * (t + 1)], ACT.Exp,
                                   bias=nm[:, u % 4:u % 4 + 1], scale=0.125,
                                   accum_out=sm[:, u % 4:u % 4 + 1]).then_inc(s["p_exp"], 1)
                if 1 <= u <= NU:
                    w = u - 1
                    t = w // 8
                    act.wait_ge(s["p_pT"], w + 1)
                    if w >= 2:
                        act.wait_ge(s["pav_done"], w - 1)
                    act.activation(ppt[:, w % 2, 0:t + 1], cut(ps[:, 6 + w % 2], 0, t + 1, P),
                                   ACT.Copy).then_inc(s["p_pT_out"], 1)
                if u >= 2 and (u - 2) % 8 == 7:
                    t = (u - 2) // 8
                    act.wait_ge(s["pav_done"], u - 1)
                    act.activation(aq3[:, :, P * t:P * (t + 1)], cut(ps[:, t % 2], 0, 4, P), ACT.Copy).then_inc(s["oA_out"], 1)
                evacs("p", u)
            evacs("need", "cq", 3)
            evacs("need", "pb", 13)
            evacs("close", "p", 0)
            flat = ps[:, 4:7].rearrange("p a b -> p (a b)")[:, 0:KEYS]
            for hb in range(2):
                act.wait_ge(s["s_max"], hb + 1)
                if hb:
                    act.wait_ge(s["s_pT"], hb)
                act.activation(pr, flat, ACT.Exp, bias=nm[:, 0:1], scale=0.125, accum_out=sm[:, 0:1]).then_inc(s["s_exp"], 1)
                act.wait_ge(s["s_pT"], hb + 1)
                if hb:
                    act.wait_ge(s["vs_used"], 4)
                act.activation(pt[:, 0:4], cut(ps[:, 0], 0, 4, P), ACT.Copy).then_inc(s["s_pT_out"], 1)
                act.activation(pt[:, 4:8], cut(ps[:, 1], 0, 4, P), ACT.Copy).then_inc(s["s_pT_out"], 1)
                act.activation(pt[0:NS, 8], ps[0:NS, 2, 0:P], ACT.Copy).then_inc(s["s_pT_out"], 1)
                act.wait_ge(s["vs_used"], 4 * (hb + 1))
                for g in range(2):
                    gp = slice(64 * g, 64 * g + 64)
                    dst = aq3[gp, :, SEQ + 16 * hb:SEQ + 16 * hb + 16].rearrange("p t (b q) -> p b t q", b=4)
                    src = ps[gp, 3, 0:128].rearrange("p (b g t q) -> p b g t q", b=4, g=2, t=4)[:, :, g]
                    act.activation(dst, src, ACT.Copy).then_inc(s["oA_out"], 1)
            for t in range(4):
                act.wait_ge(s["x_max"], t + 1)
                for h in range(4):
                    act.activation(xp[:, t % 2, h], ps[:, 4 + h // 2, NMEM * (h % 2):NMEM * (h % 2 + 1)], ACT.Exp,
                                   bias=nm[:, h:h + 1], scale=scale_c, accum_out=sm[:, h:h + 1]).then_inc(s["x_exp"], 1)
                evacs("x", t, 0)
                act.wait_ge(s["x_pT"], t + 1)
                for n in range(2):
                    act.activation(xpt[:, t % 2, 4 * n:4 * n + 4], cut(ps[:, 6 + n], 0, 4, P), ACT.Copy).then_inc(s["x_pT_out"], 1)
                evacs("x", t, 1)
                act.wait_ge(s["xav_done"], t + 1)
                act.activation(cq3[:, :, P * t:P * (t + 1)], cut(ps[:, t % 2], 0, 4, P), ACT.Copy).then_inc(s["oC_out"], 1)
                evacs("x", t, 2)
            act.wait_ge(s["x_max"], 5)
            act.activation(cp, ps[:, 4, 0:NMEM], ACT.Exp, bias=nm[:, 0:1], scale=scale_c,
                           accum_out=sm[:, 0:1]).then_inc(s["x_exp"], 1)
            evacs("c", 0)
            act.wait_ge(s["x_pT"], 5)
            act.activation(cpt, cut(ps[:, 5], 0, 2, P), ACT.Copy).then_inc(s["x_pT_out"], 1)
            evacs("c", 1)
            act.wait_ge(s["mvs_used"], 8)
            act.activation(cq3[:, :, SEQ:TOK].rearrange("p h (b q) -> p b h q", b=DB),
                           ps[:, 0, 0:P].rearrange("p (b h q) -> p b h q", b=DB, h=4), ACT.Copy).then_inc(s["oC_out"], 1)
            evacs("c", 2)
            evacs("need", "pb", 8)
            act.wait_ge(s["mix"], 2)
            act.activation(t12[0:64], tA[0:64], ACT.Tanh)
            act.activation(t12[64:128], tA[64:128], ACT.Copy).then_inc(s["t12"], 1)
            act.activation(t13, tB, ACT.Sigmoid).then_inc(s["t12"], 1)
            for j in range(4):
                if j:
                    evacs("need", "pb", 8 + j)
                act.wait_ge(s["half_bias"], 3)
                act.wait_ge(s["lora_up"], 2 * j + 1)
                act.activation(h2(lw), pair(0), ACT.Tanh, bias=hw0[:, j:j + 1], scale=0.5).then_inc(s["tanhs"], 1)
                act.wait_ge(s["lora_up"], 2 * j + 2)
                act.activation(h2(a_), pair(4), ACT.Tanh, bias=ha0[:, j:j + 1], scale=0.5).then_inc(s["tanhs"], 1)
                act.wait_ge(s["kk"], 2 * j + 1)
                act.wait_ge(s["t12"], 2)
                act.activation(tA, kk, ACT.Square).then_inc(s["kk_sq"], 1)
                evacs("prep", j, 0)
                act.wait_ge(s["kk_ss"], j + 1)
                act.activation(h2(tA), pair(0), ACT.Sqrt).then_inc(s["kk_rt"], 1)
                act.wait_ge(s["lx"], j + 1)
                act.activation(tA, L_, ACT.Exp).then_inc(s["exps"], 1)
                act.activation(tB, L_, ACT.Exp, scale=-1.0).then_inc(s["exps"], 1)
                act.activation(lw, a_, ACT.Exp).then_inc(s["exps"], 1)
                act.activation(scf, scf, ACT.Exp).then_inc(s["exps"], 1)
                evacs("prep", j, 1)
                evacs("prep", j, 2)
                evacs("close", "tm", j)
                act.wait_ge(s["tm"], j + 1)
                for n in range(3):
                    act.activation(tm[:, n], cut(ps[:, n], 0, 4, P), ACT.Copy).then_inc(s["tm_out"], 1)
                act.activation(tms[0:NS], cut(ps[0:NS, 3], 0, 3, P), ACT.Copy).then_inc(s["tm_out"], 1)
                for hh in range(2):
                    g = 2 * j + hh
                    hp = slice(64 * hh, 64 * hh + 64)
                    if hh:
                        evacs("close", "group", 2 * j)
                    for r in range(3):
                        for c in range(4):
                            act.wait_ge(s["round"], 16 * g + 4 * r + c + 1)
                            act.activation(dx[:, c, 0::2], cut(ps[:, 4 + c], 0, 4, P)[:, 0::2], ACT.Copy).then_inc(s["dsq"], 1)
                    for l in range(3):
                        for c in range(4):
                            act.wait_ge(s["mx"], 12 * g + 4 * l + c + 1)
                            act.activation(tt[:, c], ps[:, 4 + c, 0:P], ACT.Copy).then_inc(s["mx_out"], 1)
                    for c in range(4):
                        n = 4 * g + c
                        act.wait_ge(s["z"], n + 1)
                        act.activation(zs, ps[:, 4, 0:64], ACT.Copy).then_inc(s["z_out"], 1)
                        evacs("chunk", n, 0)
                        act.wait_ge(s["u"], n + 1)
                        act.activation(us, ps[:, 5, 0:64], ACT.Copy).then_inc(s["u_out"], 1)
                        evacs("chunk", n, 1)
                        act.wait_ge(s["ychunk"], n + 1)
                        act.activation(y_[hp, C * c:C * (c + 1)], ps[hp, 6, 0:P], ACT.Copy).then_inc(s["y_chunk"], 1)
                        evacs("chunk", n, 2)
                for hh in range(2):
                    n = 2 * j + hh
                    hp = slice(64 * hh, 64 * hh + 64)
                    evacs("dec", n, 0)
                    evacs("dec", n, 1)
                    act.wait_ge(s["s_z"], n + 1)
                    act.activation(zs[0:NS], ps[0:NS, 0, 0:64], ACT.Copy).then_inc(s["s_z_out"], 1)
                    evacs("dec", n, 2)
                    act.wait_ge(s["s_u"], n + 1)
                    act.activation(us[0:NS], ps[0:NS, 1, 0:64], ACT.Copy).then_inc(s["s_u_out"], 1)
                    evacs("dec", n, 3)
                    act.wait_ge(s["s_y"], n + 1)
                    act.activation(y_[hp, SEQ:TOK], ps[hp, 5, 0:NS], ACT.Copy).then_inc(s["s_y_out"], 1)
                    evacs("dec", n, 4)
                act.wait_ge(s["yc"], j + 1)
                act.activation(tA, y_, ACT.Square).then_inc(s["yc_sq"], 1)
                evacs("gn", j, 0)
                act.wait_ge(s["var"], j + 1)
                act.activation(h2(tA), pair(4), ACT.Sqrt, bias=gneps, scale=1.0 / 64).then_inc(s["y_rt"], 1)
                evacs("gn", j, 1)
                evacs("gn", j, 2)
            evacs("need", "gate", 23)
            act.wait_ge(s["gemm_done"], SPLIT0)
            act.wait_ge(s["oB_out"], 4)
            weights_hi(act, SPLIT0)
            for n, (src, hi, _) in enumerate(SOURCES):
                if n == 0:
                    act.wait_ge(s["t0s_out"], 16 * 4)
                if n == 4:
                    weights_hi(act, SPLIT0 + 1)
                act.activation(hi, src, ACT.Copy).then_inc(s["part_hi"], 1)
            for n in range(SPLIT0, job_at("out", 0)):
                kind, idx, *_ = JOBS[n]
                act.wait_ge(s["gemm_done"], n + 1)
                weights_hi(act, n + 2)
                if merge_at(idx)[1] == 2:
                    dj = merge_at(idx)[0]
                    act.wait_ge(s["merged"], merges(idx))
                    act.activation(M[0][dj], acc[:, dj % 2], ACT.Copy).then_inc(s["part_hi"], 1)
            for n in range(job_at("out", 0), job_at("up", 0)):
                j = JOBS[n][1]
                weights_hi(act, n + 2)
                if j >= 1:
                    square(2, xT3, TOK, j - 1)
            norm(2, xT3, TOK, KT - 1)
            for k in range(KT):
                act.wait_ge(s["norm_out"], 16 + k + 1)
                act.activation(X[0][k], nx[:, k % 2], ACT.Copy).then_inc(s["part_hi"], 1)
            for n in range(job_at("up", 0), NJOB):
                kind, idx, *_ = JOBS[n]
                if kind == "up":
                    if idx == 0:
                        act.wait_ge(s["part_lo"], PART["x"] + KT)
                    evac(n)
                    weights_hi(act, n + 2)
                    act.wait_ge(s["evac_a"], evacuated(n, "a"))
                    act.activation(H[idx // 8 % 2][0][idx % 8], ub2[:, idx % 2], ACT.Square).then_inc(s["part_hi"], 1)
                else:
                    weights_hi(act, n + 2)
                    if idx >= 25:
                        square(3, xT3, TOK, idx - 25)
            norm(3, xT3, TOK, KT - 1)

        @block.vector
        def _(dve):
            step = Steps(dve, s["dve_step"])

            def norm(n, src, dst, N, g):
                dve.wait_ge(s["norm_rt"], n + 1)
                if n:
                    dve.wait_ge(s["norm_out"], 8 * n)
                rt, rc = nbuf[n][1:]
                dve.reciprocal(rc[:, 0:N], rt[:, 0:N]).then_inc(s["norm_rc"], 1)
                dve.wait_ge(s["norm_rc"], n + 1)
                for k in range(KT):
                    to = dst[:, k % 2] if n == 2 else dst[:, k]
                    if n == 2 and k >= 2:
                        dve.wait_ge(s["part_lo"], PART["x"] + k - 1)
                    dve.scalar_tensor_tensor(to, src[:, k], v_(g, k), rc[:, 0:N], ALU.mult,
                                             ALU.mult).then_inc(s["norm_out"], 1)
                    if n == 2 and k:
                        x_rest(k - 1)

            def x_rest(k):
                dve.wait_ge(s["part_hi"], PART["x"] + k + 1)
                dve.tensor_tensor(X[1][k], nx[:, k % 2], X[0][k].bitcast(F32), ALU.subtract).then_inc(s["part_lo"], 1)

            def rope(n):
                kind, idx, raw = ROPE[n]
                dve.wait_ge(s["rope_rot"], n + 1)
                if n:
                    dve.wait_ge(s["rope_out"], n)
                dve.tensor_tensor(h2(rope1), pair(4 + 2 * (n % 2)), h2(k_("sin")), ALU.mult).then_inc(s["rope_sin"], 1)
                dve.wait_ge(s["rope_sin"], n + 1)
                dve.wait_ge(s["rope_cos"], n + 1)
                dve.tensor_tensor(raw, rope1, rope2[:, n % 2], ALU.add).then_inc(s["rope_out"], 1)

            dve.wait_ge(s["inputs_in"], 48)
            dve.tensor_copy(identb[:, :], ident).then_inc(s["bf_const"], 1)
            dve.tensor_copy(repb[0:NS, :], k_("rep")[0:NS]).then_inc(s["bf_const"], 1)
            dve.tensor_scalar(hw0, vec[:, VOFF["rwkv_w0"][0]:VOFF["rwkv_w0"][0] + 4], 0.5, None, ALU.mult).then_inc(s["half_bias"], 1)
            dve.tensor_scalar(ha0, vec[:, VOFF["rwkv_a0"][0]:VOFF["rwkv_a0"][0] + 4], 0.5, None, ALU.mult).then_inc(s["half_bias"], 1)
            dve.tensor_scalar(hgate, vec[:, VOFF["b_gate"][0]:VOFF["b_gate"][0] + 24], 0.5, None, ALU.mult).then_inc(s["half_bias"], 1)
            norm(0, xT3, xn3, TOK, "norm_mix_g")
            norm(1, memT, memn, NMEM, "norm_mem_g")
            for n in range(3):
                rope(n)
            dve.wait_ge(s["pool_step"], 3)
            dve.wait_ge(s["rope_out"], 3)
            for h in range(4):
                hp = slice(64 * (h % 2), 64 * (h % 2) + 64)
                dst = zi[0:64, 32 * h:32 * h + DB * 132].rearrange("p (b c) -> p b c", c=132)[:, :, 0:4] if h < 4 else None
                dve.tensor_copy(dst, iq[hp, h // 2, SEQ:TOK].rearrange("p (b q) -> p b q", q=4)).then_inc(s["zi_set"], 1)
            dve.wait_ge(s["iw_tok"], 1)
            step(dve.tensor_scalar(iwc[:, 0:16], ps[:, 7, 0:16], 0.0625, None, ALU.mult))
            step(dve.tensor_scalar(iwc[0:NS, 16:20], ps[0:NS, 7, 16:20], 0.0625, None, ALU.mult))
            for h in range(4):
                ins = dve.tensor_copy(iws[32 * h:32 * h + 32], iwc[0:NS, 16 + h:17 + h])
                if h < 3:
                    step(ins)
                else:
                    ins.then_inc(s["zi_set"], 1)
            dve.wait_ge(s["zi_set"], 5)
            flat = ps[:, 4:7].rearrange("p a b -> p (a b)")[:, 0:KEYS]
            dve.tensor_copy(biasp[:, 0, 0:P], k_("caus")).then_inc(s["bias_done"], 1)

            def take_eight(sc, m8):
                step(dve.max(m8, sc))
                step(dve.match_replace(sc, m8, sc, GONE))

            m8 = small[:, 132:140]
            for t in range(1, 4):
                n = P * (t + 1)
                sc = scp[:, 0:n]
                for h in range(4):
                    dve.wait_ge(s["relu"], 4 * (t - 1) + h + 1)
                    if h == 0:
                        ins = dve.tensor_scalar(sc, rl[:, 0, 0:n], iwc[:, 4 * t:4 * t + 1], None, ALU.mult)
                    else:
                        dve.wait_ge(s["isum"], 4 * (t - 1) + h)
                        ins = dve.scalar_tensor_tensor(sc, rl[:, h, 0:n], iwc[:, 4 * t + h:4 * t + h + 1], sc, ALU.mult, ALU.add)
                    ins.then_inc(s["isum"], 1)
                dve.wait_ge(s["isum"], 4 * t)
                step(dve.tensor_tensor(sc[:, P * t:n], sc[:, P * t:n], k_("caus"), ALU.add))
                for _ in range(TOPK_P // 8):
                    take_eight(sc, m8)
                dve.tensor_scalar(biasp[:, t, 0:n], sc, -2e38, NEG, ALU.is_gt, ALU.mult).then_inc(s["bias_done"], 1)
                dve.wait_ge(s["bias_done"], t + 1)
            dve.wait_ge(s["ki_used"], 8)
            dve.tensor_scalar(rs, flat, 0.0, iws, ALU.max, ALU.mult).then_inc(s["rs"], 1)
            dve.wait_ge(s["ssum"], 1)
            step(dve.tensor_copy(ss[:, 0:PAST], flat[0:NS, 0:PAST]))
            dve.tensor_tensor(ss[:, PAST:KEYS], flat[0:NS, PAST:KEYS], k_("snew")[0:NS], ALU.add).then_inc(s["ss_out"], 1)
            dve.wait_ge(s["ss_out"], 1)
            for n in range(3, 8):
                rope(n)
            dve.wait_ge(s["pool_step"], 4)
            dve.wait_ge(s["rope_out"], 8)
            for hb in range(2):
                for g in range(2):
                    gp = slice(64 * g, 64 * g + 64)
                    dst = za[gp, 640 * hb:640 * hb + 640].rearrange("p (b c) -> p b c", c=160)[:, :, 16 * g:16 * g + 16]
                    dst = dst.rearrange("p b (t q) -> p b t q", q=4)
                    src = aq3[gp, :, SEQ + 16 * hb:SEQ + 16 * hb + 16].rearrange("p t (b q) -> p b t q", b=4)
                    dve.tensor_copy(dst, src).then_inc(s["za_set"], 1)
            for u in range(NU + 1):
                if u < NU:
                    t, q = u // 8, u % 4
                    dve.wait_ge(s["p_score"], u + 1)
                    if u >= 4:
                        dve.wait_ge(s["p_exp"], u - 3)
                    step(dve.tensor_reduce(mx[:, q:q + 1], ps[:, 4 + u % 2, 0:P * (t + 1)], AX.X, ALU.max))
                    dve.tensor_scalar(nm[:, q:q + 1], mx[:, q:q + 1], -0.125, None, ALU.mult).then_inc(s["p_max"], 1)
                if u >= 1:
                    w = u - 1
                    t, q = w // 8, w % 4
                    dve.wait_ge(s["p_exp"], w + 1)
                    step(dve.reciprocal(ri[:, q:q + 1], sm[:, q:q + 1]))
                    dve.tensor_scalar(pp[:, w % 2, 0:P * (t + 1)], pp[:, w % 2, 0:P * (t + 1)], ri[:, q:q + 1], None,
                                      ALU.mult).then_inc(s["p_prob"], 1)
                for _ in range(TOPK_S // 8 * u // NU, TOPK_S // 8 * (u + 1) // NU if u < NU else TOPK_S // 8):
                    take_eight(ss, m8[0:NS])
            dve.wait_ge(s["p_prob"], NU)
            dve.tensor_scalar(biass[0:NS], ss, -2e38, NEG, ALU.is_gt, ALU.mult).then_inc(s["selected"], 1)
            for hb in range(2):
                dve.wait_ge(s["s_score"], hb + 1)
                step(dve.tensor_reduce(mx[:, 0:1], flat, AX.X, ALU.max))
                if hb:
                    dve.wait_ge(s["s_exp"], hb)
                dve.tensor_scalar(nm[:, 0:1], mx[:, 0:1], -0.125, None, ALU.mult).then_inc(s["s_max"], 1)
                dve.wait_ge(s["s_exp"], hb + 1)
                step(dve.reciprocal(ri[:, 0:1], sm[:, 0:1]))
                dve.tensor_scalar(pr, pr, ri[:, 0:1], None, ALU.mult).then_inc(s["s_prob"], 1)
            for t in range(4):
                dve.wait_ge(s["x_score"], t + 1)
                step(dve.tensor_reduce(mx, ps[:, 4:6].rearrange("p a (h m) -> p (a h) m", h=2), AX.X, ALU.max))
                dve.tensor_scalar(nm, mx, -scale_c, None, ALU.mult).then_inc(s["x_max"], 1)
                dve.wait_ge(s["x_exp"], 4 * (t + 1))
                step(dve.reciprocal(ri, sm))
                dve.tensor_tensor(xp[:, t % 2], xp[:, t % 2], ri.unsqueeze(2).to_broadcast([P, 4, NMEM]),
                                  ALU.mult).then_inc(s["x_prob"], 1)
            dve.wait_ge(s["pool_step"], 5)
            dve.tensor_copy(zc.rearrange("p (b h c) -> p b h c", b=DB, h=4)[:, :, :, 0:4],
                            cq3[:, :, SEQ:TOK].rearrange("p h (b q) -> p b h q", b=DB)).then_inc(s["zc_set"], 1)
            dve.wait_ge(s["mks_used"], 8)
            dve.wait_ge(s["x_prob"], 4)
            step(dve.tensor_reduce(mx[:, 0:1], ps[:, 4, 0:NMEM], AX.X, ALU.max))
            dve.tensor_scalar(nm[:, 0:1], mx[:, 0:1], -scale_c, None, ALU.mult).then_inc(s["x_max"], 1)
            dve.wait_ge(s["x_exp"], 17)
            step(dve.reciprocal(ri[:, 0:1], sm[:, 0:1]))
            dve.tensor_scalar(cp, cp, ri[:, 0:1], None, ALU.mult).then_inc(s["x_prob"], 1)

            def mix(dst, tile, n):
                cur = pb3[:, tile]
                dve.wait_ge(s["diff"], n + 1)
                mu = v_("rwkv_mu", tile)
                dve.scalar_tensor_tensor(dst[:, 0:SEQ], dst[:, 0:SEQ], mu, cur[:, 1:SEQ + 1], ALU.mult, ALU.add)
                d4 = dst[:, SEQ:TOK].rearrange("p (b c) -> p b c", c=4)
                c5 = cur[:, SEQ + 1:PBW].rearrange("p (b c) -> p b c", c=5)
                dve.scalar_tensor_tensor(d4, d4, mu, c5[:, :, 1:5], ALU.mult, ALU.add).then_inc(s["mix"], 1)

            mix(tA, 12, 0)
            mix(tB, 13, 1)
            CL = -0.5 * float(np.exp(-0.5))
            for j in range(4):
                for n, (dst, tile) in enumerate(((r_, j), (k__, 4 + j), (v__, 8 + j))):
                    mix(dst, tile, 2 + 3 * j + n)
                dve.wait_ge(s["mix"], 2 + 3 * (j + 1))
                dve.tensor_scalar(kk, k__, v_("rwkv_k_k", j), None, ALU.mult).then_inc(s["kk"], 1)
                dve.wait_ge(s["tanhs"], 2 * j + 1)
                step(dve.tensor_scalar(lw, lw, CL, CL, ALU.mult, ALU.add))
                dve.wait_ge(s["tanhs"], 2 * j + 2)
                step(dve.tensor_scalar(a_, a_, 0.5, 0.5, ALU.mult, ALU.add))
                step(dve.tensor_tensor_scan(L_, k_("reset"), lw, 0.0, ALU.mult, ALU.add))
                dve.wait_ge(s["kk_rt"], j + 1)
                step(dve.tensor_scalar(tA, tA, 1e-12, None, ALU.max))
                step(dve.reciprocal(tB, tA))
                dve.tensor_tensor(kk, kk, tB, ALU.mult).then_inc(s["kk"], 1)
                dve.wait_ge(s["kk"], 2 * j + 2)
                dve.tensor_tensor(bt, kk, a_, ALU.mult)
                step(dve.tensor_scalar(tB, a_, 1.0, v_("rwkv_k_a", j), ALU.subtract, ALU.mult))
                step(dve.scalar_tensor_tensor(kh, tB, 1.0, k__, ALU.add, ALU.mult))
                step(dve.tensor_copy(c0, L_[:, C // 2 - 1:SEQ:C]))
                l3 = L_[:, 0:SEQ].rearrange("p (c t) -> p c t", c=4)
                step(dve.tensor_tensor(l3, l3, c0.unsqueeze(2).to_broadcast([P, 4, C]), ALU.subtract))
                step(dve.tensor_copy(scf, L_[:, C - 1:SEQ:C]))
                step(dve.tensor_tensor(scf[:, 0:3], scf[:, 0:3], c0[:, 1:4], ALU.add))
                dve.tensor_tensor(a_, L_, lw, ALU.subtract).then_inc(s["lx"], 1)
                dve.wait_ge(s["exps"], 4 * (j + 1))
                dve.scalar_tensor_tensor(L_, r_, v_("rwkv_r_k", j), kh, ALU.mult, ALU.mult).then_inc(s["rk"], 1)
                dve.tensor_copy(sdec, tA[:, SEQ + 3:TOK:4])
                dve.tensor_tensor(AR[:, 1], r_, tA, ALU.mult)
                dve.scalar_tensor_tensor(AR[:, 0], kk, -1.0, lw, ALU.mult, ALU.mult)
                dve.tensor_tensor(bt, bt, tB, ALU.mult)
                dve.tensor_tensor(kt_, kh, tB, ALU.mult).then_inc(s["factors"], 1)
                dve.wait_ge(s["rk_sum"], j + 1)
                dve.tensor_tensor(h2(L_), pair(6), h2(v__), ALU.mult).then_inc(s["bonus"], 1)
                for hh in range(2):
                    g = 2 * j + hh
                    hp = slice(64 * hh, 64 * hh + 64)
                    for c in range(4):
                        dve.wait_ge(s["pairs"], 4 * g + c + 1)
                        if c == 0 and hh == 0 and j:
                            dve.wait_ge(s["t0s_out"], 16 * j)
                        dve.tensor_tensor(m4[:, c], cut(ps[:, 4 + c], 0, 4, P), cut(cst, COFF["mask4"][0], 4, P),
                                          ALU.mult).then_inc(s["m4"], 1)
                    for c in range(4):
                        dve.wait_ge(s["low"], 4 * g + c + 1)
                        dve.tensor_tensor(dx[:, c, 0], ps[:, c, 0:P], k_("mlow"), ALU.mult).then_inc(s["dlow"], 1)
                    for r in range(1, 4):
                        for c in range(4):
                            dve.wait_ge(s["round"], 16 * g + 4 * r + c + 1)
                            dve.tensor_tensor(dx[:, c, 1::2], dx[:, c, 1::2], cut(ps[:, c], 0, 2, P),
                                              ALU.add).then_inc(s["xup"], 1)
                    for l in range(3):
                        for c in range(4):
                            dve.wait_ge(s["xmx"], 12 * g + 4 * l + c + 1)
                            if l < 2:
                                ins = dve.tensor_tensor(dx[:, c, 1::2], dx[:, c, 1::2], cut(ps[:, c], 0, 2, P), ALU.add)
                            else:
                                ins = dve.tensor_tensor(dx[:, c, 3], dx[:, c, 3], ps[:, c, P:256], ALU.add)
                            ins.then_inc(s["xlev"], 1)
                    for c in range(4):
                        n = 4 * g + c
                        dve.wait_ge(s["dstate"], n + 1)
                        if c:
                            dve.wait_ge(s["ychunk"], n)
                            dve.wait_ge(s["ychunk"], n + 1)
                            step(dve.tensor_tensor(T0[hp], T0[hp], ps[hp, 7, 0:64], ALU.add))
                            ins = dve.tensor_scalar(T0[hp], T0[hp], scf[hp, c:c + 1], None, ALU.mult)
                        else:
                            if j:
                                dve.wait_ge(s["T0_out"], 16 * j)
                            ins = dve.tensor_scalar(T0[hp], ps[hp, 7, 0:64], scf[hp, 0:1], None, ALU.mult)
                        ins.then_inc(s["state"], 1)
                for hh in range(2):
                    n = 2 * j + hh
                    hp = slice(64 * hh, 64 * hh + 64)
                    dve.wait_ge(s["s_pairs"], n + 1)
                    dve.tensor_tensor(sm4[0:NS], cut(ps[0:NS, 4], 0, 4, NS), cut(cst, COFF["smask4"][0], 4, NS)[0:NS],
                                      ALU.mult).then_inc(s["s_m4"], 1)
                    dve.tensor_tensor(sdl, ps[0:NS, 5, 0:NS], k_("slow")[0:NS], ALU.mult).then_inc(s["s_m4"], 1)
                    dve.wait_ge(s["s_m4"], 3 * n + 2)
                    dve.tensor_tensor(sx1, sm4[0:NS, 0], ident[0:NS, 0:NS], ALU.add).then_inc(s["s_m4"], 1)
                    dve.wait_ge(s["s_inv"], 2 * n + 1)
                    dve.tensor_copy(sd2, ps[0:NS, 6, 0:NS]).then_inc(s["s_inv_out"], 1)
                    dve.wait_ge(s["s_inv"], 2 * n + 2)
                    dve.tensor_tensor(sxt, sx1, ps[0:NS, 7, 0:NS], ALU.add).then_inc(s["s_inv_out"], 1)
                    bl = k_("sblk")[0:NS].unsqueeze(2).to_broadcast([NS, DB, 64])
                    dve.tensor_tensor(vb[0:NS], tms[0:NS, 0:1, hp].to_broadcast([NS, DB, 64]), bl, ALU.mult).then_inc(s["s_blk"], 1)
                    dve.wait_ge(s["s_u_out"], n + 1)
                    dve.tensor_tensor(ub[0:NS], us[0:NS].unsqueeze(1).to_broadcast([NS, DB, 64]), bl, ALU.mult).then_inc(s["s_blk"], 1)
                    dve.wait_ge(s["s_dstate"], n + 1)
                    step(dve.tensor_tensor(t0s[hp], t0s[hp], cut(ps[hp, 4], 0, DB, 64), ALU.add))
                    dve.tensor_tensor(t0s[hp], t0s[hp], sdec[hp].unsqueeze(2).to_broadcast([64, DB, 64]), ALU.mult).then_inc(s["sstate"], 1)
                dve.wait_ge(s["mean"], j + 1)
                dve.scalar_tensor_tensor(h2(y_), pair(0), -1.0 / 64, h2(y_), ALU.mult, ALU.add).then_inc(s["yc"], 1)
                dve.wait_ge(s["y_rt"], j + 1)
                step(dve.reciprocal(tB, tA))
                step(dve.tensor_tensor(y_, y_, tB, ALU.mult))
                step(dve.tensor_scalar(y_, y_, v_("rwkv_ln_g", j), v_("rwkv_ln_b", j), ALU.mult, ALU.add))
                step(dve.tensor_tensor(y_, y_, L_, ALU.add))
                dve.wait_ge(s["g"], j + 1)
                dve.tensor_tensor(h2(pb3[:, j, 0:TOK]), pair(0), h2(y_), ALU.mult).then_inc(s["oB_out"], 1)

            weights_lo(dve, SPLIT0)
            for n, (src, hi, lo) in enumerate(SOURCES):
                if n == 4:
                    weights_lo(dve, SPLIT0 + 1)
                dve.wait_ge(s["part_hi"], n + 1)
                dve.tensor_tensor(lo, src, hi.bitcast(F32), ALU.subtract).then_inc(s["part_lo"], 1)
            for n in range(SPLIT0, job_at("out", 0)):
                kind, idx, _, _, _, e = JOBS[n]
                if e == "v":
                    b = bank_of(n)
                    dve.wait_ge(s["gemm_done"], n + 1)
                    dve.wait_ge(s[f"gate_in{idx % 3}"], 16 * (idx // 3 + 1))
                    dj, br = merge_at(idx)
                    to = acc[:, dj % 2]
                    if br == 0 and dj >= 2:
                        dve.wait_ge(s["part_lo"], PART["merge"] + dj - 1)
                    dve.scalar_tensor_tensor(h2(mt if br else to), h2(gb[:, idx % 3]), 1.0, pair(b), ALU.add, ALU.mult).then_inc(s["evac_v"], 1)
                    if br:
                        dve.wait_ge(s["evac_v"], evacuated(n, "v"))
                        dve.tensor_tensor(to, to, mt, ALU.add).then_inc(s["merged"], 1)
                        dve.wait_ge(s["merged"], merges(idx))
                weights_lo(dve, n + 2)
                if e == "v" and br == 2:
                    dve.wait_ge(s["part_hi"], PART["merge"] + dj + 1)
                    dve.tensor_tensor(M[1][dj], to, M[0][dj].bitcast(F32), ALU.subtract).then_inc(s["part_lo"], 1)
            for n in range(job_at("out", 0), job_at("up", 0)):
                weights_lo(dve, n + 2)
                dve.wait_ge(s["gemm_done"], n + 1)
                x = h2(xT3[:, JOBS[n][1]])
                dve.scalar_tensor_tensor(x, pair(bank_of(n)), 0.5, x, ALU.mult, ALU.add).then_inc(s["evac_v"], 1)
            norm(2, xT3, nx, TOK, "norm_mlp_g")
            x_rest(KT - 1)
            for n in range(job_at("up", 0), NJOB):
                kind, idx, *_ = JOBS[n]
                if kind == "up":
                    out_of(n, dve)
                    if idx >= 2:
                        dve.wait_ge(s["part_lo"], PART["hid"] + idx - 1)
                    dve.tensor_tensor(hsq[:, idx % 2], ub2[:, idx % 2], ub2[:, idx % 2], ALU.mult).then_inc(s["hid_sq"], 1)
                    weights_lo(dve, n + 2)
                    dve.wait_ge(s["part_hi"], PART["hid"] + idx + 1)
                    dve.wait_ge(s["hid_sq"], idx + 1)
                    hi, lo = (h[idx % 8] for h in H[idx // 8 % 2])
                    dve.tensor_tensor(lo, hsq[:, idx % 2], hi.bitcast(F32), ALU.subtract).then_inc(s["part_lo"], 1)
                else:
                    weights_lo(dve, n + 2)
                    dve.wait_ge(s["gemm_done"], n + 1)
                    x = xT3[:, idx % 8]
                    if idx >= 8:
                        out_of(job_at("down", idx - 8), dve)
                    dve.tensor_tensor(h2(x), pair(bank_of(n)), h2(x), ALU.add).then_inc(s["evac_v"], 1)
            out_of(NJOB - 1, dve)
            norm(3, xT3, cut(yo, 0, KT, TOK), TOK, "norm_final_g")


_OUTS = {"yT": (P, KT, TOK), "kT": (P, TOK), "vT": (P, TOK), "ikT": (64, TOK), "mkT": (P, 4, NMEM), "mv": (P, 2, 512),
         "wkvP": (4, P, 64), "wkvS": (4, P, DB, 64), "shT": (P, PBT * 9)}


def kernel(**a):
    import concourse.bacc as bacc
    from concourse.bass_utils import run_bass_kernel_spmd

    a = {k: np.asarray(v) for k, v in a.items()}
    n_phys = a["cache_k"].shape[0]

    def feat(x):
        return np.ascontiguousarray(x.T.reshape(-1, P, x.shape[0]).transpose(1, 0, 2))

    order = np.concatenate([np.arange(64) + 64 * (t + o) for t in range(4) for o in (0, 4)])
    w = {k: a[k] for k in ("w_in", "w_mem_kv", "w_branch_b", "w_branch_c", "w_out", "w_mlp_up", "w_mlp_down")}
    w["w_branch_a"] = a["w_branch_a"][order]
    slabs = np.zeros((NSLAB, P, SLABW), np.float32)
    for n, (name, r0, kts, cols) in enumerate(SLABS):
        m = np.concatenate([w[name][r0:r0 + kts * P, c:c + k] for c, k in cols], 1)
        slabs[n, :, 0:kts * m.shape[1]] = m.reshape(kts, P, -1).transpose(1, 0, 2).reshape(P, -1)
    ins = {
        "xT": feat(np.concatenate([a["x_prompt"].reshape(SEQ, D), a["x_sample"].reshape(NS, D)])),
        "memT": feat(a["mem_prompt"].reshape(NMEM, D)),
        "const": constants(),
        "vec": np.concatenate([a[k].reshape(-1, P).T for k, _ in VECS], 1),
        "slabs": slabs,
        "lora": np.concatenate([np.concatenate([a["rwkv_w_up"], a["rwkv_a_up"]], 0), a["rwkv_g_up"]], 1),
        "shT": feat(a["state_shift"]).reshape(P, -1),
        "pages": a["page_table"].reshape(1, -1),
        "ki": a["cache_idx_k"].transpose(0, 2, 1),
        "kv": np.concatenate([a["cache_k"].reshape(n_phys, PAGE, P).transpose(0, 2, 1),
                              a["cache_v"].reshape(n_phys, PAGE, P)], 2),
        "mks": a["cache_mem_k"].transpose(0, 3, 2, 1).reshape(DB, P, 4 * NMEM),
        "mvs": a["cache_mem_v"].reshape(DB, 2, P, 512).transpose(0, 2, 1, 3).reshape(DB, P, 1024),
        "wkvT": a["state_wkv"].transpose(1, 3, 0, 2).reshape(4, P, DB, 64),
    }
    nc = bacc.Bacc("TRN2", target_bir_lowering=False, num_devices=1)
    arrays, i, o = {}, {}, {}
    for k, x in ins.items():
        x = np.ascontiguousarray(x)
        arrays["in_" + k] = x
        i[k] = nc.dram_tensor("in_" + k, x.shape, mybir.dt.from_np(x.dtype), kind="ExternalInput").ap()
    for k, shape in _OUTS.items():
        o[k] = nc.dram_tensor("out_" + k, shape, F32, kind="ExternalOutput").ap()
    i["gates"] = nc.dram_tensor("gates", (24, P, TOK), F32, kind="Internal").ap()
    build(nc, i, o)
    r = run_bass_kernel_spmd(nc, [arrays], core_ids=[0]).results[0]
    g = {k: r["out_" + k] for k in _OUTS}
    y = g["yT"].transpose(2, 1, 0).reshape(TOK, D)
    k, v, ik = g["kT"].T, g["vT"].T, g["ikT"].T
    sh = g["shT"].reshape(P, PBT, 9).transpose(2, 1, 0).reshape(9, PB)
    mkT = g["mkT"].reshape(P, 4, NMEM).transpose(2, 1, 0)
    mv = g["mv"].transpose(1, 0, 2).reshape(NMEM, 4, P)
    wp = g["wkvP"].reshape(8, 64, 64).transpose(0, 2, 1)
    ws = g["wkvS"].reshape(8, 64, DB, 64).transpose(2, 0, 3, 1)
    out = (y[:SEQ].reshape(1, SEQ, D), y[SEQ:].reshape(DB, DS, D), k[:SEQ].reshape(1, SEQ, 2, 64), v[:SEQ].reshape(1, SEQ, 2, 64),
           ik[:SEQ].reshape(1, SEQ, 64), mkT[None], mv[None], wp[None], sh[0:1], k[SEQ:].reshape(DB, DS, 2, 64),
           v[SEQ:].reshape(DB, DS, 2, 64), ik[SEQ:].reshape(DB, DS, 64), ws, sh[1:])
    return tuple(np.ascontiguousarray(x) for x in out)
```

```python
from contextlib import ExitStack

import numpy as np
import concourse.bass as bass
from concourse import mybir

F32 = mybir.dt.float32
F32R = mybir.dt.float32r
BF16 = mybir.dt.bfloat16
I32 = mybir.dt.int32
U32 = mybir.dt.uint32
ALU = mybir.AluOpType
ACT = mybir.ActivationFunctionType
AX = mybir.AxisListType

P = 128
D = 1024
KT = D // P
SEQ, DB, DS = 512, 8, 4
NS = DB * DS
TOK = SEQ + NS
HALF = TOK // 2
PAST, PAGE, TOPK_P, TOPK_S = 1024, 128, 128, 256
KEYS = PAST + NS
NMEM = 256
PB = 1792
PBT = PB // P
PBW = SEQ + 1 + DB * (DS + 1)
C = 128
NCH = SEQ // C
FF = 4096
NEG, GONE = -1e30, -3e38
EPS, GN_EPS = 1e-6, 64e-5
SLABW = KT * 256
RING = 5

AQ, AK, AV, IQ, IK, PBC = 0, 512, 640, 768, 1024, 1092
CQ = PBC + PB
GATE = CQ + 512

CONSTS = [("ident", 128), ("rot", 128), ("blk", 128), ("ones", 128), ("cos", TOK), ("sin", TOK),
          ("mask4", 512), ("lev", 512), ("mlow", 128), ("reset", TOK), ("caus", 128),
          ("rep", 256), ("sel", 32), ("smask4", 128), ("slow", 32), ("snew", 32), ("sblk", 8)]
COFF, _n = {}, 0
for _k, _w in CONSTS:
    COFF[_k] = (_n, _w)
    _n += _w
NCONST = _n


def constants():
    c = {k: np.zeros((P, w), np.float32) for k, w in CONSTS}
    c["ident"][:] = np.eye(P)
    for base in (0, 64):
        for i in range(8):
            c["rot"][base + 8 + i, base + i] = -1.0
            c["rot"][base + i, base + 8 + i] = 1.0
    f = np.arange(P)
    c["blk"][:] = (f[:, None] // 64 == f[None, :] // 64)
    c["ones"][:] = 1.0
    pos = np.concatenate([np.arange(SEQ), np.tile(PAST + np.arange(DS), DB)]).astype(np.float32)
    inv = (np.float32(500000.0) ** (-np.arange(8, dtype=np.float32) / np.float32(8))).astype(np.float32)
    ang = (pos[None, :] * inv[:, None]).astype(np.float32)
    c["cos"][:] = 1.0
    for base in (0, 8, 64, 72):
        c["cos"][base:base + 8] = np.cos(ang)
        c["sin"][base:base + 8] = np.sin(ang)
    s, t = f[:, None], f[None, :]
    strict, incl = (s < t), (s <= t)
    c["mask4"][:] = np.concatenate([strict, incl, strict, incl], 1)
    lev = [strict & (s // 16 == t // 16)]
    for b in (16, 32, 64):
        lev.append((s // (2 * b) == t // (2 * b)) & (s // b < t // b))
    c["lev"][:] = np.concatenate(lev, 1)
    c["mlow"][:] = lev[0].T
    c["reset"][:] = 1.0
    c["reset"][:, 0:SEQ:C] = 0.0
    c["reset"][:, SEQ::DS] = 0.0
    c["caus"][:] = np.where(t > s, NEG, 0.0)
    r = np.arange(P)
    for hb in range(2):
        c["rep"][(hb * 4 + r // 32) * 4 + r % 4, hb * P + r] = 1.0
    c["sel"][r, r % 32] = 1.0
    a = np.arange(NS)
    sb_, tb = a[:, None], a[None, :]
    same = sb_ // 4 == tb // 4
    c["smask4"][0:NS] = np.concatenate([same & (sb_ < tb), same & (sb_ <= tb)] * 2, 1)
    c["slow"][0:NS] = same & (sb_ > tb)
    c["snew"][0:NS] = np.where(same & (tb <= sb_), 0.0, NEG)
    c["sblk"][0:NS] = sb_ // 4 == np.arange(8)[None, :]
    return np.concatenate([c[k] for k, _ in CONSTS], 1).astype(np.float32)


VECS = [("norm_mix_g", 8), ("norm_mem_g", 8), ("norm_mlp_g", 8), ("norm_final_g", 8), ("b_gate", 24),
        ("rwkv_mu", 14), ("rwkv_w0", 4), ("rwkv_a0", 4), ("rwkv_k_k", 4), ("rwkv_k_a", 4),
        ("rwkv_r_k", 4), ("rwkv_ln_g", 4), ("rwkv_ln_b", 4)]
VOFF, _n = {}, 0
for _k, _w in VECS:
    VOFF[_k] = (_n, _w)
    _n += _w
NVEC = _n


MLP_ORDER = [("up", 0), ("up", 1), ("down", 0), ("up", 2), ("down", 1), ("up", 3), ("down", 2), ("down", 3)]


PB_ORDER = [12, 13] + [t for j in range(4) for t in (j, 4 + j, 8 + j)]


def slab_plan():
    def head(base, h):
        return (base + 64 * h, 64)

    s = [("w_in", 0, KT, [(IK, 64), (IK, 64), (IK + 64, 4)]), ("w_in", 0, KT, [(IQ, 256)])]
    s += [("w_in", 0, KT, [head(AQ, t + o) for t in (2 * n, 2 * n + 1) for o in (0, 4)]) for n in range(2)]
    s += [("w_in", 0, KT, [(AK, 256)])]
    s += [("w_mem_kv", 0, KT, [(256 * i, 256)]) for i in range(4)]
    s += [("w_in", 0, KT, [(CQ + 256 * i, 256)]) for i in range(2)]
    s += [("w_in", 0, KT, [(PBC + P * a, P), (PBC + P * b, P)]) for a, b in zip(PB_ORDER[::2], PB_ORDER[1::2])]
    s += [("w_in", 0, KT, [(GATE + D * i + 256 * jj, 256)]) for jj in range(4) for i in range(3)]
    s += [(f"w_branch_{'abc'[i]}", 0, 4, [(256 * jj, 256)]) for jj in range(4) for i in range(3)]
    s += [("w_out", 0, KT, [(256 * jj, 256)]) for jj in range(4)]
    for kind, r in MLP_ORDER:
        if kind == "up":
            s += [("w_mlp_up", 0, KT, [(256 * (4 * r + jj), 256)]) for jj in range(4)]
        else:
            s += [("w_mlp_down", D * r, KT, [(256 * jj, 256)]) for jj in range(4)]
    return s


def job_plan():
    jobs = [("ik", 0, 0, 0, 128, "a"), ("iw", 0, 0, 128, 4, "a"), ("iq", 0, 1, 0, 128, "a"), ("iq", 1, 1, 128, 128, "a")]
    jobs += [("aq", i, 2 + i // 2, 128 * (i % 2), 128, "a") for i in range(4)]
    jobs += [("ak", 0, 4, 0, 128, "a"), ("av", 0, 4, 128, 128, "a")]
    jobs += [("mk", h, 5 + h // 2, 128 * (h % 2), 128, "a") for h in range(4)]
    jobs += [("mv", 2 * n + m, 7 + n, 0, 256, "a") for n in range(2) for m in range(2)]
    jobs += [("cq", i, 9 + i // 2, 128 * (i % 2), 128, "a") for i in range(4)]
    jobs += [("pb", t, 11 + n // 2, 128 * (n % 2), 128, "a") for n, t in enumerate(PB_ORDER)]
    s = 18
    jobs += [("gate", m, s + m // 2, 128 * (m % 2), 128, "a") for m in range(24)]
    s += 12
    jobs += [("branch", m, s + m // 2, 128 * (m % 2), 128, "v") for m in range(24)]
    s += 12
    jobs += [("out", j, s + j // 2, 128 * (j % 2), 128, "v") for j in range(8)]
    s += 4
    for kind, r in MLP_ORDER:
        jobs += [(kind, 8 * r + j, s + j // 2, 128 * (j % 2), 128, "a" if kind == "up" else "v") for j in range(8)]
        s += 4
    return jobs


SLABS = slab_plan()
NSLAB = len(SLABS)
JOBS = job_plan()
NJOB = len(JOBS)
SPLIT0 = next(n for n, j in enumerate(JOBS) if j[0] == "branch")
SPLIT_SLAB = JOBS[SPLIT0][2]
FILL0 = next(n for n, j in enumerate(JOBS) if j[0] == "mk")
LAND = 3
FREED = {}
for _n, _j in enumerate(JOBS):
    FREED[_j[2]] = _n + 1 - (SPLIT0 if _n >= SPLIT0 else 0)


PART = {"source": 0, "merge": 12, "x": KT + 12, "hid": 2 * KT + 12}


def merge_at(m):
    return 2 * (m // 6) + m % 2, m % 6 // 2


def merges(m):
    return sum(m_ % 6 >= 2 for m_ in range(m + 1))


def job_at(kind, i=0):
    return next(n for n, j in enumerate(JOBS) if j[0] == kind and j[1] == i)


def evacuated(n, eng):
    return sum(j[5] == eng for j in JOBS[:n + 1])


def bank_of(n):
    return 2 if FILL0 <= n < SPLIT0 else 2 * (n % 2)


def before_in_bank(n):
    return next((m for m in range(n - 1, -1, -1) if bank_of(m) == bank_of(n)), None)


def fill_plan():
    steps = [(n, k) for n in range(FILL0, SPLIT0) for k in range(KT)]
    waits = [(("p", u), 5) for u in range(35)] + [(("need", "cq", 3), 0), (("need", "pb", 13), 0), (("close", "p", 0), 0)]
    waits += [(("x", v), 4) for v in range(11)] + [(("need", "pb", 8), 0)] + [(("c", n), 6) for n in range(3)]
    for j in range(4):
        waits += [(("prep", j, n), b) for n, b in enumerate((8, 8, 8) if j else (8, 14, 8))]
        if j < 3:
            waits += [(("need", "pb", 9 + j), 0)]
        waits += [(("close", "tm", j), 0)]
        for g in (2 * j, 2 * j + 1):
            waits += [(("chunk", 4 * g + c, n), 2) for c in range(4) for n in range(3)]
            if g % 2 == 0:
                waits += [(("close", "group", g), 0)]
        waits += [(("dec", j, n), 4) for n in range(5)]
        waits += [(("gn", j, n), b) for n, b in enumerate((6, 6, 10))]
    waits += [(("need", "gate", 23), 0)]
    plan, done, at = {}, {}, 0
    for tag, budget in waits:
        plan[tag], done[tag] = [], []
        while at < len(steps):
            n, k = steps[at]
            cost = 1 if JOBS[n][0] in ("mk", "mv") else 2
            if tag[0] == "need":
                if n > job_at(tag[1], tag[2]):
                    break
            elif tag[0] == "close":
                if k == 0:
                    break
            elif budget < cost:
                break
            budget -= cost
            plan[tag].append((n, k))
            if k == KT - 1:
                done[tag].append(n)
            at += 1
    assert at == len(steps)
    return plan, done


FILLS, FILLED = fill_plan()


def slabs_before(*parts):
    return 1 + max(JOBS[n][2] for tag in FILLS if any(tag[:len(p)] == p for p in parts) for n, _ in FILLS[tag])


KV_SLAB = slabs_before(("p",), ("need", "cq", 3), ("need", "pb", 13), ("close", "p", 0)) + RING
MKS_SLAB = max(KV_SLAB, slabs_before(("x",), ("need", "pb", 8)))
MVS_SLAB = max(MKS_SLAB, slabs_before(("c", 0), ("c", 1)))


class Sems(dict):

    def __init__(self, make):
        super().__init__()
        self.make = make

    def __missing__(self, name):
        self[name] = self.make(name)
        return self[name]


class Steps:

    def __init__(self, eng, sem):
        self.eng, self.sem, self.n = eng, sem, 0

    def __call__(self, ins):
        self.n += 1
        ins.then_inc(self.sem, 1)
        self.eng.wait_ge(self.sem, self.n)


def build(nc, i, o):
    with ExitStack() as ctx:
        def sb(name, cols, dt=F32):
            return ctx.enter_context(nc.sbuf_tensor(name, [P, cols], dt))

        s = Sems(lambda name: ctx.enter_context(nc.semaphore(name)))
        cst = sb("cst", NCONST)
        vec = sb("vec", NVEC)
        xT = sb("xT", KT * TOK)
        identb = sb("identb", 128, BF16)
        repb = sb("repb", 256, BF16)
        small = sb("small", 192)
        pages = sb("pages", DB * 8, I32)
        sh_in = sb("sh_in", PBT * DB)
        sh_out = sb("sh_out", PBT * 9 + 2)

        def over(name, off, cols, dt=F32):
            with ExitStack() as put:
                if off:
                    put.enter_context(nc.sbuf_tensor("under_" + name, [P, off], F32))
                return put.enter_context(nc.sbuf_tensor(name, [P, cols], dt))

        XN, AQO, CQO, RINGO = 0, KT * TOK, 12 * TOK, 16 * TOK
        PBO = RINGO + RING * SLABW
        RO = PBO + -(-PBT * PBW // 8) * 8
        xn, aq, cq = over("xn", XN, KT * TOK), over("aq", AQO, 4 * TOK), over("cq", CQO, 4 * TOK)
        ring, pb, R = over("ring", RINGO, RING * SLABW), over("pb", PBO, PBT * PBW), over("R", RO, 32 * TOK)
        land = over("land", RINGO, LAND * SLABW)
        wh, wl = over("wh", RINGO + 6144, 2048, F32R), over("wl", RINGO + 8192, 2048, F32R)
        FREE = PBO + -(-4 * PBW // 8) * 8
        xlo, xhi = over("xlo", XN, KT * TOK, F32R), over("xhi", RO, KT * TOK, F32R)
        alo, clo = over("alo", AQO, 4 * TOK, F32R), over("clo", CQO, 4 * TOK, F32R)
        blo, bhi = over("blo", PBO, 4 * PBW, F32R), over("bhi", RO + 14 * TOK, 4 * TOK, F32R)
        achi = over("achi", FREE, 8 * TOK, F32R)
        mhi, mlo = over("mhi", RO + 20 * TOK, 8 * TOK, F32R), over("mlo", RO, 8 * TOK, F32R)
        merge = over("merge", RO + 8 * TOK, 6 * TOK)
        tail = over("tail", FREE + 4 * TOK, 4 * TOK)
        hh0, hl0 = over("hh0", RO + 8 * TOK, 8 * TOK, F32R), over("hl0", RO + 16 * TOK, 8 * TOK, F32R)
        hh1, hl1 = over("hh1", RO + 24 * TOK, 8 * TOK, F32R), over("hl1", AQO, 8 * TOK, F32R)
        mlpt = over("mlpt", FREE, 4 * TOK)
        yo = over("yo", RO, KT * TOK)
        ps = ctx.enter_context(nc.psum_tensor("ps", [P, 8, 512], F32))

        def cut(t, off, *dims):
            n = int(np.prod(dims))
            a = t[:, off:off + n]
            names = "abc"[:len(dims)]
            if len(dims) == 1:
                return a
            return a.rearrange("p (%s) -> p %s" % (" ".join(names), " ".join(names)), **dict(zip(names, dims)))

        def k_(name):
            off, w = COFF[name]
            return cst[:, off:off + w]

        def v_(name, j=0):
            off, _ = VOFF[name]
            return vec[:, off + j:off + j + 1]

        ident = k_("ident")
        lora = cst[:, COFF["cos"][0]:COFF["cos"][0] + 1024]
        xT3, xn3 = cut(xT, 0, KT, TOK), cut(xn, 0, KT, TOK)
        aq3, cq3 = cut(aq, 0, 4, TOK), cut(cq, 0, 4, TOK)
        pb3 = cut(pb, 0, PBT, PBW)
        memT, memn = cut(pb, 0, KT, NMEM), cut(pb, KT * NMEM, KT, NMEM)
        ik, iwT, iq = R[:, 0:TOK], R[:, TOK:2 * TOK], cut(R, 2 * TOK, 2, TOK)
        ak, av = R[:, 4 * TOK:5 * TOK], R[:, 5 * TOK:6 * TOK]
        r0 = 6 * TOK
        vt = cut(R, r0, 5, P)
        mkT = cut(R, r0 + 640, 4, NMEM)
        mv = cut(R, r0 + 1664, 2, 512)
        biasp = cut(R, r0 + 2688, 1024).bitcast(BF16).rearrange("p (a b) -> p a b", a=4)
        biass = cut(R, r0 + 3712, KEYS // 2).bitcast(BF16)
        B = r0 + 3712 + KEYS // 2
        ki = [R[0:64, B + PAST * n:B + PAST * (n + 1)] for n in range(2)]
        ki += [R[0:64, r0 + 640 + PAST * n:r0 + 640 + PAST * (n + 1)] for n in range(2)]
        ki += [cq[0:64, PAST * n:PAST * (n + 1)] for n in range(2)]
        ki += [pb[0:64, 4096 + PAST * n:4096 + PAST * (n + 1)] for n in range(2)]
        zi = R[:, B + 2048:B + 3200]
        rs = R[:, B + 3200:B + 4256]
        ss = R[0:NS, B + 4256:B + 5312]
        rl = cut(R, B + 5312, 4, 512)
        scp = rs[:, 0:512]
        NB = 28 * TOK
        assert B + 7360 <= NB
        sq = cut(R, NB, 2, TOK)
        rt, rc = R[:, NB + 2 * TOK:NB + 3 * TOK], R[:, NB + 3 * TOK:NB + 4 * TOK]
        rope1, rope2 = rt, sq
        kvb = [cut(xT, 2048 * n, 8, 2 * P) for n in range(2)]
        kvb += [cut(R, B + 5312, 8, 2 * P), cut(R, B + 7360, 8, 2 * P)]
        kvb += [cut(pb, 2048 * n, 8, 2 * P) for n in range(3)] + [cut(R, 0, 8, 2 * P)]
        za = R[:, B + 2560:B + 3840]
        pr = [R[:, B + 4256:B + 5312], R[:, B + 1152:B + 1152 + KEYS]]
        s_bank = (4, 0)
        pt = cut(R, B, 9, P)
        pp, ppt = cut(R, B, 3, 512), cut(R, B + 1536, 2, 4, P)
        zc = R[:, B + 4224:B + 4224 + 32 * 132]
        mks = cut(xT, 0, 4, 1024)
        mvb = [R[:, 3 * TOK:3 * TOK + 1024], R[:, B + 2560:B + 3584]]
        mvs = [mvb[0], mvb[1], mks[:, 0], mks[:, 1], mks[:, 2], mks[:, 3], mvb[0], mvb[1]]
        cp, cpt = R[:, B + 8448:B + 8448 + NMEM], cut(R, B + 8448 + NMEM, 2, P)
        xp = cut(R, B, 3, 2, NMEM)
        iwc, iws = small[:, 0:20], small[:, 20:21]
        mx, nm, sm, ri = small[:, 24:28], small[:, 28:32], small[:, 32:36], small[:, 36:40]
        epsc, gneps = small[:, 40:41], small[:, 41:42]
        hgate = small[:, 144:168]
        hw0, ha0 = small[:, 44:48], small[:, 48:52]
        c0, scf, sdec = small[:, 52:56], small[:, 56:60], small[:, 60:68]
        T0 = small[:, 68:132]
        slot = [R[:, TOK * n:TOK * (n + 1)] for n in range(14)]
        r_, k__, v__, lw, L_, a_, kk, kh = slot[:8]
        AR, bt, kt_, tA, tB = cut(R, 8 * TOK, 2, TOK), slot[10], slot[11], slot[12], slot[13]
        y_ = r_
        G = 14 * TOK
        m4 = cut(R, G, 4, 4, P)
        lev = cut(R, G + 2048, 4, 4, P)
        dx = cut(R, G + 4096, 4, 4, P)
        tt = cut(R, G + 6144, 4, P)
        tm = R[:, G + 6656:G + 6656 + 1536].rearrange("p (a b c) -> p a b c", a=3, b=4)
        zs, us = R[:, G + 8192:G + 8256], R[:, G + 8256:G + 8320]
        tms = cut(R, G + 8320, 3, P)
        assert G + 8704 <= 32 * TOK
        t0s = cut(R, G, DB, 64)
        zaa = R[:, G + 512:G + 800]
        dec = []
        for n in range(2):
            q = G + 1024 + 1408 * n
            dec.append(dict(ub=cut(R, q, DB, 64), vb=cut(R, q + 512, DB, 64), m4=cut(R, q + 1024, 4, NS),
                            low=R[0:NS, q + 1152:q + 1184], sq=R[0:NS, q + 1184:q + 1216],
                            x=R[0:NS, q + 1216:q + 1248], xt=R[0:NS, q + 1248:q + 1280],
                            z=R[0:NS, q + 1280:q + 1344], u=R[0:NS, q + 1344:q + 1408]))
        tail3, mlpt3, merge3 = cut(tail, 0, 4, TOK), cut(mlpt, 0, 4, TOK), cut(merge, 0, 6, TOK)
        gb, mt, acc = merge3[:, 0:3], merge3[:, 3], merge3[:, 4:6]
        ub2, hsq, nx = mlpt3[:, 0:2], mlpt3[:, 2:4], mlpt3[:, 0:2]
        nbuf = [(sq, rt, rc)] * 2 + [(tail3[:, 0:2], tail3[:, 2], tail3[:, 3])] * 2
        gst = cut(R, 30 * TOK, 2, TOK)
        squares = tail3[:, 3]
        t12, t13 = pb3[:, 12, 0:TOK], pb3[:, 13, 0:TOK]

        def tiles(t, n, pitch=TOK):
            return [t[:, pitch * k:pitch * k + TOK] for k in range(n)]

        X = (tiles(xhi, 8), tiles(xlo, 8))
        AC = tiles(achi, 8)
        HEADS = [(AC[0:4], tiles(alo, 4)), (tiles(bhi, 4), tiles(blo, 4, PBW)), (AC[4:8], tiles(clo, 4))]
        M = (tiles(mhi, 8), tiles(mlo, 8))
        H = [(tiles(hh0, 8), tiles(hl0, 8)), (tiles(hh1, 8), tiles(hl1, 8))]
        SOURCES = []
        for _src, _to in ((aq3, HEADS[0]), (cq3, HEADS[2]), (pb3[:, 0:4, 0:TOK], HEADS[1])):
            SOURCES += [(_src[:, k], _to[0][k], _to[1][k]) for k in range(4)]

        def source_hi(act, n):
            src, hi, _ = SOURCES[n]
            act.activation(hi, src, ACT.Copy).then_inc(s["part_hi"], 1)

        def source_lo(dve, n):
            src, hi, lo = SOURCES[n]
            dve.wait_ge(s["part_hi"], n + 1)
            dve.tensor_tensor(lo, src, hi.bitcast(F32), ALU.subtract).then_inc(s["part_lo"], 1)

        def slab(n):
            w = sum(c for _, c in SLABS[n][3])
            if n >= SPLIT_SLAB:
                return cut(land, (n - SPLIT_SLAB) % LAND * SLABW, SLABS[n][2], w)
            return cut(ring, (n % RING) * SLABW, SLABS[n][2], w)

        def slab_wait(eng, n):
            if n >= SPLIT_SLAB:
                m = n - SPLIT_SLAB
                eng.wait_ge(s[f"land{m % LAND}"], 16 * (m // LAND + 1))
            else:
                eng.wait_ge(s[f"slab{n % RING}"], 16 * (n // RING + 1))

        def split_views(n):
            _, _, sl, c0_, w, _ = JOBS[n]
            kts, q = SLABS[sl][2], n % 2
            return (slab(sl)[:, :, c0_:c0_ + w], cut(wh, 1024 * q, kts, P), cut(wl, 1024 * q, kts, P))

        def weights_hi(act, n):
            if n >= NJOB:
                return
            slab_wait(act, JOBS[n][2])
            act.wait_ge(s["gemm_done"], max(n - 1, SPLIT0))
            src, hi, _ = split_views(n)
            act.activation(hi, src, ACT.Copy).then_inc(s["weights_hi"], 1)

        def weights_lo(dve, n):
            if n >= NJOB:
                return
            dve.wait_ge(s["weights_hi"], n - SPLIT0 + 1)
            src, hi, lo = split_views(n)
            dve.tensor_tensor(lo, src, hi.bitcast(F32), ALU.subtract).then_inc(s["weights_lo"], 1)

        def out_of(n, eng):
            e = JOBS[n][5]
            eng.wait_ge(s["evac_" + e], evacuated(n, e))

        def bank_free(n, eng):
            if before_in_bank(n) is not None:
                out_of(before_in_bank(n), eng)

        def page_dma(eng, dst, pages_of, b, j, sem):
            pg = eng.value_load(pages[0:1, 8 * b + j:8 * b + j + 1], min_val=0, max_val=i["ki"].shape[0] - 1)
            eng.dma_start(dst, pages_of[bass.ds(pg, 1)].rearrange("o p c -> (o p) c")).then_inc(sem, 16)

        def kv_sem(b):
            name, before = (("cache_in0", 0), ("cache_in1", 0), ("cache_in2", 0), ("cache_in3", 0),
                            ("ki_in0", 128 * 4), ("ki_in1", 128 * 4), ("aux_in", 48), ("mvs_in1", 0))[b]
            return s[name], before + 128

        def mks_full(b):
            return 128 + 16 * (b // 4 + 1)

        def mvs_full(b):
            if 2 <= b < 6:
                return s[f"cache_in{b - 2}"], mks_full(b + 2) + 16
            return s[f"mvs_in{b % 2}"], 128 * (b % 2) + 16 * (b // 4 + 1)

        def pair(b):
            return ps[:, b:b + 2, 0:HALF]

        def h2(t):
            return t.rearrange("p (h c) -> p h c", h=2)

        ROPE = [("ik", 0, ik), ("iq", 0, iq[:, 0]), ("iq", 1, iq[:, 1])]
        ROPE += [("aq", t, aq3[:, t]) for t in range(4)] + [("ak", 0, ak)]
        NX = 8
        NU = 32
        scale_c = float(np.float32(128.0 ** -0.5))
        block = ctx.enter_context(nc.Block())

        @block.sync
        def _(sp):
            first = COFF["cos"][0]
            sp.dma_start(cst[:, 0:first], i["const"][:, 0:first]).then_inc(s["ones_in"], 16)
            for n in range(2):
                sp.dma_start(xT3[:, 4 * n:4 * n + 4], i["xT"][:, 4 * n:4 * n + 4]).then_inc(s[f"x_in{n}"], 16)
            sp.dma_start(vec[:, :], i["vec"]).then_inc(s["inputs_in"], 16)
            sp.dma_start(cst[:, first:], i["const"][:, first:]).then_inc(s["inputs_in"], 16)

            def stream(first, last):
                for n in range(first, last):
                    _, _, kts, cols = SLABS[n]
                    w = kts * sum(c for _, c in cols)
                    if n >= RING:
                        sp.wait_ge(s["gemm_done"], FREED[n - RING])
                    off = (n % RING) * SLABW
                    sp.dma_start(ring[:, off:off + w], i["slabs"][n, :, 0:w]).then_inc(s[f"slab{n % RING}"], 16)

            stream(0, 2)
            sp.dma_start(pages[0:1, :], i["pages"]).then_inc(s["aux_in"], 16)
            sp.dma_start(memT, i["memT"]).then_inc(s["aux_in"], 16)
            sp.dma_start(sh_in[:, :], i["shT"]).then_inc(s["aux_in"], 16)
            stream(2, RING)
            sp.wait_ge(s["aux_in"], 48)
            for b in range(DB):
                for j in range(8):
                    page_dma(sp, ki[b][:, P * j:P * (j + 1)], i["ki"], b, j, s[f"ki_in{b % 2}"])

            def kv_row(b):
                for j in range(8):
                    page_dma(sp, kvb[b][:, j], i["kv"], b, j, kv_sem(b)[0])

            stream(RING, 13)
            sp.wait_ge(s["norm_out"], 8)
            kv_row(0)
            kv_row(1)
            sp.wait_ge(s["isum"], 12)
            kv_row(2)
            sp.wait_ge(s["rope_out"], 8)
            kv_row(3)
            sp.wait_ge(s["gemm_done"], job_at("mv", 3) + 1)
            for b in range(4, 7):
                kv_row(b)
            sp.wait_ge(s["stored"], 16 * 5)
            kv_row(7)
            stream(13, KV_SLAB)
            def mks_in(b):
                sp.wait_ge(s["mks_used"] if b >= 4 else s["vs_used"], b - 3 if b >= 4 else 8)
                sp.dma_start(mks[:, b % 4], i["mks"][b]).then_inc(s[f"cache_in{b % 4}"], 16)

            def mvs_in(b):
                if b >= 6:
                    sp.wait_ge(s["mvs_used"], b - 5)
                elif b >= 2:
                    sp.wait_ge(s["mks_used"], b + 3)
                sp.dma_start(mvs[b], i["mvs"][b]).then_inc(mvs_full(b)[0], 16)

            for b in range(4):
                mks_in(b)
            for b in range(2):
                mvs_in(b)
            stream(KV_SLAB, MKS_SLAB)
            for b in range(4, DB):
                mks_in(b)
            stream(MKS_SLAB, MVS_SLAB)
            for b in range(2, DB):
                mvs_in(b)
            stored_gates = 0
            for n in range(MVS_SLAB, SPLIT_SLAB + RING):
                if n < SPLIT_SLAB:
                    stream(n, n + 1)
                while stored_gates < 24 and JOBS[job_at("gate", stored_gates)][2] <= n - RING:
                    m = stored_gates
                    out_of(job_at("gate", m), sp)
                    sp.dma_start(i["gates"][m], gst[:, m % 2]).then_inc(s[f"gate_stored{m % 2}"], 16)
                    stored_gates += 1
            def gate_in(m):
                if m >= 3:
                    out_of(job_at("branch", m - 3), sp)
                sp.dma_start(gb[:, m % 3], i["gates"][m]).then_inc(s[f"gate_in{m % 3}"], 16)

            for n in range(SPLIT_SLAB, NSLAB):
                _, _, kts, cols = SLABS[n]
                w = kts * sum(c for _, c in cols)
                m = n - SPLIT_SLAB
                if m < LAND:
                    sp.wait_ge(s["gemm_done"], SPLIT0)
                else:
                    sp.wait_ge(s["weights_lo"], FREED[n - LAND])
                off = m % LAND * SLABW
                sp.dma_start(land[:, off:off + w], i["slabs"][n, :, 0:w]).then_inc(s[f"land{m % LAND}"], 16)
                if m == 0:
                    sp.dma_start(xT3, i["xT"]).then_inc(s["inputs_in"], 16)
                if m == 1:
                    sp.wait_ge(s["oB_out"], 4)
                    for q in range(2):
                        sp.wait_ge(s[f"gate_stored{q}"], 16 * 12)
                if 1 <= m <= 12:
                    gate_in(2 * (m - 1))
                    gate_in(2 * (m - 1) + 1)

            for k in range(KT):
                sp.wait_ge(s["norm_out"], 25 + k)
                sp.dma_start(o["yT"][:, k], cut(yo, 0, KT, TOK)[:, k]).then_inc(s["y_stored"], 16)
            sp.wait_ge(s["y_stored"], 16 * KT)

        @block.gpsimd
        def _(pool):
            step = Steps(pool, s["pool_step"])
            step(pool.memset(epsc, EPS))
            step(pool.memset(gneps, GN_EPS))
            pool.wait_ge(s["norm_out"], 16)
            step(pool.memset(zi[0:64, :], 0.0))
            pool.wait_ge(s["aux_in"], 48)

            def rope_cos(n):
                kind, idx, raw = ROPE[n]
                out_of(job_at(kind, idx), pool)
                if n == 0:
                    pool.wait_ge(s["inputs_in"], 32)
                if n >= 2:
                    pool.wait_ge(s["rope_out"], n - 1)
                pool.tensor_tensor(rope2[:, n % 2], raw, k_("cos"), ALU.mult).then_inc(s["rope_cos"], 1)

            for n in range(3):
                rope_cos(n)
            pool.wait_ge(s["rope_out"], 1)
            pool.dma_start(o["ikT"], ik[0:64, :]).then_inc(s["stored"], 16)
            for n in range(3, 8):
                rope_cos(n)


            def edges(tiles_):
                pool.memset(pb3[:, tiles_, 0:1], 0.0).then_inc(s["pb_edge"], 1)
                pool.tensor_copy(pb3[:, tiles_, SEQ + 1:PBW:5], cut(sh_in, 0, PBT, DB)[:, tiles_]).then_inc(s["pb_edge"], 1)

            edges(slice(12, 14))
            pool.wait_ge(s["ss_out"], 1)
            step(pool.memset(za, 0.0))
            pool.wait_ge(s["rope_out"], 8)
            pool.dma_start(lora, i["lora"]).then_inc(s["lora_in"], 16)
            pool.dma_start(o["kT"], ak).then_inc(s["stored"], 16)
            out_of(job_at("av"), pool)
            pool.dma_start(o["vT"], av).then_inc(s["stored"], 16)
            out_of(job_at("mv", 3), pool)
            pool.dma_start(o["mkT"], mkT).then_inc(s["stored"], 16)
            pool.dma_start(o["mv"], mv).then_inc(s["stored"], 16)
            pool.wait_ge(s["vs_used"], 8)
            edges(slice(0, 12))

            step(pool.memset(zc, 0.0))
            pool.wait_ge(s["stored"], 16 * 5)
            so = cut(sh_out, 0, PBT, 9)
            levels = cut(cst, COFF["lev"][0], 4, P)

            def diff(dst, tile):
                cur = pb3[:, tile]
                out_of(job_at("pb", tile), pool)
                pool.tensor_copy(so[:, tile, 0:1], cur[:, SEQ:SEQ + 1])
                pool.tensor_copy(so[:, tile, 1:9], cur[:, SEQ + 5:PBW:5])
                pool.tensor_tensor(dst[:, 0:SEQ], cur[:, 0:SEQ], cur[:, 1:SEQ + 1], ALU.subtract)
                c5 = cur[:, SEQ + 1:PBW].rearrange("p (b c) -> p b c", c=5)
                pool.tensor_tensor(dst[:, SEQ:TOK].rearrange("p (b c) -> p b c", c=4), c5[:, :, 0:4], c5[:, :, 1:5],
                                   ALU.subtract).then_inc(s["diff"], 1)

            pool.wait_ge(s["pb_edge"], 4)
            diff(tA, 12)
            diff(r_, 13)
            diff(k__, 4)
            diff(v__, 8)
            for j in range(4):
                if j:
                    pool.wait_ge(s["oB_out"], j)
                else:
                    pool.wait_ge(s["t12"], 2)
                diff(r_, j)
                for hh in range(2):
                    g = 2 * j + hh
                    for c in range(4):
                        pool.wait_ge(s["m4"], 4 * g + c + 1)
                        pool.wait_ge(s["dlow"], 4 * g + c + 1)
                        if g and c == 0:
                            pool.wait_ge(s["t0s_out"] if hh == 0 else s["state"], 16 * j if hh == 0 else 4 * g)
                        pool.tensor_tensor(dx[:, c, 2], m4[:, c, 0], levels[:, 0], ALU.mult).then_inc(s["lev"], 1)
                        pool.tensor_tensor(dx[:, c, 1], dx[:, c, 0], ident, ALU.add)
                        pool.wait_ge(s["lev"], 8 * g + c + 1)
                        pool.tensor_tensor(dx[:, c, 3], dx[:, c, 2], ident, ALU.add).then_inc(s["dx_set"], 1)
                    for c in range(4):
                        pool.tensor_tensor(lev[:, c, 1:4], m4[:, c, 0:1].to_broadcast([P, 3, P]), levels[:, 1:4],
                                           ALU.mult).then_inc(s["lev"], 1)
                    if hh == 0 and j < 3:
                        pool.wait_ge(s["tm"], j + 1)
                        diff(k__, 5 + j)
                        diff(v__, 9 + j)
                pool.wait_ge(s["state"], 4 * (2 * j + 2))
                pool.dma_start(t0s, i["wkvT"][j]).then_inc(s["t0s_in"], 16)
                step(pool.memset(zaa, 0.0))
                for hh in range(2):
                    pbs = slice(64 * hh, 64 * hh + 64)
                    pool.tensor_copy(zaa[pbs].rearrange("p (b c) -> p b c", c=36)[:, :, 0:4],
                                     AR[pbs, 0, SEQ:TOK].rearrange("p (b c) -> p b c", c=4)).then_inc(s["zaa"], 1)
                pool.wait_ge(s["state"], 4 * (2 * j + 2))
                pool.dma_start(o["wkvP"][j], T0).then_inc(s["T0_out"], 16)
                pool.wait_ge(s["sstate"], 2 * (j + 1))
                pool.dma_start(o["wkvS"][j], t0s).then_inc(s["t0s_out"], 16)
            pool.wait_ge(s["diff"], 14)
            pool.dma_start(o["shT"], sh_out[:, 0:PBT * 9]).then_inc(s["stored"], 16)
            pool.wait_ge(s["stored"], 16 * 6)
            pool.wait_ge(s["T0_out"], 16 * 4)
            pool.wait_ge(s["t0s_out"], 16 * 4)

        @block.tensor
        def _(pe):
            def norm(n, N):
                hn = N // 2 if N > 512 else N
                for k in range(KT):
                    pe.wait_ge(s["norm_sq"], KT * n + k + 1)
                    for h in range(2 if N > 512 else 1):
                        mm = pe.matmul(ps[:, 4 + h, 0:hn], k_("ones"), nbuf[n][0][:, k % 2, h * hn:(h + 1) * hn],
                                       start=(k == 0), stop=(k == KT - 1))
                    mm.then_inc(s["norm_ss"], 1)

            def job(n, src, only=None):
                kind, idx, sl, c0_, w, _ = JOBS[n]
                if only in (None, 0):
                    slab_wait(pe, sl)
                    bank_free(n, pe)
                W = slab(sl)
                b = bank_of(n)
                kts = SLABS[sl][2]
                for k in range(kts) if only is None else (only,):
                    a, z = k == 0, k == kts - 1
                    if kind == "mk":
                        mm = pe.matmul(ps[:, b, 0:NMEM], W[:, k, c0_:c0_ + w], memn[:, k], start=a, stop=z)
                    elif kind == "mv":
                        m = idx % 2
                        mm = pe.matmul(ps[:, b, 0:w], memn[:, k, P * m:P * (m + 1)], W[:, k, 0:w], start=a, stop=z)
                    else:
                        for h in range(2):
                            mm = pe.matmul(ps[0:w, b + h, 0:HALF], W[:, k, c0_:c0_ + w],
                                           src[:, k, h * HALF:(h + 1) * HALF], start=a, stop=z)
                if only in (None, kts - 1):
                    mm.then_inc(s["gemm_done"], 1)

            filled = [FILL0 - 1]

            def fill(*tag):
                for n, k in FILLS[tag]:
                    job(n, xn3, only=k)
                    filled[0] = n

            def fill_close(*tag):
                fill("close", *tag)
                out_of(filled[0], pe)

            def rope(n):
                kind, idx, raw = ROPE[n]
                out_of(job_at(kind, idx), pe)
                if n >= 2:
                    pe.wait_ge(s["rope_sin"], n - 1)
                for h in range(2):
                    mm = pe.matmul(ps[:, 4 + 2 * (n % 2) + h, 0:HALF], k_("rot"), raw[:, h * HALF:(h + 1) * HALF],
                                   start=True, stop=True)
                mm.then_inc(s["rope_rot"], 1)

            pe.wait_ge(s["ones_in"], 16)
            norm(0, TOK)
            pe.wait_ge(s["inputs_in"], 32)
            pe.wait_ge(s["norm_rt"], 1)
            norm(1, NMEM)
            pe.wait_ge(s["norm_out"], 8)
            for n in range(4):
                job(n, xn3)
            pe.wait_ge(s["norm_rt"], 2)
            for n in range(3):
                rope(n)
            pe.wait_ge(s["rope_sin"], 3)
            out_of(1, pe)
            for t in range(5):
                w = P if t < 4 else NS
                mm = pe.transpose(ps[0:w, 7, 4 * t:4 * t + 4], iwT[0:4, P * t:P * t + w], ident[0:4, 0:4])
            mm.then_inc(s["iw_tok"], 1)
            pe.wait_ge(s["zi_set"], 5)
            for t in range(1, 4):
                for h in range(4):
                    if t >= 2:
                        pe.wait_ge(s["relu"], 4 * (t - 2) + h + 1)
                    hp = slice(64 * (h % 2), 64 * (h % 2) + 64)
                    pe.matmul(ps[:, 4 + h, 0:P * (t + 1)], iq[hp, h // 2, P * t:P * (t + 1)], ik[hp, 0:P * (t + 1)],
                              start=True, stop=True).then_inc(s["iscore"], 1)
            for n in range(4, FILL0):
                job(n, xn3)
            pe.wait_ge(s["zi_set"], 4)
            for q in range(2):
                pe.wait_ge(s[f"ki_in{q}"], 128 * 4)
            pe.wait_ge(s["relu"], 12)
            for b in range(DB):
                for h in range(2):
                    pe.matmul(ps[:, 4 + h, :], zi[0:64, P * b:P * (b + 1)], ki[b][:, 512 * h:512 * (h + 1)],
                              start=(b == 0), stop=(b == DB - 1))
                pe.matmul(ps[:, 6, 0:NS], zi[0:64, P * b:P * (b + 1)], ik[0:64, SEQ:TOK],
                          start=(b == 0), stop=(b == DB - 1)).then_inc(s["ki_used"], 1)
            pe.wait_ge(s["rs"], 1)
            for h in range(3):
                w = 512 if h < 2 else NS
                mm = pe.matmul(ps[0:NS, 4 + h, 0:w], k_("sel"), rs[:, 512 * h:512 * h + w], start=True, stop=True)
            mm.then_inc(s["ssum"], 1)
            pe.wait_ge(s["ss_out"], 1)
            for n in range(3, 8):
                rope(n)
            pe.wait_ge(s["rope_sin"], 8)
            out_of(job_at("av"), pe)
            for t in range(5):
                w = P if t < 4 else NS
                mm = pe.transpose(ps[0:w, 6 + t // 4, P * (t % 4):P * (t % 4 + 1)], av[:, P * t:P * t + w], ident)
            mm.then_inc(s["v_tok"], 1)

            def unit(u):
                t, h = u // 8, u % 8
                return t, h // 2, slice(64 * (h % 2), 64 * (h % 2) + 64), h % 2

            def turn_bank(u):
                return 1 if u % 2 else 7

            def p_score(u):
                t, ht, hp, half = unit(u)
                if u >= 3:
                    pe.wait_ge(s["p_exp"], u - 2)
                pe.matmul(ps[:, 4 + u % 3, 0:P * (t + 1)], aq3[hp, ht, P * t:P * (t + 1)], ak[hp, 0:P * (t + 1)],
                          start=True, stop=False)
                pe.matmul(ps[:, 4 + u % 3, 0:P * (t + 1)], identb[:, :], biasp[:, t, 0:P * (t + 1)],
                          start=False, stop=True).then_inc(s["p_score"], 1)

            def p_turn(u):
                t, ht, hp, half = unit(u)
                pe.wait_ge(s["p_prob"], u + 1)
                if u >= 2:
                    pe.wait_ge(s["p_pT_out"], u - 1)
                for k in range(t + 1):
                    mm = pe.transpose(ps[:, turn_bank(u), P * k:P * (k + 1)], pp[:, u % 3, P * k:P * (k + 1)], ident)
                mm.then_inc(s["p_pT"], 1)

            def p_out(u):
                t, ht, hp, half = unit(u)
                pe.wait_ge(s["p_pT_out"], u + 1)
                if u % 8 == 0 and t >= 1:
                    pe.wait_ge(s["oA_out"], t)
                for k in range(t + 1):
                    mm = pe.matmul(ps[hp, 0, P * ht:P * (ht + 1)], vt[:, k, hp], ppt[:, u % 2, k],
                                   start=(k == 0), stop=(k == t))
                mm.then_inc(s["pav_done"], 1)

            pe.wait_ge(s["rope_out"], 8)
            pe.wait_ge(s["bias_done"], 4)
            pe.wait_ge(s["v_tok_out"], 2)
            pe.wait_ge(s["bf_const"], 2)
            for u in range(NU + 3):
                if u < NU:
                    p_score(u)
                if 2 <= u < NU + 2:
                    p_turn(u - 2)
                if u == 1:
                    pe.wait_ge(s["ss_out"], 1)
                if u >= 3:
                    p_out(u - 3)
                fill("p", u)
            fill("need", "cq", 3)
            fill("need", "pb", 13)
            fill_close("p", 0)

            pe.wait_ge(s["za_set"], 4)
            pe.wait_ge(s["p_exp"], NU)
            pe.wait_ge(s["p_pT_out"], NU)
            pe.wait_ge(s["selected"], 1)
            pe.wait_ge(s["oA_out"], 4)
            for hb in range(2):
                sb_ = s_bank[hb]
                for b4 in range(4):
                    b = 4 * hb + b4
                    pe.wait_ge(*kv_sem(b))
                    w = za[:, 640 * hb + P * b4:640 * hb + P * (b4 + 1)]
                    for h in range(2):
                        pe.matmul(ps[:, sb_ + h, :], w, kvb[b][:, 4 * h:4 * h + 4, 0:P], start=(b4 == 0), stop=False)
                    pe.matmul(ps[:, sb_ + 2, 0:NS], w, ak[:, SEQ:TOK], start=(b4 == 0), stop=False)
                for h in range(3):
                    w = 512 if h < 2 else NS
                    mm = pe.matmul(ps[:, sb_ + h, 0:w], repb[0:NS, P * hb:P * (hb + 1)], biass[0:NS, 512 * h:512 * h + w],
                                   start=False, stop=True)
                mm.then_inc(s["s_score"], 1)
            for hb in range(2):
                sb_ = s_bank[hb]
                pe.wait_ge(s["s_prob"], hb + 1)
                for t in range(9):
                    w = P if t < 8 else NS
                    mm = pe.transpose(ps[0:w, sb_ + t // 4, P * (t % 4):P * (t % 4 + 1)], pr[hb][:, P * t:P * t + w], ident)
                mm.then_inc(s["s_pT"], 1)
                pe.wait_ge(s["s_pT_out"], 3 * (hb + 1))
                for b4 in range(4):
                    kv = kvb[4 * hb + b4]
                    for t in range(8):
                        pe.matmul(ps[:, sb_ + 3, 32 * b4:32 * b4 + 32], kv[:, t, P:2 * P], pt[:, t, 32 * b4:32 * b4 + 32],
                                  start=(t == 0), stop=False)
                    pe.matmul(ps[:, sb_ + 3, 32 * b4:32 * b4 + 32], vt[0:NS, 4], pt[0:NS, 8, 32 * b4:32 * b4 + 32],
                              start=False, stop=True).then_inc(s["vs_used"], 1)

            pe.wait_ge(s["s_exp"], 2)
            pe.wait_ge(s["oA_out"], 8)
            def x_score(v):
                t, h0 = v // 2, 2 * (v % 2)
                if v >= 3:
                    pe.wait_ge(s["x_exp"], 2 * (v - 2))
                for h in range(2):
                    mm = pe.matmul(ps[:, 4 + v % 3, NMEM * h:NMEM * (h + 1)], cq3[:, h0 + h, P * t:P * (t + 1)],
                                   mkT[:, h0 + h], start=True, stop=True)
                mm.then_inc(s["x_score"], 1)

            def x_turn(v):
                pe.wait_ge(s["x_prob"], v + 1)
                if v >= 2:
                    pe.wait_ge(s["x_pT_out"], v - 1)
                for h in range(2):
                    for m in range(2):
                        mm = pe.transpose(ps[:, turn_bank(v), P * (2 * h + m):P * (2 * h + m + 1)],
                                          xp[:, v % 3, h, P * m:P * (m + 1)], ident)
                mm.then_inc(s["x_pT"], 1)

            def x_out(v):
                t, h0 = v // 2, 2 * (v % 2)
                pe.wait_ge(s["x_pT_out"], v + 1)
                if v % 2 == 0 and t >= 1:
                    pe.wait_ge(s["oC_out"], t)
                for h in range(h0, h0 + 2):
                    for m in range(2):
                        mm = pe.matmul(ps[:, 0, P * h:P * (h + 1)], mv[:, m, P * h:P * (h + 1)],
                                       ppt[:, v % 2, 2 * (h - h0) + m], start=(m == 0), stop=(m == 1))
                mm.then_inc(s["xav_done"], 1)

            for v in range(NX + 3):
                if v < NX:
                    x_score(v)
                if 2 <= v < NX + 2:
                    x_turn(v - 2)
                if v >= 3:
                    x_out(v - 3)
                fill("x", v)
            fill("need", "pb", 8)

            pe.wait_ge(s["zc_set"], 1)
            pe.wait_ge(s["x_exp"], 16)
            for b in range(DB):
                pe.wait_ge(s[f"cache_in{b % 4}"], mks_full(b))
                for h in range(4):
                    n = 4 * b + h
                    mm = pe.matmul(ps[:, 4, 0:NMEM], zc[:, P * n:P * (n + 1)], mks[:, b % 4, NMEM * h:NMEM * (h + 1)],
                                   start=(n == 0), stop=(n == 31))
                mm.then_inc(s["mks_used"], 1)
            fill("c", 0)
            pe.wait_ge(s["x_prob"], 9)
            for m in range(2):
                mm = pe.transpose(ps[:, 5, P * m:P * (m + 1)], cp[:, P * m:P * (m + 1)], ident)
            mm.then_inc(s["x_pT"], 1)
            fill("c", 1)
            pe.wait_ge(s["x_pT_out"], 9)
            pe.wait_ge(s["oC_out"], 4)
            for b in range(DB):
                pe.wait_ge(*mvs_full(b))
                for h in range(4):
                    n = 4 * b + h
                    for m in range(2):
                        mm = pe.matmul(ps[:, 0, 4 * n:4 * n + 4], mvs[b][:, 512 * m + P * h:512 * m + P * (h + 1)],
                                       cpt[:, m, 4 * n:4 * n + 4], start=(m == 0), stop=(m == 1))
                mm.then_inc(s["mvs_used"], 1)
            fill("c", 2)

            def wide(b, w, src):
                for h in range(2):
                    mm = pe.matmul(ps[:, b + h, 0:HALF], w, src[:, h * HALF:(h + 1) * HALF], start=True, stop=True)
                return mm

            def early(j, n):
                cols = slice(P * j, P * (j + 1))
                if n == 0:
                    wide(0, lora[0:64, cols], t12[0:64]).then_inc(s["lora_up"], 1)
                elif n == 1:
                    pe.wait_ge(s["tanhs"], 2 * j + 1)
                    wide(0, lora[64:128, cols], t12[64:128]).then_inc(s["lora_up"], 1)
                else:
                    pe.wait_ge(s["kk_sq"], j + 1)
                    pe.wait_ge(s["tanhs"], 2 * j + 2)
                    wide(0, k_("blk"), tA).then_inc(s["kk_ss"], 1)

            pe.wait_ge(s["oC_out"], 5)
            pe.wait_ge(s["lora_in"], 16)
            for j in range(4):
                if j == 0:
                    pe.wait_ge(s["t12"], 2)
                    for n in range(3):
                        early(0, n)
                        if n == 0:
                            fill("prep", 0, 0)
                else:
                    fill("prep", j, 0)
                fill("prep", j, 1)
                pe.wait_ge(s["rk"], j + 1)
                wide(6, k_("blk"), L_).then_inc(s["rk_sum"], 1)
                fill("prep", j, 2)
                if j < 3:
                    fill("need", "pb", 9 + j)
                if j:
                    pe.wait_ge(s["oB_out"], j)
                pe.wait_ge(s["factors"], j + 1)
                pe.wait_ge(s["bonus"], j + 1)
                fill_close("tm", j)
                for n, src in enumerate((v__, bt, kt_)):
                    for c in range(4):
                        pe.transpose(ps[:, n, P * c:P * (c + 1)], src[:, P * c:P * (c + 1)], ident)
                    mm = pe.transpose(ps[0:NS, 3, P * n:P * (n + 1)], src[:, SEQ:TOK], ident)
                mm.then_inc(s["tm"], 1)
                for hh in range(2):
                    g = 2 * j + hh
                    hp = slice(64 * hh, 64 * hh + 64)
                    for c in range(4):
                        t = slice(C * c, C * (c + 1))
                        if hh:
                            pe.wait_ge(s["state"], 4 * g)
                            pe.wait_ge(s["y_chunk"], 4 * g)
                        pe.matmul(ps[:, 4 + c, 0:256], bt[hp, t], AR[hp, :, t], start=True, stop=True)
                        pe.matmul(ps[:, 4 + c, 256:512], kt_[hp, t], AR[hp, :, t], start=True,
                                  stop=True).then_inc(s["pairs"], 1)
                    if hh == 0:
                        pe.wait_ge(s["tm_out"], 4 * (j + 1))
                    if hh:
                        fill_close("group", 2 * j)
                        if j < 3:
                            pe.wait_ge(s["kk_rt"], j + 2)
                    for c in range(4):
                        t = slice(C * c, C * (c + 1))
                        pe.matmul(ps[:, c, 0:P], AR[hp, 0, t], bt[hp, t], start=True, stop=True).then_inc(s["low"], 1)
                    for r in range(4):
                        for c in range(4):
                            if r == 0:
                                pe.wait_ge(s["dx_set"], 4 * g + c + 1)
                                pe.matmul(ps[:, 4 + c, 0:P], dx[:, c, 2], dx[:, c, 0], start=True, stop=True)
                                mm = pe.matmul(ps[:, 4 + c, 256:256 + P], dx[:, c, 0], dx[:, c, 2], start=True, stop=True)
                            else:
                                pe.wait_ge(s["dsq"], 12 * g + 4 * (r - 1) + c + 1)
                                if r > 1:
                                    pe.wait_ge(s["xup"], 12 * g + 4 * (r - 2) + c + 1)
                                if r < 3:
                                    pe.matmul(ps[:, 4 + c, 0:P], dx[:, c, 2], dx[:, c, 0], start=True, stop=True)
                                    pe.matmul(ps[:, 4 + c, 256:256 + P], dx[:, c, 0], dx[:, c, 2], start=True, stop=True)
                                pe.matmul(ps[:, c, 0:P], dx[:, c, 2], dx[:, c, 1], start=True, stop=True)
                                mm = pe.matmul(ps[:, c, P:256], dx[:, c, 0], dx[:, c, 3], start=True, stop=True)
                            mm.then_inc(s["round"], 1)
                    for l in range(3):
                        for c in range(4):
                            if l == 0:
                                pe.wait_ge(s["lev"], 8 * g + 4 + c + 1)
                                pe.wait_ge(s["xup"], 12 * g + 8 + c + 1)
                            else:
                                pe.wait_ge(s["xlev"], 12 * g + 4 * (l - 1) + c + 1)
                            pe.matmul(ps[:, 4 + c, 0:P], lev[:, c, l + 1], dx[:, c, 1], start=True,
                                      stop=True).then_inc(s["mx"], 1)
                        for c in range(4):
                            pe.wait_ge(s["mx_out"], 12 * g + 4 * l + c + 1)
                            if l < 2:
                                pe.matmul(ps[:, c, 0:P], dx[:, c, 3], tt[:, c], start=True, stop=True)
                            pe.matmul(ps[:, c, P:256], tt[:, c], dx[:, c, 3], start=True,
                                      stop=True).then_inc(s["xmx"], 1)
                    pe.wait_ge(s["mx_out"], 12 * g + 12)
                    for c in range(4):
                        t = slice(C * c, C * (c + 1))
                        n = 4 * g + c
                        mm = pe.matmul(ps[:, 4, 0:64], m4[:, c, 2], tm[:, 0, c, hp], start=True, stop=(c == 0))
                        if c:
                            pe.wait_ge(s["state"], n)
                            mm = pe.matmul(ps[:, 4, 0:64], AR[hp, 0, t], T0[hp], start=False, stop=True)
                        mm.then_inc(s["z"], 1)
                        if c == 0:
                            pe.wait_ge(s["xlev"], 12 * g + 12)
                        fill("chunk", n, 0)
                        pe.wait_ge(s["z_out"], n + 1)
                        pe.wait_ge(s["xlev"], 12 * g + 8 + c + 1)
                        pe.matmul(ps[:, 5, 0:64], dx[:, c, 3], zs, start=True, stop=True).then_inc(s["u"], 1)
                        fill("chunk", n, 1)
                        pe.wait_ge(s["u_out"], n + 1)
                        pe.matmul(ps[hp, 7, 0:64], tm[:, 1, c, hp], us, start=True, stop=False)
                        pe.matmul(ps[hp, 7, 0:64], tm[:, 2, c, hp], tm[:, 0, c, hp], start=False,
                                  stop=True).then_inc(s["dstate"], 1)
                        if c:
                            pe.wait_ge(s["y_chunk"], n)
                        pe.matmul(ps[hp, 6, 0:P], tm[:, 0, c, hp], m4[:, c, 3], start=True, stop=False)
                        if c:
                            pe.matmul(ps[hp, 6, 0:P], T0[hp], AR[hp, 1, t], start=False, stop=False)
                        pe.matmul(ps[hp, 6, 0:P], us, m4[:, c, 1], start=False, stop=True).then_inc(s["ychunk"], 1)
                        if hh == 0 and j < 3 and c in (0, 1, 3):
                            early(j + 1, (0, 1, 0, 2)[c])
                        fill("chunk", n, 2)
                pe.wait_ge(s["state"], 8 * (j + 1))
                pe.wait_ge(s["y_chunk"], 8 * (j + 1))
                pe.wait_ge(s["t0s_in"], 16 * (j + 1))
                pe.wait_ge(s["zaa"], 2 * (j + 1))
                heads = [(hh, 2 * j + hh, slice(64 * hh, 64 * hh + 64), dec[hh]) for hh in range(2)]
                st = slice(SEQ, TOK)
                pe.wait_ge(s["xlev"], 24 * j + 24)
                for hh, n, hp, d in heads:
                    pe.matmul(ps[0:NS, 4 + hh, 0:64], bt[hp, st], AR[hp, :, st], start=True, stop=True)
                    pe.matmul(ps[0:NS, 4 + hh, 64:128], kt_[hp, st], AR[hp, :, st], start=True, stop=True)
                    pe.matmul(ps[0:NS, 4 + hh, 128:160], AR[hp, 0, st], bt[hp, st], start=True, stop=True).then_inc(s["s_pairs"], 1)
                fill("dec", j, 0)
                for hh, n, hp, d in heads:
                    pe.wait_ge(s["s_m4"], 3 * n + 3)
                    pe.matmul(ps[0:NS, 6 + hh, 0:NS], d["m4"][0:NS, 0], d["low"], start=True, stop=True).then_inc(s["s_inv"], 1)
                for hh, n, hp, d in heads:
                    pe.matmul(ps[0:NS, hh, 0:64], d["m4"][0:NS, 2], tms[0:NS, 0, hp], start=True, stop=False)
                    for b in range(DB):
                        mm = pe.matmul(ps[0:NS, hh, 0:64], zaa[hp, NS * b:NS * (b + 1)], t0s[hp, b], start=False,
                                       stop=(b == DB - 1))
                    mm.then_inc(s["s_z"], 1)
                for hh, n, hp, d in heads:
                    pe.wait_ge(s["s_inv_out"], 4 * j + hh + 1)
                    pe.matmul(ps[0:NS, 6 + hh, 64:64 + NS], d["sq"], d["x"], start=True, stop=True).then_inc(s["s_inv"], 1)
                fill("dec", j, 1)
                for hh, n, hp, d in heads:
                    pe.wait_ge(s["s_z_out"], n + 1)
                    pe.wait_ge(s["s_inv_out"], 4 * j + 2 + hh + 1)
                    pe.matmul(ps[0:NS, hh, 64:128], d["xt"], d["z"], start=True, stop=True).then_inc(s["s_u"], 1)
                fill("dec", j, 2)
                for hh, n, hp, d in heads:
                    pe.wait_ge(s["s_u_out"], n + 1)
                    pe.matmul(ps[hp, 4 + hh, 256:256 + NS], tms[0:NS, 0, hp], d["m4"][0:NS, 3], start=True, stop=False)
                    for b in range(DB):
                        pe.matmul(ps[hp, 4 + hh, 256 + 4 * b:260 + 4 * b], t0s[hp, b],
                                  AR[hp, 1, SEQ + 4 * b:SEQ + 4 * b + 4], start=False, stop=False)
                    pe.matmul(ps[hp, 4 + hh, 256:256 + NS], d["u"], d["m4"][0:NS, 1], start=False, stop=True).then_inc(s["s_y"], 1)
                fill("dec", j, 3)
                for hh, n, hp, d in heads:
                    pe.wait_ge(s["s_blk"], 4 * j + 2 + hh + 1)
                    pe.matmul(ps[hp, 6 + hh, :], tms[0:NS, 1, hp], d["ub"][0:NS], start=True, stop=False)
                    pe.matmul(ps[hp, 6 + hh, :], tms[0:NS, 2, hp], d["vb"][0:NS], start=False, stop=True).then_inc(s["s_dstate"], 1)
                fill("dec", j, 4)
                pe.wait_ge(s["s_y_out"], 2 * (j + 1))
                wide(0, k_("blk"), y_).then_inc(s["mean"], 1)
                fill("gn", j, 0)
                pe.wait_ge(s["yc_sq"], j + 1)
                wide(4, k_("blk"), tA).then_inc(s["var"], 1)
                fill("gn", j, 1)
                pe.wait_ge(s["yc"], j + 1)
                wide(0, lora[:, 512 + P * j:512 + P * (j + 1)], t13).then_inc(s["g"], 1)
                fill("gn", j, 2)
            fill("need", "gate", 23)

            def split_ready(n):
                pe.wait_ge(s["weights_lo"], n - SPLIT0 + 1)
                bank_free(n, pe)

            def split_step(n, src, ks=None):
                kts = SLABS[JOBS[n][2]][2]
                _, whi, wlo = split_views(n)
                b = bank_of(n)
                hi, lo = src
                for k in ks if ks else range(kts):
                    a, z = k == 0, k == kts - 1
                    for h in range(2):
                        c = slice(h * HALF, (h + 1) * HALF)
                        pe.matmul(ps[:, b + h, 0:HALF], whi[:, k], hi[k][:, c], start=a, stop=False)
                        pe.matmul(ps[:, b + h, 0:HALF], whi[:, k], lo[k][:, c], start=False, stop=False)
                    for h in range(2):
                        c = slice(h * HALF, (h + 1) * HALF)
                        mm = pe.matmul(ps[:, b + h, 0:HALF], wlo[:, k], hi[k][:, c], start=False, stop=z)
                if z:
                    mm.then_inc(s["gemm_done"], 1)

            def split_job(n, src):
                split_ready(n)
                split_step(n, src)

            def norm_sum(n):
                pe.wait_ge(s["norm_ss"], KT * (n + 1))
                for h in range(2):
                    mm = pe.matmul(ps[:, 4 + h, 0:HALF], k_("ones"), squares[:, h * HALF:(h + 1) * HALF],
                                   start=True, stop=True)
                mm.then_inc(s["norm_sum"], 1)

            for n in range(SPLIT0, job_at("out", 0)):
                kind, idx, *_ = JOBS[n]
                br = merge_at(idx)[1]
                if idx < 6 and idx % 2 == 0:
                    pe.wait_ge(s["part_lo"], (4, 12, 12)[br])
                split_job(n, HEADS[br])
            pe.wait_ge(s["part_lo"], PART["merge"] + 8)
            for n in range(job_at("out", 0), job_at("up", 0)):
                split_job(n, M)
            norm_sum(2)
            up0 = job_at("up", 0)
            split_ready(up0)
            split_ready(up0 + 1)
            for k in range(KT):
                pe.wait_ge(s["part_lo"], PART["x"] + k + 1)
                for n in (up0, up0 + 1):
                    split_step(n, X, [k])
            for n in range(up0 + 2, NJOB):
                kind, idx, *_ = JOBS[n]
                if kind == "up":
                    split_job(n, X)
                else:
                    r = idx // 8
                    if idx % 8 == 0:
                        pe.wait_ge(s["part_lo"], PART["hid"] + 8 * (r + 1))
                    if idx == 31:
                        pe.wait_ge(s["norm_rt"], 3)
                    split_job(n, H[r % 2])
            norm_sum(3)

        @block.scalar
        def _(act):
            step = Steps(act, s["act_step"])

            def square(n, src, N, k):
                if KT * n + k >= 2:
                    act.wait_ge(s["norm_ss"], KT * n + k - 1)
                if n == 0 and k % 4 == 0:
                    act.wait_ge(s[f"x_in{k // 4}"], 16)
                if n >= 2:
                    out_of(job_at("out", k) if n == 2 else job_at("down", 24 + k), act)
                act.activation(nbuf[n][0][:, k % 2, 0:N], src[:, k], ACT.Square).then_inc(s["norm_sq"], 1)

            def norm(n, src, N, first=0):
                for k in range(first, KT):
                    square(n, src, N, k)
                if n >= 2:
                    act.wait_ge(s["norm_sum"], n - 1)
                else:
                    act.wait_ge(s["norm_ss"], KT * (n + 1))
                if n:
                    act.wait_ge(s["norm_rc"], n)
                if N > 512:
                    act.activation(h2(nbuf[n][1][:, 0:N]), pair(4), ACT.Sqrt, bias=epsc, scale=1.0 / D).then_inc(s["norm_rt"], 1)
                else:
                    act.activation(nbuf[n][1][:, 0:N], ps[:, 4, 0:N], ACT.Sqrt, bias=epsc, scale=1.0 / D).then_inc(s["norm_rt"], 1)

            def evac(n):
                kind, idx, sl, c0_, w, e = JOBS[n]
                act.wait_ge(s["gemm_done"], n + 1)
                b = bank_of(n)
                src = ps[0:min(w, P), b:b + 2, 0:HALF]
                fn = ACT.Copy
                if kind == "pb":
                    act.wait_ge(s["pb_edge"], 2 if idx >= 12 else 4)
                    dst = pb3[:, idx]
                    act.activation(dst[:, 1:HALF + 1], ps[:, b, 0:HALF], fn)
                    act.activation(dst[:, HALF + 1:SEQ + 1], ps[:, b + 1, 0:SEQ - HALF], fn)
                    last = act.activation(dst[:, SEQ + 1:PBW].rearrange("p (b c) -> p b c", c=5)[:, :, 1:5],
                                          ps[:, b + 1, SEQ - HALF:HALF].rearrange("p (b c) -> p b c", c=4), fn)
                elif kind == "mk":
                    last = act.activation(mkT[:, idx], ps[:, b, 0:NMEM], fn)
                elif kind == "mv":
                    last = act.activation(mv[:, idx % 2, 256 * (idx // 2):256 * (idx // 2 + 1)], ps[:, b, 0:w], fn)
                elif kind == "gate":
                    if idx >= 2:
                        act.wait_ge(s[f"gate_stored{idx % 2}"], 16 * (idx // 2))
                    dj, br = merge_at(idx)
                    last = act.activation(h2(gst[:, idx % 2]), src, ACT.Tanh, bias=hgate[:, 8 * br + dj:8 * br + dj + 1], scale=0.5)
                elif kind == "up":
                    if idx >= 2:
                        act.wait_ge(s["hid_sq"], idx - 1)
                        act.wait_ge(s["part_hi"], PART["hid"] + idx - 1)
                    last = act.activation(h2(ub2[:, idx % 2]), src, ACT.Relu)
                else:
                    dst = {"ik": lambda: ik, "iw": lambda: iwT[0:4], "iq": lambda: iq[:, idx], "aq": lambda: aq3[:, idx],
                           "ak": lambda: ak, "av": lambda: av, "cq": lambda: cq3[:, idx]}[kind]()
                    last = act.activation(h2(dst), src, fn)
                last.then_inc(s["evac_a"], 1)

            def evacs(*tag):
                for n in FILLED[tag]:
                    evac(n)

            act.wait_ge(s["pool_step"], 2)
            norm(0, xT3, TOK)
            act.wait_ge(s["aux_in"], 48)
            norm(1, memT, NMEM)
            act.wait_ge(s["norm_out"], 16)
            for n in range(4):
                evac(n)
            for t in range(1, 4):
                for h in range(4):
                    act.wait_ge(s["iscore"], 4 * (t - 1) + h + 1)
                    if t >= 2:
                        act.wait_ge(s["isum"], 4 * (t - 2) + h + 1)
                    act.activation(rl[:, h, 0:P * (t + 1)], ps[:, 4 + h, 0:P * (t + 1)], ACT.Relu).then_inc(s["relu"], 1)
            for n in range(4, FILL0):
                evac(n)
            act.wait_ge(s["v_tok"], 1)
            act.activation(vt[:, 0:4], cut(ps[:, 6], 0, 4, P), ACT.Copy).then_inc(s["v_tok_out"], 1)
            act.activation(vt[0:NS, 4], ps[0:NS, 7, 0:P], ACT.Copy).then_inc(s["v_tok_out"], 1)
            for u in range(NU + 3):
                if u < NU:
                    t = u // 8
                    act.wait_ge(s["p_max"], u + 1)
                    if u >= 3:
                        act.wait_ge(s["p_pT"], u - 2)
                    act.activation(pp[:, u % 3, 0:P * (t + 1)], ps[:, 4 + u % 3, 0:P * (t + 1)], ACT.Exp,
                                   bias=nm[:, u % 4:u % 4 + 1], scale=0.125,
                                   accum_out=sm[:, u % 4:u % 4 + 1]).then_inc(s["p_exp"], 1)
                if 2 <= u < NU + 2:
                    w = u - 2
                    t = w // 8
                    act.wait_ge(s["p_pT"], w + 1)
                    if w >= 2:
                        act.wait_ge(s["pav_done"], w - 1)
                    act.activation(ppt[:, w % 2, 0:t + 1], cut(ps[:, 1 if w % 2 else 7], 0, t + 1, P),
                                   ACT.Copy).then_inc(s["p_pT_out"], 1)
                if u >= 3 and (u - 3) % 8 == 7:
                    t = (u - 3) // 8
                    act.wait_ge(s["pav_done"], u - 2)
                    act.activation(aq3[:, :, P * t:P * (t + 1)], cut(ps[:, 0], 0, 4, P), ACT.Copy).then_inc(s["oA_out"], 1)
                evacs("p", u)
            evacs("need", "cq", 3)
            evacs("need", "pb", 13)
            evacs("close", "p", 0)
            for hb in range(2):
                act.wait_ge(s["s_max"], hb + 1)
                flat = ps[:, s_bank[hb]:s_bank[hb] + 3].rearrange("p a b -> p (a b)")[:, 0:KEYS]
                act.activation(pr[hb], flat, ACT.Exp, bias=nm[:, hb:hb + 1], scale=0.125,
                               accum_out=sm[:, hb:hb + 1]).then_inc(s["s_exp"], 1)
            for hb in range(2):
                sb_ = s_bank[hb]
                act.wait_ge(s["s_pT"], hb + 1)
                act.activation(pt[:, 0:4], cut(ps[:, sb_], 0, 4, P), ACT.Copy).then_inc(s["s_pT_out"], 1)
                act.activation(pt[:, 4:8], cut(ps[:, sb_ + 1], 0, 4, P), ACT.Copy).then_inc(s["s_pT_out"], 1)
                act.activation(pt[0:NS, 8], ps[0:NS, sb_ + 2, 0:P], ACT.Copy).then_inc(s["s_pT_out"], 1)
                act.wait_ge(s["vs_used"], 4 * (hb + 1))
                for g in range(2):
                    gp = slice(64 * g, 64 * g + 64)
                    dst = aq3[gp, :, SEQ + 16 * hb:SEQ + 16 * hb + 16].rearrange("p t (b q) -> p b t q", b=4)
                    src = ps[gp, sb_ + 3, 0:128].rearrange("p (b g t q) -> p b g t q", b=4, g=2, t=4)[:, :, g]
                    act.activation(dst, src, ACT.Copy).then_inc(s["oA_out"], 1)
            for v in range(NX + 3):
                if v < NX:
                    act.wait_ge(s["x_max"], v + 1)
                    if v >= 3:
                        act.wait_ge(s["x_pT"], v - 2)
                    for h in range(2):
                        q = 2 * (v % 2) + h
                        act.activation(xp[:, v % 3, h], ps[:, 4 + v % 3, NMEM * h:NMEM * (h + 1)], ACT.Exp,
                                       bias=nm[:, q:q + 1], scale=scale_c, accum_out=sm[:, q:q + 1]).then_inc(s["x_exp"], 1)
                if 2 <= v < NX + 2:
                    w = v - 2
                    act.wait_ge(s["x_pT"], w + 1)
                    if w >= 2:
                        act.wait_ge(s["xav_done"], w - 1)
                    act.activation(ppt[:, w % 2], cut(ps[:, 1 if w % 2 else 7], 0, 4, P), ACT.Copy).then_inc(s["x_pT_out"], 1)
                if v >= 3 and (v - 3) % 2:
                    t = (v - 3) // 2
                    act.wait_ge(s["xav_done"], v - 2)
                    act.activation(cq3[:, :, P * t:P * (t + 1)], cut(ps[:, 0], 0, 4, P), ACT.Copy).then_inc(s["oC_out"], 1)
                evacs("x", v)
            evacs("need", "pb", 8)
            def early(j, n):
                if n == 0:
                    if j:
                        act.wait_ge(s["factors"], j)
                    act.wait_ge(s["lora_up"], 2 * j + 1)
                    act.activation(h2(lw), pair(0), ACT.Tanh, bias=hw0[:, j:j + 1], scale=0.5).then_inc(s["tanhs"], 1)
                elif n == 1:
                    act.wait_ge(s["lora_up"], 2 * j + 2)
                    act.activation(h2(a_), pair(0), ACT.Tanh, bias=ha0[:, j:j + 1], scale=0.5).then_inc(s["tanhs"], 1)
                elif n == 2:
                    act.wait_ge(s["kk"], 2 * j + 1)
                    if j == 0:
                        act.wait_ge(s["t12"], 2)
                    act.activation(tA, kk, ACT.Square).then_inc(s["kk_sq"], 1)
                else:
                    act.wait_ge(s["kk_ss"], j + 1)
                    act.activation(h2(tA), pair(0), ACT.Sqrt).then_inc(s["kk_rt"], 1)

            act.wait_ge(s["mix"], 2)
            act.activation(t12[0:64], tA[0:64], ACT.Tanh)
            act.activation(t12[64:128], tA[64:128], ACT.Copy).then_inc(s["t12"], 1)
            act.activation(t13, r_, ACT.Sigmoid).then_inc(s["t12"], 1)
            early(0, 2)
            act.wait_ge(s["x_max"], 9)
            act.activation(cp, ps[:, 4, 0:NMEM], ACT.Exp, bias=nm[:, 0:1], scale=scale_c,
                           accum_out=sm[:, 0:1]).then_inc(s["x_exp"], 1)
            evacs("c", 0)
            act.wait_ge(s["x_pT"], 9)
            act.activation(cpt, cut(ps[:, 5], 0, 2, P), ACT.Copy).then_inc(s["x_pT_out"], 1)
            evacs("c", 1)
            act.wait_ge(s["mvs_used"], 8)
            act.activation(cq3[:, :, SEQ:TOK].rearrange("p h (b q) -> p b h q", b=DB),
                           ps[:, 0, 0:P].rearrange("p (b h q) -> p b h q", b=DB, h=4), ACT.Copy).then_inc(s["oC_out"], 1)
            evacs("c", 2)
            for j in range(4):
                if j == 0:
                    act.wait_ge(s["half_bias"], 3)
                    for n in (0, 1, 3):
                        early(0, n)
                        if n == 0:
                            evacs("prep", 0, 0)
                else:
                    evacs("prep", j, 0)
                act.wait_ge(s["lx"], j + 1)
                act.activation(tA, L_, ACT.Exp).then_inc(s["exps"], 1)
                act.activation(tB, L_, ACT.Exp, scale=-1.0).then_inc(s["exps"], 1)
                act.activation(lw, a_, ACT.Exp).then_inc(s["exps"], 1)
                act.activation(scf, scf, ACT.Exp).then_inc(s["exps"], 1)
                evacs("prep", j, 1)
                evacs("prep", j, 2)
                if j < 3:
                    evacs("need", "pb", 9 + j)
                evacs("close", "tm", j)
                act.wait_ge(s["tm"], j + 1)
                for n in range(3):
                    act.activation(tm[:, n], cut(ps[:, n], 0, 4, P), ACT.Copy).then_inc(s["tm_out"], 1)
                act.activation(tms[0:NS], cut(ps[0:NS, 3], 0, 3, P), ACT.Copy).then_inc(s["tm_out"], 1)
                for hh in range(2):
                    g = 2 * j + hh
                    hp = slice(64 * hh, 64 * hh + 64)
                    if hh:
                        evacs("close", "group", 2 * j)
                    for r in range(3):
                        for c in range(4):
                            act.wait_ge(s["round"], 16 * g + 4 * r + c + 1)
                            act.activation(dx[:, c, 0::2], cut(ps[:, 4 + c], 0, 4, P)[:, 0::2], ACT.Copy).then_inc(s["dsq"], 1)
                    for l in range(3):
                        for c in range(4):
                            act.wait_ge(s["mx"], 12 * g + 4 * l + c + 1)
                            act.activation(tt[:, c], ps[:, 4 + c, 0:P], ACT.Copy).then_inc(s["mx_out"], 1)
                    for c in range(4):
                        n = 4 * g + c
                        act.wait_ge(s["z"], n + 1)
                        act.activation(zs, ps[:, 4, 0:64], ACT.Copy).then_inc(s["z_out"], 1)
                        evacs("chunk", n, 0)
                        act.wait_ge(s["u"], n + 1)
                        act.activation(us, ps[:, 5, 0:64], ACT.Copy).then_inc(s["u_out"], 1)
                        evacs("chunk", n, 1)
                        act.wait_ge(s["ychunk"], n + 1)
                        act.activation(y_[hp, C * c:C * (c + 1)], ps[hp, 6, 0:P], ACT.Copy).then_inc(s["y_chunk"], 1)
                        if hh == 0 and j < 3:
                            early(j + 1, c)
                        if j == 3:
                            if n == 24:
                                act.wait_ge(s["diff"], 14)
                                act.wait_ge(s["mix"], 14)
                            source_hi(act, n - 24)
                        evacs("chunk", n, 2)
                heads = [(hh, 2 * j + hh, slice(64 * hh, 64 * hh + 64), dec[hh]) for hh in range(2)]
                evacs("dec", j, 0)
                for hh, n, hp, d in heads:
                    act.wait_ge(s["s_z"], n + 1)
                    act.activation(d["z"], ps[0:NS, hh, 0:64], ACT.Copy).then_inc(s["s_z_out"], 1)
                evacs("dec", j, 1)
                for hh, n, hp, d in heads:
                    act.wait_ge(s["s_u"], n + 1)
                    act.activation(d["u"], ps[0:NS, hh, 64:128], ACT.Copy).then_inc(s["s_u_out"], 1)
                evacs("dec", j, 2)
                for hh, n, hp, d in heads:
                    act.wait_ge(s["s_y"], n + 1)
                    act.activation(y_[hp, SEQ:TOK], ps[hp, 4 + hh, 256:256 + NS], ACT.Copy).then_inc(s["s_y_out"], 1)
                evacs("dec", j, 3)
                evacs("dec", j, 4)
                act.wait_ge(s["yc"], j + 1)
                act.activation(tA, y_, ACT.Square).then_inc(s["yc_sq"], 1)
                evacs("gn", j, 0)
                act.wait_ge(s["var"], j + 1)
                act.activation(h2(tA), pair(4), ACT.Sqrt, bias=gneps, scale=1.0 / 64).then_inc(s["y_rt"], 1)
                evacs("gn", j, 1)
                evacs("gn", j, 2)
            evacs("need", "gate", 23)
            weights_hi(act, SPLIT0)
            weights_hi(act, SPLIT0 + 1)
            act.wait_ge(s["oB_out"], 4)
            act.wait_ge(s["t0s_out"], 16 * 4)
            for n in range(8, 12):
                source_hi(act, n)
            for n in range(SPLIT0, job_at("out", 0)):
                kind, idx, *_ = JOBS[n]
                act.wait_ge(s["gemm_done"], n + 1)
                weights_hi(act, n + 2)
                if merge_at(idx)[1] == 2:
                    dj = merge_at(idx)[0]
                    act.wait_ge(s["merged"], merges(idx))
                    act.activation(M[0][dj], acc[:, dj % 2], ACT.Copy).then_inc(s["part_hi"], 1)
            for n in range(job_at("out", 0), job_at("up", 0)):
                j = JOBS[n][1]
                weights_hi(act, n + 2)
                if j >= 1:
                    square(2, xT3, TOK, j - 1)
            norm(2, xT3, TOK, KT - 1)
            for k in range(KT):
                act.wait_ge(s["norm_out"], 16 + k + 1)
                act.activation(X[0][k], nx[:, k % 2], ACT.Copy).then_inc(s["part_hi"], 1)
            for n in range(job_at("up", 0), NJOB):
                kind, idx, *_ = JOBS[n]
                if kind == "up":
                    if idx == 0:
                        act.wait_ge(s["part_lo"], PART["x"] + KT)
                    evac(n)
                    weights_hi(act, n + 2)
                    act.wait_ge(s["evac_a"], evacuated(n, "a"))
                    act.activation(H[idx // 8 % 2][0][idx % 8], ub2[:, idx % 2], ACT.Square).then_inc(s["part_hi"], 1)
                else:
                    weights_hi(act, n + 2)
                    if idx >= 25:
                        square(3, xT3, TOK, idx - 25)
            norm(3, xT3, TOK, KT - 1)

        @block.vector
        def _(dve):
            step = Steps(dve, s["dve_step"])

            def norm(n, src, dst, N, g):
                dve.wait_ge(s["norm_rt"], n + 1)
                if n:
                    dve.wait_ge(s["norm_out"], 8 * n)
                rt, rc = nbuf[n][1:]
                dve.reciprocal(rc[:, 0:N], rt[:, 0:N]).then_inc(s["norm_rc"], 1)
                dve.wait_ge(s["norm_rc"], n + 1)
                for k in range(KT):
                    to = dst[:, k % 2] if n == 2 else dst[:, k]
                    if n == 2 and k >= 2:
                        dve.wait_ge(s["part_lo"], PART["x"] + k - 1)
                    dve.scalar_tensor_tensor(to, src[:, k], v_(g, k), rc[:, 0:N], ALU.mult,
                                             ALU.mult).then_inc(s["norm_out"], 1)
                    if n == 2 and k:
                        x_rest(k - 1)

            def add_square(n, k):
                sq_ = nbuf[n][0][:, k % 2]
                dve.wait_ge(s["norm_sq"], KT * n + k + 1)
                if k:
                    dve.wait_ge(s["norm_ss"], KT * n + k)
                    dve.tensor_tensor(squares, squares, sq_, ALU.add).then_inc(s["norm_ss"], 1)
                else:
                    dve.tensor_copy(squares, sq_).then_inc(s["norm_ss"], 1)

            def x_rest(k):
                dve.wait_ge(s["part_hi"], PART["x"] + k + 1)
                dve.tensor_tensor(X[1][k], nx[:, k % 2], X[0][k].bitcast(F32), ALU.subtract).then_inc(s["part_lo"], 1)

            def rope(n):
                kind, idx, raw = ROPE[n]
                dve.wait_ge(s["rope_rot"], n + 1)
                if n:
                    dve.wait_ge(s["rope_out"], n)
                dve.tensor_tensor(h2(rope1), pair(4 + 2 * (n % 2)), h2(k_("sin")), ALU.mult).then_inc(s["rope_sin"], 1)
                dve.wait_ge(s["rope_sin"], n + 1)
                dve.wait_ge(s["rope_cos"], n + 1)
                dve.tensor_tensor(raw, rope1, rope2[:, n % 2], ALU.add).then_inc(s["rope_out"], 1)

            dve.wait_ge(s["ones_in"], 16)
            dve.wait_ge(s["inputs_in"], 32)
            dve.tensor_copy(identb[:, :], ident).then_inc(s["bf_const"], 1)
            dve.tensor_copy(repb[0:NS, :], k_("rep")[0:NS]).then_inc(s["bf_const"], 1)
            dve.tensor_scalar(hw0, vec[:, VOFF["rwkv_w0"][0]:VOFF["rwkv_w0"][0] + 4], 0.5, None, ALU.mult).then_inc(s["half_bias"], 1)
            dve.tensor_scalar(ha0, vec[:, VOFF["rwkv_a0"][0]:VOFF["rwkv_a0"][0] + 4], 0.5, None, ALU.mult).then_inc(s["half_bias"], 1)
            dve.tensor_scalar(hgate, vec[:, VOFF["b_gate"][0]:VOFF["b_gate"][0] + 24], 0.5, None, ALU.mult).then_inc(s["half_bias"], 1)
            norm(0, xT3, xn3, TOK, "norm_mix_g")
            norm(1, memT, memn, NMEM, "norm_mem_g")
            for n in range(3):
                rope(n)
            dve.wait_ge(s["pool_step"], 3)
            dve.wait_ge(s["rope_out"], 3)
            for h in range(4):
                hp = slice(64 * (h % 2), 64 * (h % 2) + 64)
                dst = zi[0:64, 32 * h:32 * h + DB * 132].rearrange("p (b c) -> p b c", c=132)[:, :, 0:4]
                dve.tensor_copy(dst, iq[hp, h // 2, SEQ:TOK].rearrange("p (b q) -> p b q", q=4)).then_inc(s["zi_set"], 1)
            dve.wait_ge(s["iw_tok"], 1)
            step(dve.tensor_scalar(iwc[:, 0:16], ps[:, 7, 0:16], 0.0625, None, ALU.mult))
            step(dve.tensor_scalar(iwc[0:NS, 16:20], ps[0:NS, 7, 16:20], 0.0625, None, ALU.mult))
            for h in range(4):
                ins = dve.tensor_copy(iws[32 * h:32 * h + 32], iwc[0:NS, 16 + h:17 + h])
                if h < 3:
                    step(ins)
                else:
                    ins.then_inc(s["zi_set"], 1)
            dve.wait_ge(s["zi_set"], 5)
            flat = ps[:, 4:7].rearrange("p a b -> p (a b)")[:, 0:KEYS]
            dve.tensor_copy(biasp[:, 0, 0:P], k_("caus")).then_inc(s["bias_done"], 1)

            def take_eight(sc, m8):
                step(dve.max(m8, sc))
                step(dve.match_replace(sc, m8, sc, GONE))

            m8 = small[:, 132:140]
            for t in range(1, 4):
                n = P * (t + 1)
                sc = scp[:, 0:n]
                for h in range(4):
                    dve.wait_ge(s["relu"], 4 * (t - 1) + h + 1)
                    if h == 0:
                        ins = dve.tensor_scalar(sc, rl[:, 0, 0:n], iwc[:, 4 * t:4 * t + 1], None, ALU.mult)
                    else:
                        dve.wait_ge(s["isum"], 4 * (t - 1) + h)
                        ins = dve.scalar_tensor_tensor(sc, rl[:, h, 0:n], iwc[:, 4 * t + h:4 * t + h + 1], sc, ALU.mult, ALU.add)
                    ins.then_inc(s["isum"], 1)
                dve.wait_ge(s["isum"], 4 * t)
                step(dve.tensor_tensor(sc[:, P * t:n], sc[:, P * t:n], k_("caus"), ALU.add))
                for _ in range(TOPK_P // 8):
                    take_eight(sc, m8)
                dve.tensor_scalar(biasp[:, t, 0:n], sc, -2e38, NEG, ALU.is_gt, ALU.mult).then_inc(s["bias_done"], 1)
                dve.wait_ge(s["bias_done"], t + 1)
            dve.wait_ge(s["ki_used"], 8)
            dve.tensor_scalar(rs, flat, 0.0, iws, ALU.max, ALU.mult).then_inc(s["rs"], 1)
            dve.wait_ge(s["ssum"], 1)
            step(dve.tensor_copy(ss[:, 0:PAST], flat[0:NS, 0:PAST]))
            dve.tensor_tensor(ss[:, PAST:KEYS], flat[0:NS, PAST:KEYS], k_("snew")[0:NS], ALU.add).then_inc(s["ss_out"], 1)
            dve.wait_ge(s["ss_out"], 1)
            for n in range(3, 8):
                rope(n)
            dve.wait_ge(s["pool_step"], 4)
            dve.wait_ge(s["rope_out"], 8)
            for hb in range(2):
                for g in range(2):
                    gp = slice(64 * g, 64 * g + 64)
                    dst = za[gp, 640 * hb:640 * hb + 640].rearrange("p (b c) -> p b c", c=160)[:, :, 16 * g:16 * g + 16]
                    dst = dst.rearrange("p b (t q) -> p b t q", q=4)
                    src = aq3[gp, :, SEQ + 16 * hb:SEQ + 16 * hb + 16].rearrange("p t (b q) -> p b t q", b=4)
                    dve.tensor_copy(dst, src).then_inc(s["za_set"], 1)
            for u in range(NU + 1):
                if u < NU:
                    t, q = u // 8, u % 4
                    dve.wait_ge(s["p_score"], u + 1)
                    if u >= 4:
                        dve.wait_ge(s["p_exp"], u - 3)
                    step(dve.tensor_reduce(mx[:, q:q + 1], ps[:, 4 + u % 3, 0:P * (t + 1)], AX.X, ALU.max))
                    dve.tensor_scalar(nm[:, q:q + 1], mx[:, q:q + 1], -0.125, None, ALU.mult).then_inc(s["p_max"], 1)
                if u >= 1:
                    w = u - 1
                    t, q = w // 8, w % 4
                    dve.wait_ge(s["p_exp"], w + 1)
                    step(dve.reciprocal(ri[:, q:q + 1], sm[:, q:q + 1]))
                    dve.tensor_scalar(pp[:, w % 3, 0:P * (t + 1)], pp[:, w % 3, 0:P * (t + 1)], ri[:, q:q + 1], None,
                                      ALU.mult).then_inc(s["p_prob"], 1)
                for _ in range(TOPK_S // 8 * u // NU, TOPK_S // 8 * (u + 1) // NU if u < NU else TOPK_S // 8):
                    take_eight(ss, m8[0:NS])
            dve.wait_ge(s["p_prob"], NU)
            dve.tensor_scalar(biass[0:NS], ss, -2e38, NEG, ALU.is_gt, ALU.mult).then_inc(s["selected"], 1)
            for hb in range(2):
                dve.wait_ge(s["s_score"], hb + 1)
                flat = ps[:, s_bank[hb]:s_bank[hb] + 3].rearrange("p a b -> p (a b)")[:, 0:KEYS]
                step(dve.tensor_reduce(mx[:, hb:hb + 1], flat, AX.X, ALU.max))
                dve.tensor_scalar(nm[:, hb:hb + 1], mx[:, hb:hb + 1], -0.125, None, ALU.mult).then_inc(s["s_max"], 1)
            for hb in range(2):
                dve.wait_ge(s["s_exp"], hb + 1)
                step(dve.reciprocal(ri[:, hb:hb + 1], sm[:, hb:hb + 1]))
                dve.tensor_scalar(pr[hb], pr[hb], ri[:, hb:hb + 1], None, ALU.mult).then_inc(s["s_prob"], 1)

            def mix(dst, tile, n):
                cur = pb3[:, tile]
                dve.wait_ge(s["diff"], n + 1)
                mu = v_("rwkv_mu", tile)
                dve.scalar_tensor_tensor(dst[:, 0:SEQ], dst[:, 0:SEQ], mu, cur[:, 1:SEQ + 1], ALU.mult, ALU.add)
                d4 = dst[:, SEQ:TOK].rearrange("p (b c) -> p b c", c=4)
                c5 = cur[:, SEQ + 1:PBW].rearrange("p (b c) -> p b c", c=5)
                dve.scalar_tensor_tensor(d4, d4, mu, c5[:, :, 1:5], ALU.mult, ALU.add).then_inc(s["mix"], 1)

            CL = -0.5 * float(np.exp(-0.5))

            def early(j, n):
                if n == 0:
                    mix(k__, 4 + j, 2 + 3 * j)
                elif n == 1:
                    mix(v__, 8 + j, 3 + 3 * j)
                elif n == 2:
                    dve.wait_ge(s["mix"], 3 + 3 * j)
                    dve.tensor_scalar(kk, k__, v_("rwkv_k_k", j), None, ALU.mult).then_inc(s["kk"], 1)
                elif n == 3:
                    dve.wait_ge(s["tanhs"], 2 * j + 2)
                    step(dve.tensor_scalar(lw, lw, CL, CL, ALU.mult, ALU.add))
                    step(dve.tensor_scalar(a_, a_, 0.5, 0.5, ALU.mult, ALU.add))
                elif n == 4:
                    dve.wait_ge(s["kk_rt"], j + 1)
                    step(dve.tensor_scalar(tA, tA, 1e-12, None, ALU.max))
                    step(dve.reciprocal(tB, tA))
                elif n == 5:
                    dve.tensor_tensor(kk, kk, tB, ALU.mult).then_inc(s["kk"], 1)
                    dve.wait_ge(s["kk"], 2 * j + 2)
                else:
                    step(dve.tensor_scalar(tB, a_, 1.0, v_("rwkv_k_a", j), ALU.subtract, ALU.mult))
                    step(dve.scalar_tensor_tensor(kh, tB, 1.0, k__, ALU.add, ALU.mult))

            for v in range(NX + 1):
                if v < NX:
                    q = slice(2 * (v % 2), 2 * (v % 2) + 2)
                    dve.wait_ge(s["x_score"], v + 1)
                    step(dve.tensor_reduce(mx[:, q], cut(ps[:, 4 + v % 3], 0, 2, NMEM), AX.X, ALU.max))
                    if v >= 2:
                        dve.wait_ge(s["x_exp"], 2 * (v - 1))
                    dve.tensor_scalar(nm[:, q], mx[:, q], -scale_c, None, ALU.mult).then_inc(s["x_max"], 1)
                if v >= 1:
                    w = v - 1
                    q = slice(2 * (w % 2), 2 * (w % 2) + 2)
                    dve.wait_ge(s["x_exp"], 2 * (w + 1))
                    step(dve.reciprocal(ri[:, q], sm[:, q]))
                    dve.tensor_tensor(xp[:, w % 3], xp[:, w % 3], ri[:, q].unsqueeze(2).to_broadcast([P, 2, NMEM]),
                                      ALU.mult).then_inc(s["x_prob"], 1)
            dve.wait_ge(s["pool_step"], 5)
            dve.tensor_copy(zc.rearrange("p (b h c) -> p b h c", b=DB, h=4)[:, :, :, 0:4],
                            cq3[:, :, SEQ:TOK].rearrange("p h (b q) -> p b h q", b=DB)).then_inc(s["zc_set"], 1)
            mix(tA, 12, 0)
            mix(r_, 13, 1)
            for n in range(3):
                early(0, n)
            dve.wait_ge(s["mks_used"], 8)
            dve.wait_ge(s["x_prob"], 8)
            step(dve.tensor_reduce(mx[:, 0:1], ps[:, 4, 0:NMEM], AX.X, ALU.max))
            dve.tensor_scalar(nm[:, 0:1], mx[:, 0:1], -scale_c, None, ALU.mult).then_inc(s["x_max"], 1)
            dve.wait_ge(s["x_exp"], 17)
            step(dve.reciprocal(ri[:, 0:1], sm[:, 0:1]))
            dve.tensor_scalar(cp, cp, ri[:, 0:1], None, ALU.mult).then_inc(s["x_prob"], 1)

            for j in range(4):
                if j == 0:
                    for n in range(3, 7):
                        early(0, n)
                else:
                    dve.wait_ge(s["oB_out"], j)
                mix(r_, j, 4 + 3 * j)
                step(dve.tensor_tensor_scan(L_, k_("reset"), lw, 0.0, ALU.mult, ALU.add))
                dve.tensor_tensor(bt, kk, a_, ALU.mult)
                dve.wait_ge(s["mix"], 2 + 3 * (j + 1))
                step(dve.tensor_copy(c0, L_[:, C // 2 - 1:SEQ:C]))
                l3 = L_[:, 0:SEQ].rearrange("p (c t) -> p c t", c=4)
                step(dve.tensor_tensor(l3, l3, c0.unsqueeze(2).to_broadcast([P, 4, C]), ALU.subtract))
                step(dve.tensor_copy(scf, L_[:, C - 1:SEQ:C]))
                step(dve.tensor_tensor(scf[:, 0:3], scf[:, 0:3], c0[:, 1:4], ALU.add))
                dve.tensor_tensor(a_, L_, lw, ALU.subtract).then_inc(s["lx"], 1)
                dve.wait_ge(s["exps"], 4 * (j + 1))
                dve.scalar_tensor_tensor(L_, r_, v_("rwkv_r_k", j), kh, ALU.mult, ALU.mult).then_inc(s["rk"], 1)
                dve.tensor_copy(sdec, tA[:, SEQ + 3:TOK:4])
                dve.tensor_tensor(AR[:, 1], r_, tA, ALU.mult)
                dve.scalar_tensor_tensor(AR[:, 0], kk, -1.0, lw, ALU.mult, ALU.mult)
                dve.tensor_tensor(bt, bt, tB, ALU.mult)
                dve.tensor_tensor(kt_, kh, tB, ALU.mult).then_inc(s["factors"], 1)
                dve.wait_ge(s["rk_sum"], j + 1)
                dve.tensor_tensor(h2(L_), pair(6), h2(v__), ALU.mult).then_inc(s["bonus"], 1)
                for hh in range(2):
                    g = 2 * j + hh
                    hp = slice(64 * hh, 64 * hh + 64)
                    for c in range(4):
                        dve.wait_ge(s["pairs"], 4 * g + c + 1)
                        if c == 0 and hh == 0 and j:
                            dve.wait_ge(s["t0s_out"], 16 * j)
                        dve.tensor_tensor(m4[:, c], cut(ps[:, 4 + c], 0, 4, P), cut(cst, COFF["mask4"][0], 4, P),
                                          ALU.mult).then_inc(s["m4"], 1)
                    for c in range(4):
                        dve.wait_ge(s["low"], 4 * g + c + 1)
                        dve.tensor_tensor(dx[:, c, 0], ps[:, c, 0:P], k_("mlow"), ALU.mult).then_inc(s["dlow"], 1)
                    for r in range(1, 4):
                        for c in range(4):
                            dve.wait_ge(s["round"], 16 * g + 4 * r + c + 1)
                            dve.tensor_tensor(dx[:, c, 1::2], dx[:, c, 1::2], cut(ps[:, c], 0, 2, P),
                                              ALU.add).then_inc(s["xup"], 1)
                    for l in range(3):
                        for c in range(4):
                            dve.wait_ge(s["xmx"], 12 * g + 4 * l + c + 1)
                            if l < 2:
                                ins = dve.tensor_tensor(dx[:, c, 1::2], dx[:, c, 1::2], cut(ps[:, c], 0, 2, P), ALU.add)
                            else:
                                ins = dve.tensor_tensor(dx[:, c, 3], dx[:, c, 3], ps[:, c, P:256], ALU.add)
                            ins.then_inc(s["xlev"], 1)
                    for c in range(4):
                        n = 4 * g + c
                        dve.wait_ge(s["dstate"], n + 1)
                        if c:
                            dve.wait_ge(s["ychunk"], n)
                            dve.wait_ge(s["ychunk"], n + 1)
                            step(dve.tensor_tensor(T0[hp], T0[hp], ps[hp, 7, 0:64], ALU.add))
                            ins = dve.tensor_scalar(T0[hp], T0[hp], scf[hp, c:c + 1], None, ALU.mult)
                        else:
                            if j:
                                dve.wait_ge(s["T0_out"], 16 * j)
                            ins = dve.tensor_scalar(T0[hp], ps[hp, 7, 0:64], scf[hp, 0:1], None, ALU.mult)
                        ins.then_inc(s["state"], 1)
                        if j < 3 and 4 * hh + c < 7:
                            early(j + 1, 4 * hh + c)
                        if j == 3 and n > 24:
                            source_lo(dve, n - 25)
                if j == 3:
                    source_lo(dve, 7)
                heads = [(hh, 2 * j + hh, slice(64 * hh, 64 * hh + 64), dec[hh]) for hh in range(2)]
                bl = k_("sblk")[0:NS].unsqueeze(2).to_broadcast([NS, DB, 64])
                for hh, n, hp, d in heads:
                    dve.wait_ge(s["s_pairs"], n + 1)
                    dve.tensor_tensor(d["m4"][0:NS], cut(ps[0:NS, 4 + hh], 0, 4, NS), cut(cst, COFF["smask4"][0], 4, NS)[0:NS],
                                      ALU.mult).then_inc(s["s_m4"], 1)
                    dve.tensor_tensor(d["low"], ps[0:NS, 4 + hh, 128:160], k_("slow")[0:NS], ALU.mult).then_inc(s["s_m4"], 1)
                    dve.wait_ge(s["s_m4"], 3 * n + 2)
                    dve.tensor_tensor(d["x"], d["m4"][0:NS, 0], ident[0:NS, 0:NS], ALU.add).then_inc(s["s_m4"], 1)
                for hh, n, hp, d in heads:
                    dve.wait_ge(s["s_inv"], 4 * j + hh + 1)
                    dve.tensor_copy(d["sq"], ps[0:NS, 6 + hh, 0:NS]).then_inc(s["s_inv_out"], 1)
                for hh, n, hp, d in heads:
                    dve.wait_ge(s["s_inv"], 4 * j + 2 + hh + 1)
                    dve.tensor_tensor(d["xt"], d["x"], ps[0:NS, 6 + hh, 64:64 + NS], ALU.add).then_inc(s["s_inv_out"], 1)
                for hh, n, hp, d in heads:
                    dve.tensor_tensor(d["vb"][0:NS], tms[0:NS, 0:1, hp].to_broadcast([NS, DB, 64]), bl, ALU.mult).then_inc(s["s_blk"], 1)
                for hh, n, hp, d in heads:
                    dve.wait_ge(s["s_u_out"], n + 1)
                    dve.tensor_tensor(d["ub"][0:NS], d["u"].unsqueeze(1).to_broadcast([NS, DB, 64]), bl, ALU.mult).then_inc(s["s_blk"], 1)
                for hh, n, hp, d in heads:
                    dve.wait_ge(s["s_dstate"], n + 1)
                    step(dve.tensor_tensor(t0s[hp], t0s[hp], cut(ps[hp, 6 + hh], 0, DB, 64), ALU.add))
                    dve.tensor_tensor(t0s[hp], t0s[hp], sdec[hp].unsqueeze(2).to_broadcast([64, DB, 64]), ALU.mult).then_inc(s["sstate"], 1)
                dve.wait_ge(s["mean"], j + 1)
                dve.scalar_tensor_tensor(h2(y_), pair(0), -1.0 / 64, h2(y_), ALU.mult, ALU.add).then_inc(s["yc"], 1)
                dve.wait_ge(s["y_rt"], j + 1)
                step(dve.reciprocal(tB, tA))
                step(dve.tensor_tensor(y_, y_, tB, ALU.mult))
                step(dve.tensor_scalar(y_, y_, v_("rwkv_ln_g", j), v_("rwkv_ln_b", j), ALU.mult, ALU.add))
                step(dve.tensor_tensor(y_, y_, L_, ALU.add))
                dve.wait_ge(s["g"], j + 1)
                dve.tensor_tensor(h2(pb3[:, j, 0:TOK]), pair(0), h2(y_), ALU.mult).then_inc(s["oB_out"], 1)

            weights_lo(dve, SPLIT0)
            weights_lo(dve, SPLIT0 + 1)
            for n in range(8, 12):
                source_lo(dve, n)
            for n in range(SPLIT0, job_at("out", 0)):
                kind, idx, _, _, _, e = JOBS[n]
                if e == "v":
                    b = bank_of(n)
                    dve.wait_ge(s["gemm_done"], n + 1)
                    dve.wait_ge(s[f"gate_in{idx % 3}"], 16 * (idx // 3 + 1))
                    dj, br = merge_at(idx)
                    to = acc[:, dj % 2]
                    if br == 0 and dj >= 2:
                        dve.wait_ge(s["part_lo"], PART["merge"] + dj - 1)
                    dve.scalar_tensor_tensor(h2(mt if br else to), h2(gb[:, idx % 3]), 1.0, pair(b), ALU.add, ALU.mult).then_inc(s["evac_v"], 1)
                    if br:
                        dve.wait_ge(s["evac_v"], evacuated(n, "v"))
                        dve.tensor_tensor(to, to, mt, ALU.add).then_inc(s["merged"], 1)
                        dve.wait_ge(s["merged"], merges(idx))
                weights_lo(dve, n + 2)
                if e == "v" and br == 2:
                    dve.wait_ge(s["part_hi"], PART["merge"] + dj + 1)
                    dve.tensor_tensor(M[1][dj], to, M[0][dj].bitcast(F32), ALU.subtract).then_inc(s["part_lo"], 1)
            for n in range(job_at("out", 0), job_at("up", 0)):
                weights_lo(dve, n + 2)
                dve.wait_ge(s["gemm_done"], n + 1)
                dve.wait_ge(s["inputs_in"], 48)
                x = h2(xT3[:, JOBS[n][1]])
                dve.scalar_tensor_tensor(x, pair(bank_of(n)), 0.5, x, ALU.mult, ALU.add).then_inc(s["evac_v"], 1)
                if JOBS[n][1] >= 2:
                    add_square(2, JOBS[n][1] - 2)
            add_square(2, 6)
            add_square(2, 7)
            norm(2, xT3, nx, TOK, "norm_mlp_g")
            x_rest(KT - 1)
            for n in range(job_at("up", 0), NJOB):
                kind, idx, *_ = JOBS[n]
                if kind == "up":
                    out_of(n, dve)
                    if idx >= 2:
                        dve.wait_ge(s["part_lo"], PART["hid"] + idx - 1)
                    dve.tensor_tensor(hsq[:, idx % 2], ub2[:, idx % 2], ub2[:, idx % 2], ALU.mult).then_inc(s["hid_sq"], 1)
                    weights_lo(dve, n + 2)
                    dve.wait_ge(s["part_hi"], PART["hid"] + idx + 1)
                    dve.wait_ge(s["hid_sq"], idx + 1)
                    hi, lo = (h[idx % 8] for h in H[idx // 8 % 2])
                    dve.tensor_tensor(lo, hsq[:, idx % 2], hi.bitcast(F32), ALU.subtract).then_inc(s["part_lo"], 1)
                else:
                    weights_lo(dve, n + 2)
                    dve.wait_ge(s["gemm_done"], n + 1)
                    x = xT3[:, idx % 8]
                    if idx >= 8:
                        out_of(job_at("down", idx - 8), dve)
                    dve.tensor_tensor(h2(x), pair(bank_of(n)), h2(x), ALU.add).then_inc(s["evac_v"], 1)
                    if idx >= 26:
                        add_square(3, idx - 26)
            add_square(3, 6)
            add_square(3, 7)
            out_of(NJOB - 1, dve)
            norm(3, xT3, cut(yo, 0, KT, TOK), TOK, "norm_final_g")


_OUTS = {"yT": (P, KT, TOK), "kT": (P, TOK), "vT": (P, TOK), "ikT": (64, TOK), "mkT": (P, 4, NMEM), "mv": (P, 2, 512),
         "wkvP": (4, P, 64), "wkvS": (4, P, DB, 64), "shT": (P, PBT * 9)}


def kernel(**a):
    import concourse.bacc as bacc
    from concourse.bass_utils import run_bass_kernel_spmd

    a = {k: np.asarray(v) for k, v in a.items()}
    n_phys = a["cache_k"].shape[0]

    def feat(x):
        return np.ascontiguousarray(x.T.reshape(-1, P, x.shape[0]).transpose(1, 0, 2))

    order = np.concatenate([np.arange(64) + 64 * (t + o) for t in range(4) for o in (0, 4)])
    w = {k: a[k] for k in ("w_in", "w_mem_kv", "w_branch_b", "w_branch_c", "w_out", "w_mlp_up", "w_mlp_down")}
    w["w_branch_a"] = a["w_branch_a"][order]
    slabs = np.zeros((NSLAB, P, SLABW), np.float32)
    for n, (name, r0, kts, cols) in enumerate(SLABS):
        m = np.concatenate([w[name][r0:r0 + kts * P, c:c + k] for c, k in cols], 1)
        slabs[n, :, 0:kts * m.shape[1]] = m.reshape(kts, P, -1).transpose(1, 0, 2).reshape(P, -1)
    ins = {
        "xT": feat(np.concatenate([a["x_prompt"].reshape(SEQ, D), a["x_sample"].reshape(NS, D)])),
        "memT": feat(a["mem_prompt"].reshape(NMEM, D)),
        "const": constants(),
        "vec": np.concatenate([a[k].reshape(-1, P).T for k, _ in VECS], 1),
        "slabs": slabs,
        "lora": np.concatenate([np.concatenate([a["rwkv_w_up"], a["rwkv_a_up"]], 0), a["rwkv_g_up"]], 1),
        "shT": feat(a["state_shift"]).reshape(P, -1),
        "pages": a["page_table"].reshape(1, -1),
        "ki": a["cache_idx_k"].transpose(0, 2, 1),
        "kv": np.concatenate([a["cache_k"].reshape(n_phys, PAGE, P).transpose(0, 2, 1),
                              a["cache_v"].reshape(n_phys, PAGE, P)], 2),
        "mks": a["cache_mem_k"].transpose(0, 3, 2, 1).reshape(DB, P, 4 * NMEM),
        "mvs": a["cache_mem_v"].reshape(DB, 2, P, 512).transpose(0, 2, 1, 3).reshape(DB, P, 1024),
        "wkvT": a["state_wkv"].transpose(1, 3, 0, 2).reshape(4, P, DB, 64),
    }
    nc = bacc.Bacc("TRN2", target_bir_lowering=False, num_devices=1)
    arrays, i, o = {}, {}, {}
    for k, x in ins.items():
        x = np.ascontiguousarray(x)
        arrays["in_" + k] = x
        i[k] = nc.dram_tensor("in_" + k, x.shape, mybir.dt.from_np(x.dtype), kind="ExternalInput").ap()
    for k, shape in _OUTS.items():
        o[k] = nc.dram_tensor("out_" + k, shape, F32, kind="ExternalOutput").ap()
    i["gates"] = nc.dram_tensor("gates", (24, P, TOK), F32, kind="Internal").ap()
    build(nc, i, o)
    r = run_bass_kernel_spmd(nc, [arrays], core_ids=[0]).results[0]
    g = {k: r["out_" + k] for k in _OUTS}
    y = g["yT"].transpose(2, 1, 0).reshape(TOK, D)
    k, v, ik = g["kT"].T, g["vT"].T, g["ikT"].T
    sh = g["shT"].reshape(P, PBT, 9).transpose(2, 1, 0).reshape(9, PB)
    mkT = g["mkT"].reshape(P, 4, NMEM).transpose(2, 1, 0)
    mv = g["mv"].transpose(1, 0, 2).reshape(NMEM, 4, P)
    wp = g["wkvP"].reshape(8, 64, 64).transpose(0, 2, 1)
    ws = g["wkvS"].reshape(8, 64, DB, 64).transpose(2, 0, 3, 1)
    out = (y[:SEQ].reshape(1, SEQ, D), y[SEQ:].reshape(DB, DS, D), k[:SEQ].reshape(1, SEQ, 2, 64), v[:SEQ].reshape(1, SEQ, 2, 64),
           ik[:SEQ].reshape(1, SEQ, 64), mkT[None], mv[None], wp[None], sh[0:1], k[SEQ:].reshape(DB, DS, 2, 64),
           v[SEQ:].reshape(DB, DS, 2, 64), ik[SEQ:].reshape(DB, DS, 64), ws, sh[1:])
    return tuple(np.ascontiguousarray(x) for x in out)
```
